# Optimizing a Trainium2 kernel written in Bass

```python
import math
import jax, jax.numpy as jnp
from jax import lax
import numpy as np

D_MODEL = 2048
BATCH = 1
SEQ = 256
DEPTH = 1

MLA_HEADS = 16
MLA_Q_RANK = 512
MLA_KV_RANK = 256
MLA_NOPE_DIM = 128
MLA_ROPE_DIM = 64
MLA_V_DIM = 128
ROPE_THETA = 10000.0
SWA_Q_HEADS = 32
SWA_KV_HEADS = 4
SWA_HEAD_DIM = 64
SWA_GROUP = SWA_Q_HEADS // SWA_KV_HEADS
WINDOW = 128
BLOCK = 128
REL_BUCKETS = 32
REL_MAX_DIST = 128
D_FF = 5632
CONV_WIDTH = 3
N_BRANCHES = 2
EPS = 1e-6

MLA_WIDTH = MLA_HEADS * MLA_V_DIM
SWA_WIDTH = SWA_Q_HEADS * SWA_HEAD_DIM
SWA_KV_WIDTH = SWA_KV_HEADS * SWA_HEAD_DIM
IN_SPLITS = (MLA_Q_RANK, MLA_KV_RANK, MLA_ROPE_DIM, SWA_WIDTH, SWA_KV_WIDTH, SWA_KV_WIDTH, N_BRANCHES * D_MODEL)
IN_COLS = MLA_Q_RANK + MLA_KV_RANK + MLA_ROPE_DIM + SWA_WIDTH + 2 * SWA_KV_WIDTH + N_BRANCHES * D_MODEL


def rms_norm(x, g):
    xf = x.astype(jnp.float32)
    y = xf * lax.rsqrt(jnp.mean(xf * xf, axis=-1, keepdims=True) + EPS)
    return (y * g.astype(jnp.float32)).astype(x.dtype)

def rope_angles(pos, dim):
    inv = ROPE_THETA ** (-jnp.arange(0, dim, 2, dtype=jnp.float32) / dim)
    ang = pos.astype(jnp.float32)[:, None] * inv[None, :]
    return jnp.cos(ang), jnp.sin(ang)

def apply_rope(x, cos, sin):
    half = x.shape[-1] // 2
    x1, x2 = x[..., :half], x[..., half:]
    cos = cos.astype(x.dtype)
    sin = sin.astype(x.dtype)
    return jnp.concatenate([x1 * cos - x2 * sin, x2 * cos + x1 * sin], axis=-1)

def t5_bucket(dist):
    n = jnp.maximum(dist, 0)
    max_exact = REL_BUCKETS // 2
    large = max_exact + (jnp.log(jnp.maximum(n, 1).astype(jnp.float32) / max_exact)
                         / math.log(REL_MAX_DIST / max_exact)
                         * (REL_BUCKETS - max_exact)).astype(jnp.int32)
    large = jnp.minimum(large, REL_BUCKETS - 1)
    return jnp.where(n < max_exact, n, large)

def mla_attention(q_nope, q_rope, k_nope, k_rope, v):
    B, S, H, _ = q_nope.shape
    nb = S // BLOCK
    scale = (MLA_NOPE_DIM + MLA_ROPE_DIM) ** -0.5
    qn = q_nope.reshape(B, nb, BLOCK, H, MLA_NOPE_DIM).transpose(1, 0, 2, 3, 4)
    qr = q_rope.reshape(B, nb, BLOCK, H, MLA_ROPE_DIM).transpose(1, 0, 2, 3, 4)
    k_pos = jnp.arange(S)

    def one_block(args):
        qn_b, qr_b, i = args
        s = (jnp.einsum('bqhd,bkhd->bhqk', qn_b, k_nope)
             + jnp.einsum('bqhr,bkr->bhqk', qr_b, k_rope)).astype(jnp.float32) * scale
        q_pos = i * BLOCK + jnp.arange(BLOCK)
        causal = k_pos[None, :] <= q_pos[:, None]
        s = jnp.where(causal, s, -jnp.inf)
        p = jax.nn.softmax(s, axis=-1).astype(v.dtype)
        return jnp.einsum('bhqk,bkhd->bqhd', p, v)

    out = lax.map(one_block, (qn, qr, jnp.arange(nb)))
    return out.transpose(1, 0, 2, 3, 4).reshape(B, S, H * MLA_V_DIM)

def swa_attention(q, k, v, sinks, rel_table):
    B, S, _ = q.shape
    nb = S // BLOCK
    q = q.reshape(B, nb, BLOCK, SWA_KV_HEADS, SWA_GROUP, SWA_HEAD_DIM)
    k = k.reshape(B, nb, BLOCK, SWA_KV_HEADS, SWA_HEAD_DIM)
    v = v.reshape(B, nb, BLOCK, SWA_KV_HEADS, SWA_HEAD_DIM)

    def band(t):
        prev = jnp.pad(t[:, :-1], ((0, 0), (1, 0), (0, 0), (0, 0), (0, 0)))
        return jnp.concatenate([prev, t], axis=2)

    kb, vb = band(k), band(v)
    s = jnp.einsum('bnqhgd,bnkhd->bhgnqk', q, kb).astype(jnp.float32) * SWA_HEAD_DIM ** -0.5
    qi = jnp.arange(BLOCK)[:, None]
    kj = jnp.arange(2 * BLOCK)[None, :]
    dist = qi + BLOCK - kj
    in_window = (dist >= 0) & (dist < WINDOW)
    has_prev = (jnp.arange(nb)[:, None, None] > 0) | (kj >= BLOCK)[None]
    mask = in_window[None] & has_prev
    bias = rel_table.astype(jnp.float32)[t5_bucket(dist)]
    bias = bias.transpose(2, 0, 1).reshape(SWA_KV_HEADS, SWA_GROUP, 1, BLOCK, 2 * BLOCK)
    s = jnp.where(mask[None, None, None], s + bias[None], -jnp.inf)
    sink = sinks.astype(jnp.float32).reshape(SWA_KV_HEADS, SWA_GROUP)[None, :, :, None, None]
    m = jnp.maximum(jnp.max(s, axis=-1), sink)
    p = jnp.exp(s - m[..., None])
    denom = jnp.sum(p, axis=-1) + jnp.exp(sink - m)
    p = (p / denom[..., None]).astype(vb.dtype)
    out = jnp.einsum('bhgnqk,bnkhd->bnqhgd', p, vb)
    return out.reshape(B, S, SWA_WIDTH)

def hybrid_mixer(h, w_in, mla_q_norm, mla_w_q_up, mla_kv_norm, mla_w_kv_up,
                 swa_sinks, rel_table, w_o_mla, w_o_swa, w_out):
    B, S, _ = h.shape
    offsets = [int(o) for o in np.cumsum(IN_SPLITS)[:-1]]
    c_q, c_kv, k_r, q_s, k_s, v_s, gates = jnp.split(h @ w_in, offsets, axis=-1)
    pos = jnp.arange(S)
    q = (rms_norm(c_q, mla_q_norm) @ mla_w_q_up).reshape(B, S, MLA_HEADS, MLA_NOPE_DIM + MLA_ROPE_DIM)
    kv = (rms_norm(c_kv, mla_kv_norm) @ mla_w_kv_up).reshape(B, S, MLA_HEADS, MLA_NOPE_DIM + MLA_V_DIM)
    cos, sin = rope_angles(pos, MLA_ROPE_DIM)
    q_rope = apply_rope(q[..., MLA_NOPE_DIM:], cos[:, None, :], sin[:, None, :])
    k_rope = apply_rope(k_r, cos, sin)
    o_a = mla_attention(q[..., :MLA_NOPE_DIM], q_rope, kv[..., :MLA_NOPE_DIM], k_rope, kv[..., MLA_NOPE_DIM:])
    o_b = swa_attention(q_s, k_s, v_s, swa_sinks, rel_table)
    g = jax.nn.sigmoid(gates.astype(jnp.float32)).reshape(B, S, N_BRANCHES, D_MODEL)
    merged = g[:, :, 0] * (o_a @ w_o_mla).astype(jnp.float32) + g[:, :, 1] * (o_b @ w_o_swa).astype(jnp.float32)
    return merged.astype(h.dtype) @ w_out

def conv_ffn(h, w_up, conv_w, conv_b, w_down):
    S = h.shape[1]
    a, b = jnp.split(h @ w_up, 2, axis=-1)
    ap = jnp.pad(a, ((0, 0), (CONV_WIDTH - 1, 0), (0, 0)))
    c = conv_b
    for j in range(CONV_WIDTH):
        c = c + conv_w[j] * ap[:, j:j + S]
    return (jax.nn.gelu(c, approximate=True) * b) @ w_down

def first_inputs(seed: int = 0) -> dict:
    key = jax.random.key(seed)
    ks = jax.random.split(key, 24)
    L = DEPTH
    f32 = jnp.float32

    def w(k, shape, fan_in):
        return jax.random.normal(k, shape, f32) * fan_in ** -0.5

    def gain(k, shape):
        return 1.0 + 0.05 * jax.random.normal(k, shape, f32)

    return {
        "x": jax.random.normal(ks[0], (BATCH, SEQ, D_MODEL), f32),
        "norm_mix_pre": gain(ks[1], (L, D_MODEL)),
        "norm_mix_post": gain(ks[2], (L, D_MODEL)),
        "norm_ffn_pre": gain(ks[3], (L, D_MODEL)),
        "norm_ffn_post": gain(ks[4], (L, D_MODEL)),
        "w_in": w(ks[5], (L, D_MODEL, IN_COLS), D_MODEL),
        "mla_q_norm": gain(ks[6], (L, MLA_Q_RANK)),
        "mla_w_q_up": w(ks[7], (L, MLA_Q_RANK, MLA_HEADS * (MLA_NOPE_DIM + MLA_ROPE_DIM)), MLA_Q_RANK),
        "mla_kv_norm": gain(ks[8], (L, MLA_KV_RANK)),
        "mla_w_kv_up": w(ks[9], (L, MLA_KV_RANK, MLA_HEADS * (MLA_NOPE_DIM + MLA_V_DIM)), MLA_KV_RANK),
        "swa_sinks": jax.random.normal(ks[10], (L, SWA_Q_HEADS), f32),
        "rel_bias_table": 0.5 * jax.random.normal(ks[11], (REL_BUCKETS, SWA_Q_HEADS), f32),
        "w_o_mla": w(ks[12], (L, MLA_WIDTH, D_MODEL), MLA_WIDTH),
        "w_o_swa": w(ks[13], (L, SWA_WIDTH, D_MODEL), SWA_WIDTH),
        "w_out": w(ks[14], (L, D_MODEL, D_MODEL), D_MODEL),
        "ffn_w_up": w(ks[15], (L, D_MODEL, 2 * D_FF), D_MODEL),
        "ffn_conv_w": w(ks[16], (L, CONV_WIDTH, D_FF), CONV_WIDTH),
        "ffn_conv_b": 0.01 * jax.random.normal(ks[17], (L, D_FF), f32),
        "ffn_w_down": w(ks[18], (L, D_FF, D_MODEL), D_FF),
    }

def first_block(x, norm_mix_pre, norm_mix_post, norm_ffn_pre, norm_ffn_post, w_in,
              mla_q_norm, mla_w_q_up, mla_kv_norm, mla_w_kv_up, swa_sinks, rel_bias_table,
              w_o_mla, w_o_swa, w_out, ffn_w_up, ffn_conv_w, ffn_conv_b, ffn_w_down):
    for l in range(DEPTH):
        h = rms_norm(x, norm_mix_pre[l])
        y = hybrid_mixer(h, w_in[l], mla_q_norm[l], mla_w_q_up[l], mla_kv_norm[l], mla_w_kv_up[l],
                         swa_sinks[l], rel_bias_table, w_o_mla[l], w_o_swa[l], w_out[l])
        x = x + rms_norm(y, norm_mix_post[l])
        h = rms_norm(x, norm_ffn_pre[l])
        y = conv_ffn(h, ffn_w_up[l], ffn_conv_w[l], ffn_conv_b[l], ffn_w_down[l])
        x = x + rms_norm(y, norm_ffn_post[l])
    return x


HEAD_DIM = 128
GRID_W = 64
Q_BLOCK = 128
A_Q_HEADS = 8
A_KV_HEADS = 2
A_GROUP = A_Q_HEADS // A_KV_HEADS
B_HEADS = 8
WIN_ROWS_MAX = 8
WIN_COLS = 16
A_WIDTH = A_Q_HEADS * HEAD_DIM
B_WIDTH = B_HEADS * HEAD_DIM
MIX_WIDTH = A_WIDTH + B_WIDTH
A_KV_WIDTH = A_KV_HEADS * HEAD_DIM
IN_WIDTH = A_WIDTH + 2 * A_KV_WIDTH + 3 * B_WIDTH
D_FF_2 = 4 * D_MODEL
PLE_DIM = 256
ROPE_AXIS_DIM = HEAD_DIM // 2
NORM_EPS = 1e-6


def rms_norm_2(x, g):
    xf = x.astype(jnp.float32)
    y = xf * lax.rsqrt(jnp.mean(xf * xf, axis=-1, keepdims=True) + NORM_EPS)
    return (y * g.astype(jnp.float32)).astype(x.dtype)

def rope_half(x, ang):
    n = ang.shape[-1]
    shape = (1, ang.shape[0]) + (1,) * (x.ndim - 3) + (n,)
    cos = jnp.cos(ang).reshape(shape)
    sin = jnp.sin(ang).reshape(shape)
    xf = x.astype(jnp.float32)
    x1, x2 = xf[..., :n], xf[..., n:]
    return jnp.concatenate([x1 * cos - x2 * sin, x2 * cos + x1 * sin], axis=-1).astype(x.dtype)

def axial_rope(x, ang_row, ang_col):
    return jnp.concatenate([rope_half(x[..., :ROPE_AXIS_DIM], ang_row),
                            rope_half(x[..., ROPE_AXIS_DIM:], ang_col)], axis=-1)

def to_blocks(a):
    b, s = a.shape[0], a.shape[1]
    a = a.reshape((b, s // Q_BLOCK, Q_BLOCK) + a.shape[2:])
    return jnp.moveaxis(a, 1, 0)

def from_blocks(a):
    a = jnp.moveaxis(a, 0, 1)
    return a.reshape((a.shape[0], a.shape[1] * a.shape[2]) + a.shape[3:])

def global_gqa(q, k, v):
    scale = 1.0 / math.sqrt(HEAD_DIM)

    def block(qb):
        s = jnp.einsum('bqkgd,bskd->bkgqs', qb, k).astype(jnp.float32) * scale
        w = jax.nn.softmax(s, axis=-1).astype(v.dtype)
        return jnp.einsum('bkgqs,bskd->bqkgd', w, v)

    o = lax.map(block, to_blocks(q))
    return from_blocks(o)

def neighbourhood_attn(q, k, v, rpb, rows):
    s_len = q.shape[1]
    win_r = min(WIN_ROWS_MAX, rows)
    scale = 1.0 / math.sqrt(HEAD_DIM)
    t_blocks = jnp.arange(s_len, dtype=jnp.int32).reshape(s_len // Q_BLOCK, Q_BLOCK)
    ar_r = jnp.arange(win_r, dtype=jnp.int32)
    ar_c = jnp.arange(WIN_COLS, dtype=jnp.int32)

    def block(args):
        qb, t = args
        r = t // GRID_W
        c = t % GRID_W
        r0 = jnp.clip(r - win_r // 2, 0, rows - win_r)
        c0 = jnp.clip(c - WIN_COLS // 2, 0, GRID_W - WIN_COLS)
        kr = r0[:, None] + ar_r[None, :]
        kc = c0[:, None] + ar_c[None, :]
        idx = (kr[:, :, None] * GRID_W + kc[:, None, :]).reshape(Q_BLOCK, win_r * WIN_COLS)
        dr = kr - r[:, None] + (WIN_ROWS_MAX - 1)
        dc = kc - c[:, None] + (WIN_COLS - 1)
        bias = rpb[:, dr[:, :, None], dc[:, None, :]].reshape(B_HEADS, Q_BLOCK, win_r * WIN_COLS)
        kg = k[:, idx]
        vg = v[:, idx]
        s = jnp.einsum('bqhd,bqnhd->bhqn', qb, kg).astype(jnp.float32) * scale
        s = s + bias.astype(jnp.float32)[None]
        w = jax.nn.softmax(s, axis=-1).astype(vg.dtype)
        return jnp.einsum('bhqn,bqnhd->bqhd', w, vg)

    o = lax.map(block, (to_blocks(q), t_blocks))
    return from_blocks(o)

def second_inputs(seed: int = 0) -> dict:
    key = jax.random.key(seed)
    ks = jax.random.split(key, 20)
    f32 = jnp.float32

    def w(k, shape, fan_in):
        return jax.random.normal(k, shape, f32) * (fan_in ** -0.5)

    def gain(k, shape):
        return 1.0 + 0.05 * jax.random.normal(k, shape, f32)

    return {
        "x": jax.random.normal(ks[0], (BATCH, SEQ, D_MODEL), f32),
        "p": jax.random.normal(ks[1], (DEPTH, BATCH, SEQ, PLE_DIM), f32),
        "pre_mix_norm": gain(ks[2], (DEPTH, D_MODEL)),
        "w_in": w(ks[3], (DEPTH, D_MODEL, IN_WIDTH), D_MODEL),
        "q_norm": gain(ks[4], (DEPTH, HEAD_DIM)),
        "k_norm": gain(ks[5], (DEPTH, HEAD_DIM)),
        "rel_pos_bias": 0.1 * jax.random.normal(ks[6], (DEPTH, B_HEADS, 2 * WIN_ROWS_MAX - 1, 2 * WIN_COLS - 1), f32),
        "w_o": w(ks[7], (DEPTH, MIX_WIDTH, D_MODEL), MIX_WIDTH),
        "post_mix_norm": gain(ks[8], (DEPTH, D_MODEL)),
        "pre_mlp_norm": gain(ks[9], (DEPTH, D_MODEL)),
        "w_up": w(ks[10], (DEPTH, D_MODEL, D_FF_2), D_MODEL),
        "w_down": w(ks[11], (DEPTH, D_FF_2, D_MODEL), D_FF_2),
        "post_mlp_norm": gain(ks[12], (DEPTH, D_MODEL)),
        "pre_ple_norm": gain(ks[13], (DEPTH, D_MODEL)),
        "w_ple_gate": w(ks[14], (DEPTH, D_MODEL, D_MODEL), D_MODEL),
        "w_ple_proj": w(ks[15], (DEPTH, PLE_DIM, D_MODEL), PLE_DIM),
        "post_ple_norm": gain(ks[16], (DEPTH, D_MODEL)),
    }

def second_block(x, p, pre_mix_norm, w_in, q_norm, k_norm, rel_pos_bias, w_o, post_mix_norm,
              pre_mlp_norm, w_up, w_down, post_mlp_norm, pre_ple_norm, w_ple_gate, w_ple_proj,
              post_ple_norm):
    b, s_len, _ = x.shape
    rows = s_len // GRID_W
    t = jnp.arange(s_len, dtype=jnp.int32)
    row = (t // GRID_W).astype(jnp.float32)
    col = (t % GRID_W).astype(jnp.float32)
    n_freq = ROPE_AXIS_DIM // 2
    freqs = ROPE_THETA ** (-jnp.arange(n_freq, dtype=jnp.float32) / n_freq)
    ang_row = row[:, None] * freqs[None, :]
    ang_col = col[:, None] * freqs[None, :]

    h = x
    for i in range(DEPTH):
        xn = rms_norm_2(h, pre_mix_norm[i])
        proj = xn @ w_in[i]
        o0 = A_WIDTH
        o1 = o0 + A_KV_WIDTH
        o2 = o1 + A_KV_WIDTH
        o3 = o2 + B_WIDTH
        o4 = o3 + B_WIDTH
        qa = proj[..., :o0].reshape(b, s_len, A_KV_HEADS, A_GROUP, HEAD_DIM)
        ka = proj[..., o0:o1].reshape(b, s_len, A_KV_HEADS, HEAD_DIM)
        va = proj[..., o1:o2].reshape(b, s_len, A_KV_HEADS, HEAD_DIM)
        qb = proj[..., o2:o3].reshape(b, s_len, B_HEADS, HEAD_DIM)
        kb = proj[..., o3:o4].reshape(b, s_len, B_HEADS, HEAD_DIM)
        vb = proj[..., o4:].reshape(b, s_len, B_HEADS, HEAD_DIM)

        qa = axial_rope(rms_norm_2(qa, q_norm[i]), ang_row, ang_col)
        ka = axial_rope(rms_norm_2(ka, k_norm[i]), ang_row, ang_col)
        out_a = global_gqa(qa, ka, va).reshape(b, s_len, A_WIDTH)
        out_b = neighbourhood_attn(qb, kb, vb, rel_pos_bias[i], rows).reshape(b, s_len, B_WIDTH)

        mix = jnp.concatenate([out_a, out_b], axis=-1) @ w_o[i]
        h = h + rms_norm_2(mix, post_mix_norm[i])

        m = rms_norm_2(h, pre_mlp_norm[i]) @ w_up[i]
        m = jnp.square(jax.nn.relu(m)) @ w_down[i]
        h = h + rms_norm_2(m, post_mlp_norm[i])

        gate = jax.nn.sigmoid(rms_norm_2(h, pre_ple_norm[i]) @ w_ple_gate[i])
        e = (p[i] @ w_ple_proj[i]) * gate
        h = h + rms_norm_2(e, post_ple_norm[i])
    return h


def setup_inputs(seed=0):
    out = dict(first_inputs(seed))
    for name, value in second_inputs(seed + 1).items():
        if name != "x":
            out[name + "_2"] = value
    return out


def reference(
    x, norm_mix_pre, norm_mix_post, norm_ffn_pre, norm_ffn_post, w_in, mla_q_norm, mla_w_q_up,
    mla_kv_norm, mla_w_kv_up, swa_sinks, rel_bias_table, w_o_mla, w_o_swa, w_out, ffn_w_up,
    ffn_conv_w, ffn_conv_b, ffn_w_down, p_2, pre_mix_norm_2, w_in_2, q_norm_2, k_norm_2,
    rel_pos_bias_2, w_o_2, post_mix_norm_2, pre_mlp_norm_2, w_up_2, w_down_2, post_mlp_norm_2,
    pre_ple_norm_2, w_ple_gate_2, w_ple_proj_2, post_ple_norm_2,
):
    x = first_block(
        x, norm_mix_pre, norm_mix_post, norm_ffn_pre, norm_ffn_post, w_in, mla_q_norm,
        mla_w_q_up, mla_kv_norm, mla_w_kv_up, swa_sinks, rel_bias_table, w_o_mla, w_o_swa,
        w_out, ffn_w_up, ffn_conv_w, ffn_conv_b, ffn_w_down,
    )
    return second_block(
        x, p_2, pre_mix_norm_2, w_in_2, q_norm_2, k_norm_2, rel_pos_bias_2, w_o_2,
        post_mix_norm_2, pre_mlp_norm_2, w_up_2, w_down_2, post_mlp_norm_2, pre_ple_norm_2,
        w_ple_gate_2, w_ple_proj_2, post_ple_norm_2,
    )


_drawn_inputs = setup_inputs


def setup_inputs(seed=0):
    import zlib

    import numpy as np

    out = dict(_drawn_inputs(seed))
    spreads = {}
    factors = {'ffn_conv_b': 8.0,
     'q_norm_2': 8.0,
     'k_norm_2': 8.0,
     'pre_ple_norm_2': 7.006,
     'post_ple_norm_2': 2.73,
     'rel_pos_bias_2': 6.293}
    for name, (base, spread) in spreads.items():
        noise = np.random.default_rng([zlib.crc32(name.encode()), seed]).standard_normal(out[name].shape)
        drawn = base * np.exp(spread * noise) if base else spread * noise
        out[name] = __import__('jax').numpy.asarray(drawn.astype(out[name].dtype))
    for name, factor in factors.items():
        out[name] = (out[name] * factor).astype(out[name].dtype)
    return out
```

```python
import math
from contextlib import ExitStack

import numpy as np

import concourse.bass as bass
from concourse import mybir

F32 = mybir.dt.float32
F32R = mybir.dt.float32r
ALU = mybir.AluOpType
ACT = mybir.ActivationFunctionType
AX_X = mybir.AxisListType.X

P = 128
SEQ = 256
TB = SEQ // P
D = 2048
KT = D // P
EPS = 1e-6
FF1 = 5632
FF2 = 8192
H1A, H1B = 32, FF1 // P - 32
H2A = FF2 // P // 2
MLA_HEADS = 16
SWA_HEADS = 32
WINDOW = 128
BUCKETS = 32
NEG = -1e30
COLS = 512
UNIT = 2048
HALF = UNIT // 2
RAW = 4
SLOTS = 4
LEAD = 2
MLA_SCALE = (128 + 64) ** -0.5
SWA_SCALE = 64 ** -0.5
HEAD_SCALE = 1.0 / math.sqrt(128)
BAND = 3 * P
RPB_W = 31 + 2 * 48

STAGES = {
    "cq": (8, 8), "k1": (3, 3), "qs": (16, 4), "qup": (6, 6), "kvk": (2, 2), "kvv": (2, 2),
    "merge": (64, 4), "wout": (16, 8), "upA": (2 * H1A, 4), "dnA": (H1A, 16), "upB": (2 * H1B, 4),
    "dnB": (H1B, H1B), "v2": (10, 10), "qk2": (26, 26), "wo2": (16, 8), "up2a": (H2A, 4),
    "dn2a": (H2A, 16), "up2b": (H2A, 4), "dn2b": (H2A, 16), "proj": (2, 2), "gate": (16, 16),
}
UNIT0 = {}
_u = 0
for _n, (_c, _) in STAGES.items():
    UNIT0[_n] = _u
    _u += _c
UNITS = _u
TILES = {}
_t = _a = _d = 0
for _n, _c, _ca, _cd in (("k1", 3, 2, 1), ("qs", 16, 8, 8), ("qup", 24, 12, 12), ("kvk", 16, 8, 8),
                         ("merge", 64, 32, 32), ("upA", 2 * H1A, 0, 2 * H1A), ("upB", 2 * H1B, 0, 2 * H1B),
                         ("qk2", 26, 18, 8), ("up2a", H2A, H2A, 0), ("up2b", H2A, H2A, 0)):
    TILES[_n] = (_t, _a, _d)
    _t, _a, _d = _t + _c, _a + _ca, _d + _cd
TILES["end"] = (_t, _a, _d)
CHUNKS = {}
_c = 0
for _n, _k in (("cq", 2), ("kvv", 4), ("wout", 4), ("dnA", 4), ("dnB", 4), ("v2", 5), ("wo2", 4),
               ("dn2a", 4), ("dn2b", 4), ("proj", 4), ("gate", 4)):
    CHUNKS[_n] = _c
    _c += _k
HID0 = {"upA": 0, "upB": H1A, "up2a": H1A + H1B, "up2b": H1A + H1B + H2A}

C_ID, C_SWAP, C_ONES = 0, 128, 256
C_COSM, C_SINM, C_COSA, C_SINA = 384, 640, 896, 1152
C_CAUSAL, C_NB, C_END = 1408, 1792, 1856
G_QN, G_KVN, G_Q2, G_K2, G_CONV, G_SINK, G_END = 0, 4, 6, 7, 8, 8 + 44 * 4, 8 + 44 * 4 + 32

N_SWA, N_MLA, N_A2, N_B2 = SWA_HEADS // 2, MLA_HEADS // 2, 4, 4


def attention_jobs(block):
    if block == 1:
        return [("swa", j) for j in range(N_SWA)] + [("mla", j) for j in range(N_MLA)]
    return [("a2", j) for j in range(N_A2)] + [("b2", j) for j in range(N_B2)]


def score_reads(g):
    return g + 1 if g < N_SWA + N_MLA else g + 1 - N_A2


def stage_loop(engine, name, body):
    units, group = STAGES[name]
    turns = units // group
    if turns > 1:
        with engine.Fori(0, turns) as i:
            for k in range(group):
                body(i, k)
    else:
        for k in range(units):
            body(0, k)


class Steps:

    def __init__(self, engine, sem):
        self.engine, self.sem, self.n, self.i, self.per, self.at = engine, sem, 0, 0, 0, 0

    def loop(self, i, per):
        self.i, self.per, self.at = i, per, 0

    def end(self, turns):
        self.n += self.per * turns
        self.i = self.per = self.at = 0

    def __call__(self, ins):
        ins.then_inc(self.sem, 1)
        if self.per:
            self.at = self.at % self.per + 1
            self.engine.wait_ge(self.sem, self.i * self.per + (self.n + self.at))
        else:
            self.n += 1
            self.engine.wait_ge(self.sem, self.n)


def program(nc, stream, x, consts, params, gain_rows, bucket_table, bucket_hot, rpb, p_t, out):
    with ExitStack() as ctx:
        base = (nc.sbuf_base + 63) // 64 * 64
        KB = 1024

        def at(name, kb, shape, dtype=F32):
            return nc.alloc_sbuf_tensor_at(name, shape, dtype, offset=base + int(kb * KB))

        def sem(name):
            return ctx.enter_context(nc.semaphore(name))

        raw = at("raw", 0, [P, RAW, UNIT])
        w_hi = at("w_hi", 32, [P, SLOTS, HALF], F32R)
        w_lo = at("w_lo", 48, [P, SLOTS, HALF], F32R)
        xt_hi = at("xt_hi", 64, [P, KT, SEQ], F32R)
        xt_lo = at("xt_lo", 80, [P, KT, SEQ], F32R)
        qs = at("qs", 96, [P, 16, TB, P])
        qn = at("qn", 112, [P, 16, TB, P])
        kn = at("kn", 128, [P, 16, SEQ])
        v1 = at("v1", 144, [P, TB, D])
        x0 = at("x0", 128, [P, TB, D])
        xn0 = at("xn0", 144, [P, TB, D])
        c1 = at("c1", 128, [P, TB, 768])
        c_junk = at("c_junk", 144, [P, TB, 768])
        kr_a = at("kr_a", 112, [P, SEQ])
        kr_b = at("kr_b", 113, [P, SEQ])
        qr = at("qr", 160, [P, 8, SEQ])
        ks = at("ks", 168, [P, 4, SEQ])
        vs = at("vs", 172, [P, TB, 4, 64])
        ct_hi = at("ct_hi", 180, [P, 6, SEQ], F32R)
        ct_lo = at("ct_lo", 186, [P, 6, SEQ], F32R)
        pr1 = at("pr1", 174, [P, 3, 2, BAND])
        pt1 = at("pt1", 183, [P, 2, 2, BAND])
        os_lo = at("os_lo", 96, [P, 16, SEQ], F32R)
        om_lo = at("om_lo", 112, [P, 16, SEQ], F32R)
        om_hi = at("om_hi", 128, [P, 16, SEQ], F32R)
        os_hi = at("os_hi", 144, [P, 16, SEQ], F32R)
        mg_hi = at("mg_hi", 160, [P, 16, SEQ], F32R)
        mg_lo = at("mg_lo", 176, [P, 16, SEQ], F32R)
        y = at("y", 96, [P, TB, D])
        res = at("res", 112, [P, TB, D])
        hid_hi = at("hid_hi", 128, [P, 32, SEQ], F32R)
        hid_lo = at("hid_lo", 160, [P, 32, SEQ], F32R)
        v2 = at("v2", 128, [P, TB, 1280])
        ka2 = at("ka2", 138, [P, 2, SEQ])
        qa2 = at("qa2", 140, [P, 8, TB, P])
        qb2 = at("qb2", 148, [P, 8, TB, P])
        kb2 = at("kb2", 156, [P, 8, SEQ])
        nb_bias = at("nb_bias", 164, [P, 2, 2, 2, SEQ])
        hn_x = at("hn_x", 172, [P, 2, SEQ])
        hn_sq = at("hn_sq", 174, [P, 2, SEQ])
        hn_r = at("hn_r", 176, [P, SEQ])
        hn_a = at("hn_a", 177, [P, SEQ])
        hn_b = at("hn_b", 178, [P, SEQ])
        pr2 = at("pr2", 96, [P, 3, 2, 2, SEQ])
        pt2 = at("pt2", 180, [P, 2, 2, 2, SEQ])
        pe_t = at("pe_t", 128, [P, 2, SEQ])
        pe_hi = at("pe_hi", 130, [P, 2, SEQ], F32R)
        pe_lo = at("pe_lo", 132, [P, 2, SEQ], F32R)
        emb = at("emb", 134, [P, TB, D])
        sig = at("sig", 150, [P, 2, COLS])
        cst = at("cst", 192, [P, C_END])
        par = at("par", 199.25, [P, G_END])
        gr_post = at("gr_post", 200.25, [P, COLS])
        gr_pre = at("gr_pre", 202.25, [P, COLS])
        squares_xt = at("squares_xt", 64, [P, TB, COLS])
        squares_hid = at("squares_hid", 154, [P, TB, COLS])
        conv = at("conv", 204.25, [P, SEQ])
        act_tmp = at("act_tmp", 205.25, [P, SEQ])
        hid_f = at("hid_f", 206.25, [P, SEQ])
        kr = at("kr", 204.25, [P, SEQ])
        sg = at("sg", 204.25, [P, 2, SEQ])
        mg_f = at("mg_f", 206.25, [P, SEQ])
        rope_b = at("rope_b", 206.25, [P, SEQ])
        stat = at("stat", 207.25, [P, 96])
        sw_bias = at("sw_bias", 200.25, [P, 2, 2, SEQ])
        table = at("table", 160, [BUCKETS + 1, 32])
        hot = at("hot", 161, [BUCKETS + 1, BAND])
        row_bias = at("row_bias", 163, [SWA_HEADS, BAND])
        ps = ctx.enter_context(nc.psum_tensor("ps", [P, 8, COLS], F32))
        band_dram = nc.dram_tensor("band_bias", (SWA_HEADS, BAND), F32, kind="Internal").ap()

        ident = cst[:, C_ID:C_ID + P]
        swap = cst[:, C_SWAP:C_SWAP + P]
        ones = cst[:, C_ONES:C_ONES + P]
        ss = stat[:, 0:2]
        ss_part = stat[:, 2:10]
        rstd = stat[:, 10:12]
        ms = stat[:, 12:14]
        ss_c = stat[:, 14:18]
        rstd_c = stat[:, 18:22]
        minus_half = stat[:, 22:26]
        eps_col = stat[:, 26:27]
        mx = stat[:, 28:40]
        nm = stat[:, 40:48]
        rs = stat[:, 48:56]
        es = stat[:, 56:64]
        minus_sink = stat[:, 64:96]
        sink = par[:, G_SINK:G_SINK + 32]

        raw_loaded = [sem(f"raw_loaded{s}") for s in range(RAW)]
        hi_ready, lo_ready, weights_used = sem("hi_ready"), sem("lo_ready"), sem("weights_used")
        t_act, t_dve, c_act, c_dve = sem("t_act"), sem("t_dve"), sem("c_act"), sem("c_dve")
        consts_in, x_in, res_in, post_in, pre_in = (sem(n) for n in ("consts_in", "x_in", "res_in", "post_in", "pre_in"))
        memset_done = sem("memset_done")
        g_post, g_pre, post_scaled, added, squared, meaned, rstd_ready, normed = (
            sem(n) for n in ("g_post", "g_pre", "post_scaled", "added", "squared", "meaned", "rstd_ready", "normed"))
        turned, xt_hi_ready, xt_lo_ready = sem("turned"), sem("xt_hi_ready"), sem("xt_lo_ready")
        dve_step, act_step, pool_step = sem("dve_step"), sem("act_step"), sem("pool_step")
        c_meaned, c_rstd, c_scaled, c_turned, ct_hi_ready, ct_lo_ready = (
            sem(n) for n in ("c_meaned", "c_rstd", "c_scaled", "c_turned", "ct_hi_ready", "ct_lo_ready"))
        row_bias_mm, row_bias_out, band_stored, table_in = (
            sem(n) for n in ("row_bias_mm", "row_bias_out", "band_stored", "table_in"))
        kr_moved, kr_ready, kr_copied, ks_copied = (
            sem(n) for n in ("kr_moved", "kr_ready", "kr_copied", "ks_copied"))
        qr_swapped, qr_ready = sem("qr_swapped"), sem("qr_ready")
        bias_in, bias_masked = [sem("bias_in0"), sem("bias_in1")], sem("bias_masked")
        scored, minus_max, exp_done, denom_ready, p_normed, p_turned = (
            sem(n) for n in ("scored", "minus_max", "exp_done", "denom_ready", "p_normed", "p_turned"))
        score_read, sink_exp = sem("score_read"), sem("sink_exp")
        pt_act, pt_dve, pv_done, o_act, o_dve = (sem(n) for n in ("pt_act", "pt_dve", "pv_done", "o_act", "o_dve"))
        om_hi_ready, om_lo_ready, gate_sig, merged, mg_hi_ready, mg_lo_ready = (
            sem(n) for n in ("om_hi_ready", "om_lo_ready", "gate_sig", "merged", "mg_hi_ready", "mg_lo_ready"))
        conved, activated, hid_product, hid_hi_ready, hid_lo_ready = (
            sem(n) for n in ("conved", "activated", "hid_product", "hid_hi_ready", "hid_lo_ready"))
        hn_scaled, hn_summed, hn_rooted, hn_done = (sem(n) for n in ("hn_scaled", "hn_summed", "hn_rooted", "hn_done"))
        pe_in, pe_hi_ready, pe_lo_ready, sig_ready, e_ready = (
            sem(n) for n in ("pe_in", "pe_hi_ready", "pe_lo_ready", "sig_ready", "e_ready"))
        out_done, y_squared = sem("out_done"), sem("y_squared")

        def flat(ap):
            return ap.rearrange("p a b -> p (a b)")

        def halves(ap):
            return ap.rearrange("p (a t) -> p a t", t=P)

        block = ctx.enter_context(nc.Block())

        @block.sync
        def _(sp):
            for u in range(RAW):
                sp.dma_start(raw[:, u, :], stream[u]).then_inc(raw_loaded[u], 16)
            turns = UNITS // RAW
            with nc.sync.Fori(1, turns) as i:
                for s in range(RAW):
                    sp.wait_ge(lo_ready, i * (2 * RAW) + (2 * (s - RAW) + 2))
                    sp.dma_start(raw[:, s, :], stream[bass.ds(i * RAW + s, 1)].rearrange("u p c -> p (u c)")
                                 ).then_inc(raw_loaded[s], 16)
            for u in range(turns * RAW, UNITS):
                sp.wait_ge(lo_ready, 2 * (u - RAW) + 2)
                sp.dma_start(raw[:, u % RAW, :], stream[u]).then_inc(raw_loaded[u % RAW], 16)

        @block.tensor
        def _(pe):
            mm = pe.matmul

            def three(dst, lhs, rhs, n_lhs, n_rhs, first, last):
                mm(dst, lhs[0][n_lhs], rhs[0][n_rhs], start=first, stop=False)
                mm(dst, lhs[0][n_lhs], rhs[1][n_rhs], start=False, stop=False)
                return mm(dst, lhs[1][n_lhs], rhs[0][n_rhs], start=False, stop=last)

            def half_at(name, i, k, j):
                u = UNIT0[name] + k
                pe.wait_ge(lo_ready, i * (2 * STAGES[name][1]) + (2 * u + j + 1))
                return (2 * u + j) % SLOTS

            def tile_free(name, i, k, n=0):
                _, a, d = TILES[name]
                if k >= 4 or not isinstance(i, int):
                    if k % 2 == 0:
                        pe.wait_ge(t_act, i * (STAGES[name][1] // 2) + (a + k // 2 - 1))
                    else:
                        pe.wait_ge(t_dve, i * (STAGES[name][1] // 2) + (d + k // 2 - 1))

            def all_tiles_read(name):
                _, a, d = TILES[name]
                pe.wait_ge(t_act, a) if a else None
                pe.wait_ge(t_dve, d) if d else None

            def chunks_read(n):
                if n > 0:
                    pe.wait_ge(c_act, n)
                    pe.wait_ge(c_dve, n)

            def t_stage(name, acts, free):
                t0 = TILES[name][0]

                def body(i, k):
                    free(i, k)
                    for j in range(2):
                        s = half_at(name, i, k, j)
                        wh = w_hi[:, s, :].rearrange("p (c n) -> p c n", n=P)
                        wl = w_lo[:, s, :].rearrange("p (c n) -> p c n", n=P)
                        hi, lo = acts(k)
                        for c in range(8):
                            kt = 8 * j + c
                            dst = ps[:, (t0 + k) % 4, 0:SEQ]
                            last = three(dst, (wh, wl), (hi, lo), (slice(None), c), (slice(None), kt),
                                         kt == 0, kt == KT - 1)
                        last.then_inc(weights_used, 1)
                stage_loop(nc.tensor, name, body)

            def n_stage(name, per_chunk, hi, lo, ready=None):
                c0 = CHUNKS[name]
                group = STAGES[name][1]

                def body(i, k):
                    ch, g = k // per_chunk, k % per_chunk
                    if g == 0 and (ch >= 1 or not isinstance(i, int)):
                        step = group // per_chunk
                        n = c0 + ch - 1
                        pe.wait_ge(c_act, i * step + n)
                        pe.wait_ge(c_dve, i * step + n)
                    if ready:
                        ready(i, k)
                    for j in range(2):
                        s = half_at(name, i, k, j)
                        for c in range(2):
                            kt = 4 * g + 2 * j + c
                            cols = (slice(None), s, slice(c * COLS, (c + 1) * COLS))
                            for tb in range(TB):
                                dst = ps[:, 4 + 2 * ((c0 + ch) % 2) + tb, :]
                                last = three(dst, (hi, lo), (w_hi, w_lo),
                                             (slice(None), kt, slice(tb * P, (tb + 1) * P)), cols,
                                             kt == 0, kt == 4 * per_chunk - 1)
                        last.then_inc(weights_used, 1)
                chunks_read(c0)
                stage_loop(nc.tensor, name, body)

            counts = {"norm": 0, "post": 0, "job": 0}

            def pre_norm(source):
                e = counts["norm"]
                counts["norm"] += 1
                for g in range(8):
                    tb, q = g // 4, g % 4
                    pe.wait_ge(normed, 2 * e + tb + 1)
                    n = 8 * e + g
                    if g >= 4:
                        pe.wait_ge(xt_hi_ready, n - 3)
                        pe.wait_ge(xt_lo_ready, n - 3)
                    for c in range(4):
                        kt = 4 * q + c
                        last = pe.transpose(ps[:, q, c * P:(c + 1) * P],
                                            source[:, tb, kt * P:(kt + 1) * P], ident)
                    last.then_inc(turned, 1)

            def xt_ready():
                pe.wait_ge(xt_lo_ready, 8 * counts["norm"])

            def gains(post, pre, tiles, chunks):
                all_tiles_read(tiles)
                if post:
                    n = counts["post"]
                    counts["post"] += 1
                    pe.wait_ge(post_in, 16 * (n + 1))
                    gain_row_now(gr_post, 0, g_post)
                chunks_read(chunks)
                if pre:
                    pe.wait_ge(pre_in, 16 * (counts["norm"] + 1))
                    gain_row_now(gr_pre, 4, g_pre)
                if post:
                    pe.wait_ge(post_scaled, 2 * counts["post"])

            def gain_row_now(tile, bank, done):
                for j in range(4):
                    last = mm(ps[:, bank + j, :], ones[32 * j:32 * j + 1, :], tile[32 * j:32 * j + 1, :],
                              start=True, stop=True)
                last.then_inc(done, 1)

            pe.wait_ge(consts_in, 16)
            pe.wait_ge(table_in, 32)
            pe.wait_ge(memset_done, 3)
            mm(ps[0:SWA_HEADS, 0, 0:BAND], table[:, :], hot[:, :], start=True, stop=True).then_inc(row_bias_mm, 1)
            pe.wait_ge(row_bias_out, 1)

            gains(False, True, "k1", 0)
            pre_norm(xn0)
            xt_ready()
            n_stage("cq", 4, xt_hi, xt_lo)

            xt = lambda k: (xt_hi, xt_lo)
            t_stage("k1", xt, lambda i, k: None)
            all_tiles_read("qs")
            t_stage("qs", xt, lambda i, k: tile_free("qs", i, k))

            chunks_read(2)
            for kt in range(6):
                src = c1[:, :, kt * P:(kt + 1) * P]
                if kt == 0:
                    pe.wait_ge(c_scaled, 4)
                for tb in range(TB):
                    last = pe.transpose(ps[:, 4 + kt // 2, (kt % 2) * SEQ + tb * P:(kt % 2) * SEQ + (tb + 1) * P],
                                        src[:, tb, :], ident)
                if kt % 2:
                    last.then_inc(c_turned, 1)

            all_tiles_read("qup")
            pe.wait_ge(ct_lo_ready, 4)
            for k in range(6):
                for j in range(2):
                    s = half_at("qup", 0, k, j)
                    for tt in range(2):
                        tile = 4 * k + 2 * j + tt
                        tile_free("qup", 0, tile)
                        wh = w_hi[:, s, :].rearrange("p (t c n) -> p t c n", t=2, n=P)
                        wl = w_lo[:, s, :].rearrange("p (t c n) -> p t c n", t=2, n=P)
                        for kt in range(4):
                            last = three(ps[:, (TILES["qup"][0] + tile) % 4, 0:SEQ], (wh, wl), (ct_hi, ct_lo),
                                         (slice(None), tt, kt), (slice(None), kt), kt == 0, kt == 3)
                    last.then_inc(weights_used, 1)
            pe.wait_ge(ct_lo_ready, 6)
            pe.wait_ge(t_act, TILES["qup"][1] + 4)
            pe.wait_ge(t_dve, TILES["qup"][2] + 4)
            for r in range(4):
                last = mm(ps[:, 4 + r, :], swap, flat(qr[:, 2 * r:2 * r + 2, :]), start=True, stop=True)
                last.then_inc(qr_swapped, 1)
            all_tiles_read("kvk")
            for k in range(2):
                for j in range(2):
                    s = half_at("kvk", 0, k, j)
                    for tt in range(4):
                        tile = 8 * k + 4 * j + tt
                        tile_free("kvk", 0, tile)
                        wh = w_hi[:, s, :].rearrange("p (t c n) -> p t c n", t=4, n=P)
                        wl = w_lo[:, s, :].rearrange("p (t c n) -> p t c n", t=4, n=P)
                        for kt in range(2):
                            last = three(ps[:, (TILES["kvk"][0] + tile) % 4, 0:SEQ], (wh, wl), (ct_hi, ct_lo),
                                         (slice(None), tt, kt), (slice(None), 4 + kt), kt == 0, kt == 1)
                    last.then_inc(weights_used, 1)

            def narrow(name, hi, lo, first_kt):
                for ch in range(4):
                    s = half_at(name, 0, ch // 2, ch % 2)
                    chunks_read(CHUNKS[name] + ch - 1)
                    for kt in range(2):
                        for tb in range(TB):
                            dst = ps[:, 4 + 2 * ((CHUNKS[name] + ch) % 2) + tb, :]
                            last = three(dst, (hi, lo), (w_hi, w_lo),
                                         (slice(None), first_kt + kt, slice(tb * P, (tb + 1) * P)),
                                         (slice(None), s, slice(kt * COLS, (kt + 1) * COLS)), kt == 0, kt == 1)
                    last.then_inc(weights_used, 1)

            pe.wait_ge(qr_ready, 8)
            narrow("kvv", ct_hi, ct_lo, 4)

            def attend(blockno):
                jobs = attention_jobs(blockno)
                g0 = counts["job"]
                counts["job"] += len(jobs)

                def scores(n):
                    kind, j = jobs[n]
                    g = g0 + n
                    if n >= 2 and jobs[n - 2][0] == "a2":
                        pe.wait_ge(exp_done, g - 1)
                    elif n >= 2:
                        pe.wait_ge(score_read, score_reads(g - 2))
                    for h in range(2):
                        bank = ps[:, 2 * (g % 2) + h, :]
                        half = slice(64 * h, 64 * h + 64)
                        if kind == "swa":
                            mm(bank[:, 0:SEQ], qs[half, j, 1, :], ks[half, j // 4, :], start=True, stop=True)
                            last = mm(bank[:, SEQ:BAND], qs[half, j, 0, :], ks[half, j // 4, 0:P],
                                      start=True, stop=True)
                        elif kind == "mla":
                            head = 2 * j + h
                            mm(bank[:, 0:SEQ], qn[:, head, 1, :], kn[:, head, :], start=True, stop=False)
                            mm(bank[:, 0:SEQ], qr[half, j, P:SEQ], kr[half, :], start=False, stop=True)
                            mm(bank[:, SEQ:BAND], qn[:, head, 0, :], kn[:, head, 0:P], start=True, stop=False)
                            last = mm(bank[:, SEQ:BAND], qr[half, j, 0:P], kr[half, 0:P], start=False, stop=True)
                        else:
                            head = 2 * j + h
                            q_t, k_t = (qa2, ka2[:, head // 4, :]) if kind == "a2" else (qb2, kb2[:, head, :])
                            for blk in range(TB):
                                last = mm(bank[:, blk * SEQ:(blk + 1) * SEQ], q_t[:, head, blk, :], k_t,
                                          start=True, stop=True)
                    last.then_inc(scored, 1)

                def turn(n):
                    g = g0 + n
                    pe.wait_ge(p_normed, g + 1)
                    if g >= 1:
                        pe.wait_ge(pt_act, g)
                    if blockno == 2 and n >= 1:
                        pe.wait_ge(pt_dve, n)
                    for h in range(2):
                        bank = ps[:, 4 + h, :]
                        if blockno == 1:
                            pr = pr1[:, g % 3, h, :]
                            pe.transpose(bank[:, 0:P], pr[:, SEQ:BAND], ident)
                            pe.transpose(bank[:, P:SEQ], pr[:, 0:P], ident)
                            last = pe.transpose(bank[:, SEQ:BAND], pr[:, P:SEQ], ident)
                        else:
                            for kt in range(2):
                                for blk in range(TB):
                                    c = (2 * kt + blk) * P
                                    last = pe.transpose(bank[:, c:c + P],
                                                        pr2[:, g % 3, h, blk, kt * P:(kt + 1) * P], ident)
                    last.then_inc(p_turned, 1)

                def values(n):
                    kind, j = jobs[n]
                    g = g0 + n
                    pe.wait_ge(pt_act, g + 1)
                    if blockno == 2:
                        pe.wait_ge(pt_dve, n + 1)
                    if g >= 2:
                        pe.wait_ge(o_act, g - 1)
                    if blockno == 2 and n >= 2:
                        pe.wait_ge(o_dve, n - 1)
                    for h in range(2):
                        dst = ps[:, 6 + g % 2, h * SEQ:(h + 1) * SEQ]
                        if blockno == 1:
                            pt = pt1[:, g % 2, h, :]
                            if kind == "swa":
                                dst = ps[64 * h:64 * h + 64, 6 + g % 2, 0:SEQ]
                                v0, v1_ = (vs[:, kt, j // 4, :] for kt in range(2))
                            else:
                                c = (2 * j + h) * P
                                v0, v1_ = (v1[:, kt, c:c + P] for kt in range(2))
                            mm(dst[:, 0:P], v0, pt[:, 0:P], start=True, stop=True)
                            mm(dst[:, P:SEQ], v0, pt[:, P:SEQ], start=True, stop=False)
                            last = mm(dst[:, P:SEQ], v1_, pt[:, SEQ:BAND], start=False, stop=True)
                        else:
                            head = 2 * j + h
                            c = (head // 4) * P if kind == "a2" else SEQ + head * P
                            for kt in range(2):
                                pt = pt2[:, g % 2, h, kt, :]
                                last = mm(dst, v2[:, kt, c:c + P], pt, start=kt == 0, stop=kt == 1)
                    last.then_inc(pv_done, 1)

                scores(0)
                for n in range(len(jobs) + 2):
                    if n + 1 < len(jobs):
                        scores(n + 1)
                    if n >= 2:
                        values(n - 2)
                    if 1 <= n <= len(jobs):
                        turn(n - 1)

            all_tiles_read("merge")
            chunks_read(6)
            pe.wait_ge(kr_copied, 16)
            pe.wait_ge(ks_copied, 32)
            attend(1)

            pe.wait_ge(score_read, N_SWA + N_MLA)
            _, ta, td = TILES["merge"]

            def merge_free(i, k):
                if k == 0:
                    pe.wait_ge(t_act, i * 2 + (ta - 1))
                elif k == 1:
                    pe.wait_ge(t_act, i * 2 + ta)
                elif k == 2:
                    pe.wait_ge(t_dve, i * 2 + (td - 1))
                    pe.wait_ge(om_lo_ready, 8)
                else:
                    pe.wait_ge(t_dve, i * 2 + td)
            operands = [(xt_hi, xt_lo), (xt_hi, xt_lo), (om_hi, om_lo), (os_hi, os_lo)]
            t_stage("merge", lambda k: operands[k], merge_free)
            pe.wait_ge(o_act, N_SWA + N_MLA)
            pe.wait_ge(mg_lo_ready, 16)
            n_stage("wout", 4, mg_hi, mg_lo)

            def ffn(up, down, per_chunk, per_tile):
                all_tiles_read(up)
                if per_tile == 2:
                    def free(i, k):
                        if k >= 4 or not isinstance(i, int):
                            pe.wait_ge(t_dve, i * 4 + (TILES[up][2] + k - 3))
                else:
                    def free(i, k):
                        if k >= 4 or not isinstance(i, int):
                            pe.wait_ge(hid_product, i * 4 + (HID0[up] + k - 3))
                t_stage(up, xt, free)
                pe.wait_ge(hid_lo_ready, HID0[up] + STAGES[up][0] // per_tile)
                n_stage(down, per_chunk, hid_hi, hid_lo)

            gains(True, True, "upA", CHUNKS["dnA"])
            pre_norm(y)
            xt_ready()
            ffn("upA", "dnA", H1A // 4, 2)
            ffn("upB", "dnB", H1B // 4, 2)
            gains(True, True, "qk2", CHUNKS["v2"])
            pre_norm(y)
            xt_ready()

            pe.wait_ge(normed, 2 * counts["norm"])
            for k in range(10):
                ch, g = k // 2, k % 2
                if g == 0:
                    chunks_read(CHUNKS["v2"] + ch - 1)
                for j in range(2):
                    s = half_at("v2", 0, k, j)
                    for c in range(4):
                        kt = 8 * g + 4 * j + c
                        for tb in range(TB):
                            dst = ps[:, 4 + 2 * ((CHUNKS["v2"] + ch) % 2) + tb, 0:SEQ]
                            last = three(dst, (xt_hi, xt_lo), (w_hi, w_lo),
                                         (slice(None), kt, slice(tb * P, (tb + 1) * P)),
                                         (slice(None), s, slice(c * SEQ, (c + 1) * SEQ)), kt == 0, kt == KT - 1)
                    last.then_inc(weights_used, 1)

            def head_sums(n):
                pe.wait_ge(hn_scaled, 2 * n + 2)
                if n == 0:
                    chunks_read(CHUNKS["v2"] + 5)
                if n >= 4:
                    pe.wait_ge(hn_done, n - 3)
                bank = ps[:, 4 + n % 4, :]
                mm(bank[:, 0:SEQ], ones, hn_sq[:, n % 2, :], start=True, stop=True)
                mm(bank[:, SEQ:2 * SEQ], swap, hn_x[:, n % 2, :], start=True, stop=True).then_inc(hn_summed, 1)

            t0 = TILES["qk2"][0]
            all_tiles_read("qk2")
            for k in range(26):
                if k >= 4:
                    n = k - 4
                    _, ta, td = TILES["qk2"]
                    if n < 10 or n % 2 == 0:
                        pe.wait_ge(t_act, ta + (n + 1 if n < 10 else n // 2 + 6))
                    else:
                        pe.wait_ge(t_dve, td + (n - 9) // 2)
                for j in range(2):
                    s = half_at("qk2", 0, k, j)
                    wh = w_hi[:, s, :].rearrange("p (c n) -> p c n", n=P)
                    wl = w_lo[:, s, :].rearrange("p (c n) -> p c n", n=P)
                    for c in range(8):
                        kt = 8 * j + c
                        last = three(ps[:, (t0 + k) % 4, 0:SEQ], (wh, wl), (xt_hi, xt_lo), (slice(None), c),
                                     (slice(None), kt), kt == 0, kt == KT - 1)
                    last.then_inc(weights_used, 1)
                if 1 <= k <= 10:
                    head_sums(k - 1)

            all_tiles_read("up2a")
            pe.wait_ge(hn_done, 10)
            attend(2)
            jobs = N_SWA + N_MLA + N_A2 + N_B2
            pe.wait_ge(o_act, jobs)
            pe.wait_ge(o_dve, N_A2 + N_B2)
            n_stage("wo2", 4, xt_hi, xt_lo)
            gains(True, True, "up2a", CHUNKS["dn2a"])
            pre_norm(y)
            xt_ready()
            ffn("up2a", "dn2a", H2A // 4, 1)
            ffn("up2b", "dn2b", H2A // 4, 1)
            gains(True, True, "end", CHUNKS["proj"])
            pre_norm(y)
            pe.wait_ge(normed, 2 * counts["norm"])

            pe.wait_ge(pe_lo_ready, 1)
            narrow("proj", pe_hi, pe_lo, 0)
            xt_ready()
            n_stage("gate", 4, xt_hi, xt_lo)
            pe.wait_ge(xt_hi_ready, 8 * counts["norm"])
            gains(True, False, "end", CHUNKS["gate"] + 4)

        @block.scalar
        def _(act):
            activation = nc.scalar.activation

            def split_hi(h, i=0, step=0):
                if h >= 2 * UNITS:
                    return
                slot, u = h % SLOTS, h // 2
                act.wait_ge(raw_loaded[u % RAW], i * (step * 16 // (2 * RAW)) + 16 * (u // RAW + 1))
                if h >= SLOTS or not isinstance(i, int):
                    act.wait_ge(weights_used, i * step + (h - SLOTS + 1))
                activation(w_hi[:, slot, :], raw[:, u % RAW, (h % 2) * HALF:(h % 2 + 1) * HALF], ACT.Copy
                           ).then_inc(hi_ready, 1)

            def ahead(name, i, k):
                h = 2 * (UNIT0[name] + k) + LEAD
                step = 2 * STAGES[name][1]
                split_hi(h, i, step)
                split_hi(h + 1, i, step)

            def used(name, i, k, j=1):
                act.wait_ge(weights_used, i * (2 * STAGES[name][1]) + (2 * (UNIT0[name] + k) + j + 1))

            counts = {"norm": 0, "post": 0, "job": 0}

            def pre_norm(source, junk):
                e = counts["norm"]
                for tb in range(TB):
                    if e == 0:
                        act.wait_ge(x_in, 16)
                    else:
                        act.wait_ge(added, 2 * (counts["post"] - 1) + tb + 1)
                    activation(junk[:, tb, :], source[:, tb, :], ACT.Square, accum_out=ss[:, tb:tb + 1]
                               ).then_inc(squared, 1)

            def turned_hi():
                e = counts["norm"]
                counts["norm"] += 1
                for g in range(8):
                    tb, q = g // 4, g % 4
                    act.wait_ge(turned, 8 * e + g + 1)
                    activation(xt_hi[:, 4 * q:4 * q + 4, tb * P:(tb + 1) * P],
                               ps[:, q, :].rearrange("p (c t) -> p c t", t=P), ACT.Copy).then_inc(xt_hi_ready, 1)

            def chunk_squares(name, per_chunk, junk):
                c0 = CHUNKS[name]
                bound = STAGES[name][1] // per_chunk

                def body(i, k):
                    ahead(name, i, k)
                    if k % per_chunk == per_chunk - 1:
                        ch = k // per_chunk
                        act.wait_ge(c_dve, i * bound + (c0 + ch + 1))
                        for tb in range(TB):
                            ins = activation(junk[:, tb, :], y[:, tb, bass.ds(i * (bound * COLS) + ch * COLS, COLS)],
                                             ACT.Square, accum_out=ss_part[:, bass.ds(i * bound + (tb * 4 + ch), 1)])
                        ins.then_inc(c_act, 1)
                stage_loop(nc.scalar, name, body)

            for h in range(LEAD):
                split_hi(h)
            pre_norm(x0, xn0)
            turned_hi()

            for k in range(8):
                ahead("cq", 0, k)
                if k == 3 or k == 7:
                    act.wait_ge(c_dve, k // 4 + 1)
                    cols = slice(0, COLS) if k == 3 else slice(COLS, COLS + SEQ)
                    q = 0 if k == 3 else 2
                    for tb in range(TB):
                        ins = activation(c_junk[:, tb, cols], c1[:, tb, cols], ACT.Square,
                                         accum_out=ss_c[:, q + tb:q + tb + 1])
                    ins.then_inc(c_act, 1)
            act.wait_ge(memset_done, 3)
            for k in range(3):
                ahead("k1", 0, k)
                if k >= 1:
                    used("k1", 0, k)
                    activation(ks[0:64, 2 * k - 2, :], ps[0:64, k, 0:SEQ], ACT.Copy)
                    activation(ks[64:128, 2 * k - 1, :], ps[64:128, k, 0:SEQ], ACT.Copy).then_inc(t_act, 1)

            def q_s(i, k):
                ahead("qs", i, k)
                used("qs", i, k)
                if k % 2 == 0:
                    dst = qs[:, bass.ds(i * 4 + k, 1), :, :].rearrange("p o a t -> p (o a) t")
                    activation(dst, halves(ps[:, (TILES["qs"][0] + k) % 4, 0:SEQ])[:, :, ::-1], ACT.Copy).then_inc(t_act, 1)
            stage_loop(nc.scalar, "qs", q_s)
            for kt in range(6):
                act.wait_ge(c_turned, kt // 2 + 1)
                g = par[:, G_QN + kt:G_QN + kt + 1]
                activation(ct_hi[:, kt, :], ps[:, 4 + kt // 2, (kt % 2) * SEQ:(kt % 2 + 1) * SEQ], ACT.Copy,
                           scale=g).then_inc(ct_hi_ready, 1)
            for k in range(6):
                ahead("qup", 0, k)
                for j in range(2):
                    used("qup", 0, k, j)
                    for tt in range(2):
                        tile = 4 * k + 2 * j + tt
                        if tile % 2 == 0:
                            dst = qr[:, tile, :] if tile < 8 else flat(qn[:, tile - 8, :, :])
                            activation(dst, ps[:, (TILES["qup"][0] + tile) % 4, 0:SEQ], ACT.Copy).then_inc(t_act, 1)
            for k in range(2):
                ahead("kvk", 0, k)
                for j in range(2):
                    used("kvk", 0, k, j)
                    for tt in range(4):
                        tile = 8 * k + 4 * j + tt
                        if tile % 2 == 0:
                            activation(kn[:, tile, :], ps[:, (TILES["kvk"][0] + tile) % 4, 0:SEQ], ACT.Copy
                                       ).then_inc(t_act, 1)
            for k in range(2):
                ahead("kvv", 0, k)
                for j in range(2):
                    ch = 2 * k + j
                    used("kvv", 0, k, j)
                    activation(v1[:, 0, ch * COLS:(ch + 1) * COLS], ps[:, 4 + 2 * ((CHUNKS["kvv"] + ch) % 2), :],
                               ACT.Copy).then_inc(c_act, 1)

            def attend(blockno):
                jobs = attention_jobs(blockno)
                g0 = counts["job"]
                counts["job"] += len(jobs)

                def exponentials(n):
                    kind, j = jobs[n]
                    g = g0 + n
                    r = g % 2
                    act.wait_ge(minus_max, g + 1)
                    if kind == "swa":
                        for h in range(2):
                            c = 4 * r + 2 * h
                            last = activation(es[:, c:c + 2], nm[:, c:c + 2], ACT.Exp,
                                              bias=sink[:, 2 * j + h:2 * j + h + 1])
                        last.then_inc(sink_exp, 1)
                    for h in range(2):
                        for blk in range(TB):
                            bias = nm[:, 4 * r + 2 * h + blk:4 * r + 2 * h + blk + 1]
                            total = rs[:, 4 * r + 2 * h + blk:4 * r + 2 * h + blk + 1]
                            if blockno == 1:
                                dst = pr1[:, g % 3, h, 0:SEQ] if blk else pr1[:, g % 3, h, SEQ:BAND]
                            else:
                                dst = pr2[:, g % 3, h, blk, :]
                            if kind == "a2":
                                src, scale = ps[:, 2 * r + h, blk * SEQ:(blk + 1) * SEQ], HEAD_SCALE
                                if h == 0 and blk == 0:
                                    act.wait_ge(p_turned, g - 2)
                            else:
                                src, scale = dst, 1.0
                            last = activation(dst, src, ACT.Exp, bias=bias, scale=scale, accum_out=total)
                    last.then_inc(exp_done, 1)

                def turned_out(n):
                    g = g0 + n
                    act.wait_ge(p_turned, g + 1)
                    if g >= 2:
                        act.wait_ge(pv_done, g - 1)
                    if blockno == 1:
                        activation(pt1[:, g % 2, :, :], ps[:, 4:6, 0:BAND], ACT.Copy).then_inc(pt_act, 1)
                    else:
                        activation(pt2[:, g % 2, 0, :, :].rearrange("p a b -> p (a b)"), ps[:, 4, :], ACT.Copy
                                   ).then_inc(pt_act, 1)

                def outputs(n):
                    kind, j = jobs[n]
                    g = g0 + n
                    act.wait_ge(pv_done, g + 1)
                    src = ps[:, 6 + g % 2, :]
                    if kind == "swa":
                        activation(qs[:, j, :, ::-1], halves(src[:, 0:SEQ]), ACT.Copy).then_inc(o_act, 1)
                    elif kind == "mla":
                        activation(qn[:, 2 * j:2 * j + 2, :, :].rearrange("p h a t -> p (h a t)"), src, ACT.Copy
                                   ).then_inc(o_act, 1)
                    elif kind == "a2":
                        activation(flat(xt_hi[:, 2 * j:2 * j + 2, :]), src, ACT.Copy).then_inc(o_act, 1)
                    else:
                        dst = xt_hi[:, 8 + 2 * j:10 + 2 * j, :].rearrange("p h (a t) -> p (h a) t", t=P)[:, :, ::-1]
                        activation(dst, src.rearrange("p (a t) -> p a t", t=P), ACT.Copy).then_inc(o_act, 1)

                for n in range(len(jobs) + 2):
                    if n >= 2:
                        turned_out(n - 2)
                    if n < len(jobs):
                        exponentials(n)
                    if n >= 2:
                        outputs(n - 2)

            attend(1)
            act.wait_ge(o_act, N_SWA + N_MLA)
            act.wait_ge(pv_done, N_SWA + N_MLA)
            for q in range(4):
                for src, dst in ((qn, om_hi), (qs, os_hi)):
                    activation(flat(dst[:, 4 * q:4 * q + 4, :]),
                               src[:, 4 * q:4 * q + 4, :, :].rearrange("p a b c -> p (a b c)"), ACT.Copy
                               ).then_inc(om_hi_ready, 1)

            def merge(i, k):
                ahead("merge", i, k)
                if k < 2:
                    used("merge", i, k)
                    activation(sg[:, k, :], ps[:, (TILES["merge"][0] + k) % 4, 0:SEQ], ACT.Sigmoid).then_inc(t_act, 1)
                if k == 3:
                    act.wait_ge(merged, i + 1)
                    activation(mg_hi[:, bass.ds(i, 1), :].rearrange("p a t -> p (a t)"), mg_f[:, :], ACT.Copy
                               ).then_inc(mg_hi_ready, 1)
            stage_loop(nc.scalar, "merge", merge)
            chunk_squares("wout", 4, squares_hid)
            counts["post"] += 1
            pre_norm(res, y)
            turned_hi()

            def plain(name):
                stage_loop(nc.scalar, name, lambda i, k: ahead(name, i, k))

            def conv_ffn(name):
                def body(i, k):
                    ahead(name, i, k)
                    if k % 2:
                        n = i * 2 + (HID0[name] + k // 2 + 1)
                        act.wait_ge(conved, n)
                        activation(act_tmp[:, :], conv[:, :], ACT.Gelu_apprx_tanh).then_inc(activated, 1)
                        act.wait_ge(hid_product, n)
                        activation(hid_hi[:, bass.ds(i * 2 + k // 2, 1), :].rearrange("p a t -> p (a t)"),
                                   hid_f[:, :], ACT.Copy).then_inc(hid_hi_ready, 1)
                act.wait_ge(weights_used, 2 * UNIT0[name])
                stage_loop(nc.scalar, name, body)

            def relu_ffn(name):
                def body(i, k):
                    ahead(name, i, k)
                    used(name, i, k)
                    n = HID0[name] + k
                    act.wait_ge(hid_product, i * 4 + n)
                    act.wait_ge(hid_hi_ready, i * 4 + n)
                    activation(act_tmp[:, :], ps[:, (TILES[name][0] + k) % 4, 0:SEQ], ACT.Relu).then_inc(t_act, 1)
                    act.wait_ge(t_act, i * 4 + (TILES[name][1] + k + 1))
                    activation(hid_hi[:, bass.ds(i * 4 + k, 1), :].rearrange("p a t -> p (a t)"),
                               act_tmp[:, :], ACT.Square).then_inc(hid_hi_ready, 1)
                act.wait_ge(weights_used, 2 * UNIT0[name])
                stage_loop(nc.scalar, name, body)

            def down(name, per_chunk):
                def body(i, k):
                    ahead(name, i, k)
                    if k % per_chunk == per_chunk - 1:
                        used(name, i, k)
                        act.wait_ge(c_dve, i * (STAGES[name][1] // per_chunk) + (CHUNKS[name] + k // per_chunk + 1))
                        act.sem_inc(c_act, 1)
                stage_loop(nc.scalar, name, body)

            conv_ffn("upA")
            down("dnA", H1A // 4)
            conv_ffn("upB")
            chunk_squares("dnB", H1B // 4, squares_xt)
            counts["post"] += 1
            pre_norm(res, y)
            turned_hi()

            for k in range(10):
                ahead("v2", 0, k)
                if k % 2:
                    ch = k // 2
                    used("v2", 0, k)
                    activation(v2[:, 0, ch * SEQ:(ch + 1) * SEQ],
                               ps[:, 4 + 2 * ((CHUNKS["v2"] + ch) % 2), 0:SEQ], ACT.Copy).then_inc(c_act, 1)
            for k in range(26):
                ahead("qk2", 0, k)
                used("qk2", 0, k)
                src = ps[:, (TILES["qk2"][0] + k) % 4, 0:SEQ]
                if k < 10:
                    if k >= 2:
                        act.wait_ge(hn_done, k - 1)
                        act.wait_ge(hn_summed, k - 1)
                    g = par[:, G_K2:G_K2 + 1] if k < 2 else par[:, G_Q2:G_Q2 + 1]
                    activation(hn_x[:, k % 2, :], src, ACT.Copy, scale=g).then_inc(hn_scaled, 1)
                    activation(hn_sq[:, k % 2, :], src, ACT.Square).then_inc(hn_scaled, 1)
                    act.wait_ge(hn_scaled, 2 * k + 2)
                    act.sem_inc(t_act, 1)
                elif k < 18 and k % 2 == 0:
                    activation(kb2[:, k - 10, :], src, ACT.Copy).then_inc(t_act, 1)
                elif k % 2 == 0:
                    activation(qb2[:, k - 18, :, ::-1], halves(src), ACT.Copy).then_inc(t_act, 1)
                if 1 <= k <= 10:
                    n = k - 1
                    act.wait_ge(hn_summed, n + 1)
                    if n >= 1:
                        act.wait_ge(hn_done, n)
                    activation(hn_r[:, :], ps[:, 4 + n % 4, 0:SEQ], ACT.Sqrt, scale=1.0 / P, bias=eps_col
                               ).then_inc(hn_rooted, 1)
            act.wait_ge(weights_used, 2 * UNIT0["wo2"])
            attend(2)
            chunk_squares("wo2", 4, squares_hid)
            counts["post"] += 1
            pre_norm(res, y)
            turned_hi()
            relu_ffn("up2a")
            down("dn2a", H2A // 4)
            relu_ffn("up2b")
            chunk_squares("dn2b", H2A // 4, squares_xt)
            counts["post"] += 1
            act.wait_ge(pe_in, 16)
            activation(pe_hi[:, :, :], pe_t[:, :, :], ACT.Copy).then_inc(pe_hi_ready, 1)
            pre_norm(res, y)
            turned_hi()
            for k in range(2):
                ahead("proj", 0, k)
                for j in range(2):
                    ch = 2 * k + j
                    used("proj", 0, k, j)
                    activation(emb[:, 0, ch * COLS:(ch + 1) * COLS], ps[:, 4 + 2 * ((CHUNKS["proj"] + ch) % 2), :],
                               ACT.Copy).then_inc(c_act, 1)
            def gated_squares(ch):
                act.wait_ge(c_dve, CHUNKS["gate"] + ch + 1)
                if ch:
                    act.wait_ge(y_squared, ch)
                for tb in range(TB):
                    last = activation(squares_hid[:, tb, :], y[:, tb, ch * COLS:(ch + 1) * COLS], ACT.Square,
                                      accum_out=ss_part[:, tb * 4 + ch:tb * 4 + ch + 1])
                last.then_inc(y_squared, 1)

            for k in range(16):
                ahead("gate", 0, k)
                if k % 4 == 3:
                    ch = k // 4
                    if ch:
                        gated_squares(ch - 1)
                    used("gate", 0, k)
                    for tb in range(TB):
                        last = activation(sig[:, tb, :], ps[:, 4 + 2 * ((CHUNKS["gate"] + ch) % 2) + tb, :],
                                          ACT.Sigmoid)
                    last.then_inc(c_act, 1)
            gated_squares(3)

        @block.vector
        def _(dve):
            tt, ts, stt = nc.vector.tensor_tensor, nc.vector.tensor_scalar, nc.vector.scalar_tensor_tensor
            step = Steps(dve, dve_step)

            def split_lo(h, i=0, stp=0):
                if h >= 2 * UNITS:
                    return
                slot, u = h % SLOTS, h // 2
                dve.wait_ge(hi_ready, i * stp + (h + 1))
                tt(w_lo[:, slot, :], raw[:, u % RAW, (h % 2) * HALF:(h % 2 + 1) * HALF],
                   w_hi[:, slot, :].bitcast(F32), ALU.subtract).then_inc(lo_ready, 1)

            def ahead(name, i, k):
                h = 2 * (UNIT0[name] + k) + LEAD
                stp = 2 * STAGES[name][1]
                split_lo(h, i, stp)
                split_lo(h + 1, i, stp)

            def used(name, i, k, j=1):
                dve.wait_ge(weights_used, i * (2 * STAGES[name][1]) + (2 * (UNIT0[name] + k) + j + 1))

            counts = {"norm": 0, "post": 0, "job": 0, "rstd": 0}

            def mean_square(src_sum):
                dve.wait_ge(rstd_ready, counts["rstd"]) if counts["rstd"] else None
                ts(ms[:, :], src_sum, 1.0 / D, EPS, ALU.mult, ALU.add).then_inc(meaned, 1)
                counts["rstd"] += 1
                dve.wait_ge(rstd_ready, counts["rstd"])

            def post_norm():
                n = counts["post"]
                counts["post"] += 1
                step(nc.vector.tensor_reduce(ss[:, :], ss_part.rearrange("p (t c) -> p t c", c=4), AX_X, ALU.add))
                mean_square(ss[:, :])
                dve.wait_ge(g_post, n + 1)
                for tb in range(TB):
                    stt(out=y[:, tb, :], in0=y[:, tb, :], scalar=rstd[:, tb:tb + 1], in1=flat(ps[:, 0:4, :]),
                        op0=ALU.mult, op1=ALU.mult).then_inc(post_scaled, 1)
                dve.wait_ge(res_in, 16)
                for tb in range(TB):
                    dve.wait_ge(post_scaled, 2 * n + tb + 1)
                    tt(res[:, tb, :], res[:, tb, :], y[:, tb, :], ALU.add).then_inc(added, 1)

            def pre_norm(source, dst):
                e = counts["norm"]
                counts["norm"] += 1
                dve.wait_ge(squared, 2 * e + 2)
                mean_square(ss[:, :])
                dve.wait_ge(g_pre, e + 1)
                for tb in range(TB):
                    stt(out=dst[:, tb, :], in0=source[:, tb, :], scalar=rstd[:, tb:tb + 1],
                        in1=flat(ps[:, 4:8, :]), op0=ALU.mult, op1=ALU.mult).then_inc(normed, 1)
                for g in range(8):
                    tb, q = g // 4, g % 4
                    dve.wait_ge(turned, 8 * e + g + 1)
                    dve.wait_ge(xt_hi_ready, 8 * e + g + 1)
                    tt(xt_lo[:, 4 * q:4 * q + 4, tb * P:(tb + 1) * P],
                       ps[:, q, :].rearrange("p (c t) -> p c t", t=P),
                       xt_hi[:, 4 * q:4 * q + 4, tb * P:(tb + 1) * P].bitcast(F32), ALU.subtract
                       ).then_inc(xt_lo_ready, 1)

            nc.vector.memset(minus_half, -0.5).then_inc(memset_done, 1)
            nc.vector.memset(eps_col, EPS).then_inc(memset_done, 1)
            nc.vector.memset(table[BUCKETS:BUCKETS + 1, :], 1.0).then_inc(memset_done, 1)
            dve.wait_ge(row_bias_mm, 1)
            nc.vector.tensor_copy(row_bias[:, :], ps[0:SWA_HEADS, 0, 0:BAND]).then_inc(row_bias_out, 1)
            for h in range(LEAD):
                split_lo(h)
            pre_norm(x0, xn0)

            for k in range(8):
                ahead("cq", 0, k)
                if k == 3:
                    used("cq", 0, k)
                    nc.vector.tensor_copy(c1[:, :, 0:COLS], ps[:, 4:6, :]).then_inc(c_dve, 1)
                if k == 7:
                    used("cq", 0, k)
                    nc.vector.tensor_copy(vs.rearrange("p t h d -> p t (h d)"), ps[:, 6:8, SEQ:COLS])
                    nc.vector.tensor_copy(c1[:, :, COLS:COLS + SEQ], ps[:, 6:8, 0:SEQ]).then_inc(c_dve, 1)
            dve.wait_ge(c_act, 2)
            ts(ss_c[:, 0:2], ss_c[:, 0:2], 1.0 / 512, EPS, ALU.mult, ALU.add).then_inc(c_meaned, 1)
            ts(ss_c[:, 2:4], ss_c[:, 2:4], 1.0 / 256, EPS, ALU.mult, ALU.add).then_inc(c_meaned, 1)
            cos_m, sin_m = cst[:, C_COSM:C_COSM + SEQ], cst[:, C_SINM:C_SINM + SEQ]
            for k in range(3):
                ahead("k1", 0, k)
                if k == 0:
                    used("k1", 0, k)
                    tt(kr_a[0:64, :], ps[0:64, 0, 0:SEQ], cos_m[0:64, :], ALU.mult)
                    tt(kr_a[64:128, :], ps[64:128, 0, 0:SEQ], sin_m[64:128, :], ALU.mult).then_inc(t_dve, 1)
                if k == 1:
                    dve.wait_ge(c_rstd, 1)
                    dve.wait_ge(c_dve, 2)
                    for q, cols in ((0, slice(0, COLS)), (2, slice(COLS, COLS + SEQ))):
                        for tb in range(TB):
                            ts(c1[:, tb, cols], c1[:, tb, cols], rstd_c[:, q + tb:q + tb + 1], None, ALU.mult
                               ).then_inc(c_scaled, 1)

            def q_s(i, k):
                ahead("qs", i, k)
                used("qs", i, k)
                if k % 2:
                    dst = qs[:, bass.ds(i * 4 + k, 1), :, :].rearrange("p o a t -> p (o a) t")
                    nc.vector.tensor_copy(dst, halves(ps[:, (TILES["qs"][0] + k) % 4, 0:SEQ])[:, :, ::-1]).then_inc(t_dve, 1)
            stage_loop(nc.vector, "qs", q_s)
            dve.wait_ge(kr_moved, 16)
            tt(kr[0:64, :], kr_a[0:64, :], kr_b[0:64, :], ALU.add).then_inc(kr_ready, 1)
            ts(minus_sink, sink, -1.0, None, ALU.mult)
            for kt in range(6):
                dve.wait_ge(ct_hi_ready, kt // 2 * 2 + 2)
                g = par[:, G_QN + kt:G_QN + kt + 1]
                stt(out=ct_lo[:, kt, :], in0=ps[:, 4 + kt // 2, (kt % 2) * SEQ:(kt % 2 + 1) * SEQ], scalar=g,
                    in1=ct_hi[:, kt, :].bitcast(F32), op0=ALU.mult, op1=ALU.subtract).then_inc(ct_lo_ready, 1)
            for k in range(6):
                ahead("qup", 0, k)
                for j in range(2):
                    used("qup", 0, k, j)
                    for tl in range(2):
                        tile = 4 * k + 2 * j + tl
                        if tile % 2:
                            dst = qr[:, tile, :] if tile < 8 else flat(qn[:, tile - 8, :, :])
                            nc.vector.tensor_copy(dst, ps[:, (TILES["qup"][0] + tile) % 4, 0:SEQ]).then_inc(t_dve, 1)
            for k in range(2):
                ahead("kvk", 0, k)
                for j in range(2):
                    used("kvk", 0, k, j)
                    for tl in range(4):
                        tile = 8 * k + 4 * j + tl
                        if tile % 2:
                            nc.vector.tensor_copy(kn[:, tile, :], ps[:, (TILES["kvk"][0] + tile) % 4, 0:SEQ]
                                                  ).then_inc(t_dve, 1)
            dve.wait_ge(t_act, TILES["qup"][1] + 4)
            for r in range(4):
                dve.wait_ge(qr_swapped, r + 1)
                for c in range(2):
                    tile, src = 2 * r + c, ps[:, 4 + r, c * SEQ:(c + 1) * SEQ]
                    if tile:
                        dve.wait_ge(qr_ready, tile)
                    tt(rope_b[:, :], src, sin_m, ALU.mult)
                    step(tt(qr[:, tile, :], qr[:, tile, :], cos_m, ALU.mult))
                    tt(qr[:, tile, :], qr[:, tile, :], rope_b[:, :], ALU.add).then_inc(qr_ready, 1)
            for k in range(2):
                ahead("kvv", 0, k)
                for j in range(2):
                    ch = 2 * k + j
                    used("kvv", 0, k, j)
                    nc.vector.tensor_copy(v1[:, 1, ch * COLS:(ch + 1) * COLS],
                                          ps[:, 5 + 2 * ((CHUNKS["kvv"] + ch) % 2), :]).then_inc(c_dve, 1)

            def attend(blockno):
                jobs = attention_jobs(blockno)
                g0 = counts["job"]
                counts["job"] += len(jobs)

                def maxima(n):
                    kind, j = jobs[n]
                    g = g0 + n
                    r = g % 2
                    dve.wait_ge(scored, g + 1)
                    m = nm[:, 4 * r:4 * r + 4]
                    if kind == "a2":
                        mm_ = mx[:, 6 * r:6 * r + 4]
                        step(nc.vector.tensor_reduce(mm_, ps[:, 2 * r:2 * r + 2, :].rearrange("p h (b k) -> p h b k", k=SEQ),
                                                     AX_X, ALU.max))
                        ts(m, mm_, -HEAD_SCALE, None, ALU.mult).then_inc(minus_max, 1)
                        return
                    if g >= 3:
                        dve.wait_ge(p_turned, g - 2)
                    banks = ps[:, 2 * r:2 * r + 2, :]
                    if kind == "b2":
                        dve.wait_ge(bias_masked, j + 1)
                        pr = pr2[:, g % 3, :, :, :].rearrange("p h b k -> p (h b) k")
                        stt(out=pr2[:, g % 3, :, :, :].rearrange("p h b k -> p h (b k)"), in0=banks, scalar=HEAD_SCALE,
                            in1=nb_bias[:, j % 2, :, :, :].rearrange("p h b k -> p h (b k)"),
                            op0=ALU.mult, op1=ALU.add).then_inc(score_read, 1)
                        dve.wait_ge(score_read, score_reads(g))
                        mm_ = mx[:, 6 * r:6 * r + 4]
                        step(nc.vector.tensor_reduce(mm_, pr, AX_X, ALU.max))
                        ts(m, mm_, -1.0, None, ALU.mult).then_inc(minus_max, 1)
                        return
                    pr = pr1[:, g % 3, :, :]
                    if kind == "swa":
                        dve.wait_ge(bias_in[j % 2], 16 * (2 * (j // 2) + 2))
                        b = sw_bias[:, j % 2, :, :]
                        stt(out=pr[:, :, 0:SEQ], in0=banks[:, :, 0:SEQ], scalar=SWA_SCALE, in1=b,
                            op0=ALU.mult, op1=ALU.add)
                        last = stt(out=pr[:, :, SEQ:BAND], in0=banks[:, :, SEQ:BAND], scalar=SWA_SCALE,
                                   in1=b[:, :, P:SEQ], op0=ALU.mult, op1=ALU.add)
                    else:
                        causal = cst[:, C_CAUSAL:C_CAUSAL + BAND]
                        for h in range(2):
                            last = stt(out=pr[:, h, :], in0=banks[:, h, 0:BAND], scalar=MLA_SCALE, in1=causal,
                                       op0=ALU.mult, op1=ALU.add)
                    last.then_inc(score_read, 1)
                    dve.wait_ge(score_read, score_reads(g))
                    m6 = mx[:, 6 * r:6 * r + 6]
                    step(nc.vector.tensor_reduce(m6, pr.rearrange("p h (s k) -> p (h s) k", k=P), AX_X, ALU.max))
                    m6 = m6.rearrange("p (h s) -> p h s", s=3)
                    step(tt(m6[:, :, 1:2], m6[:, :, 0:1], m6[:, :, 1:2], ALU.max))
                    mv = m6[:, :, 2:0:-1]
                    mo = m.rearrange("p (h b) -> p h b", b=2)
                    if kind == "mla":
                        ts(mo, mv, -1.0, None, ALU.mult).then_inc(minus_max, 1)
                    else:
                        ms_ = minus_sink[:, 2 * j:2 * j + 2].rearrange("p (h b) -> p h b", b=1).broadcast_to([P, 2, 2])
                        stt(out=mo, in0=mv, scalar=-1.0, in1=ms_, op0=ALU.mult, op1=ALU.min).then_inc(minus_max, 1)

                def denominators(n):
                    kind, j = jobs[n]
                    g = g0 + n
                    r = g % 2
                    dve.wait_ge(exp_done, g + 1)
                    t = rs[:, 4 * r:4 * r + 4]
                    if kind == "swa":
                        dve.wait_ge(sink_exp, n + 1)
                        step(tt(t, t, es[:, 4 * r:4 * r + 4], ALU.add))
                    step(nc.vector.reciprocal(t, t))
                    for h in range(2):
                        for blk in range(TB):
                            d = t[:, 2 * h + blk:2 * h + blk + 1]
                            if blockno == 1:
                                pr = pr1[:, g % 3, h, 0:SEQ] if blk else pr1[:, g % 3, h, SEQ:BAND]
                            else:
                                pr = pr2[:, g % 3, h, blk, :]
                            last = ts(pr, pr, d, None, ALU.mult)
                    last.then_inc(p_normed, 1)

                def turned_out(n):
                    g = g0 + n
                    dve.wait_ge(p_turned, g + 1)
                    if g >= 2:
                        dve.wait_ge(pv_done, g - 1)
                    nc.vector.tensor_copy(pt2[:, g % 2, 1, :, :].rearrange("p a b -> p (a b)"), ps[:, 5, :]
                                          ).then_inc(pt_dve, 1)

                def outputs(n):
                    kind, j = jobs[n]
                    g = g0 + n
                    dve.wait_ge(pv_done, g + 1)
                    src = ps[:, 6 + g % 2, :]
                    if kind == "a2":
                        dve.wait_ge(o_act, g + 1)
                        tt(flat(xt_lo[:, 2 * j:2 * j + 2, :]), src, flat(xt_hi[:, 2 * j:2 * j + 2, :]).bitcast(F32),
                           ALU.subtract).then_inc(o_dve, 1)
                    else:
                        dve.wait_ge(o_act, g + 1)

                        def rev(t):
                            return t[:, 8 + 2 * j:10 + 2 * j, :].rearrange("p h (a t) -> p (h a) t", t=P)[:, :, ::-1]
                        tt(rev(xt_lo), src.rearrange("p (a t) -> p a t", t=P), rev(xt_hi).bitcast(F32),
                           ALU.subtract).then_inc(o_dve, 1)

                for n in range(len(jobs) + 3):
                    if n < len(jobs):
                        maxima(n)
                    if blockno == 2 and 2 <= n < len(jobs) + 2:
                        turned_out(n - 2)
                    if blockno == 2 and n >= 3:
                        outputs(n - 3)
                    if 1 <= n <= len(jobs):
                        denominators(n - 1)

            attend(1)
            for q in range(4):
                for c, (src, hi, lo) in enumerate(((qn, om_hi, om_lo), (qs, os_hi, os_lo))):
                    dve.wait_ge(om_hi_ready, 2 * q + c + 1)
                    tt(flat(lo[:, 4 * q:4 * q + 4, :]), src[:, 4 * q:4 * q + 4, :, :].rearrange("p a b c -> p (a b c)"),
                       flat(hi[:, 4 * q:4 * q + 4, :]).bitcast(F32), ALU.subtract).then_inc(om_lo_ready, 1)

            _, ta, td = TILES["merge"]

            def merge(i, k):
                ahead("merge", i, k)
                if k >= 2:
                    used("merge", i, k)
                    dve.wait_ge(t_act, i * 2 + (ta + k - 1))
                    tt(sg[:, k - 2, :], ps[:, (TILES["merge"][0] + k) % 4, 0:SEQ], sg[:, k - 2, :], ALU.mult
                       ).then_inc(t_dve, 1)
                if k == 3:
                    dve.wait_ge(t_dve, i * 2 + (td + 2))
                    tt(mg_f[:, :], sg[:, 0, :], sg[:, 1, :], ALU.add).then_inc(merged, 1)
                    dve.wait_ge(merged, i + 1)
                    dve.wait_ge(mg_hi_ready, i + 1)
                    tt(mg_lo[:, bass.ds(i, 1), :].rearrange("p a t -> p (a t)"), mg_f[:, :],
                       mg_hi[:, bass.ds(i, 1), :].rearrange("p a t -> p (a t)").bitcast(F32), ALU.subtract
                       ).then_inc(mg_lo_ready, 1)
            stage_loop(nc.vector, "merge", merge)

            def take(name, per_chunk, add=False):
                c0 = CHUNKS[name]
                chunks = STAGES[name][1] // per_chunk

                def body(i, k):
                    ahead(name, i, k)
                    if k % per_chunk == per_chunk - 1:
                        ch = k // per_chunk
                        used(name, i, k)
                        b = 4 + 2 * ((c0 + ch) % 2)
                        cols = bass.ds(i * (chunks * COLS) + ch * COLS, COLS)
                        if add:
                            tt(y[:, :, cols], ps[:, b:b + 2, :], y[:, :, cols], ALU.add).then_inc(c_dve, 1)
                        else:
                            nc.vector.tensor_copy(y[:, :, cols], ps[:, b:b + 2, :]).then_inc(c_dve, 1)
                stage_loop(nc.vector, name, body)

            take("wout", 4)
            dve.wait_ge(c_act, CHUNKS["wout"] + 4)
            dve.wait_ge(c_dve, CHUNKS["wout"] + 4)
            post_norm()
            pre_norm(res, y)

            def conv_ffn(name):
                g0 = 0 if name == "upA" else H1A

                def body(i, k):
                    ahead(name, i, k)
                    if k % 2:
                        n = i * 2 + (HID0[name] + k // 2 + 1)
                        used(name, i, k)
                        a = ps[:, (TILES[name][0] + k - 1) % 4, 0:SEQ]
                        b = ps[:, (TILES[name][0] + k) % 4, 0:SEQ]

                        def w(c):
                            return par[:, bass.ds(i * 8 + (G_CONV + 4 * (g0 + k // 2) + c), 1)]
                        step(ts(conv[:, :], a, w(2), w(3), ALU.mult, ALU.add))
                        step(stt(out=conv[:, 1:SEQ], in0=a[:, 0:SEQ - 1], scalar=w(1), in1=conv[:, 1:SEQ],
                                 op0=ALU.mult, op1=ALU.add))
                        stt(out=conv[:, 2:SEQ], in0=a[:, 0:SEQ - 2], scalar=w(0), in1=conv[:, 2:SEQ],
                            op0=ALU.mult, op1=ALU.add).then_inc(conved, 1)
                        dve.wait_ge(activated, n)
                        tt(hid_f[:, :], b, act_tmp[:, :], ALU.mult).then_inc(hid_product, 1)
                        dve.wait_ge(hid_product, n)
                        dve.wait_ge(hid_hi_ready, n)
                        at_ = bass.ds(i * 2 + k // 2, 1)
                        tt(hid_lo[:, at_, :].rearrange("p a t -> p (a t)"), hid_f[:, :],
                           hid_hi[:, at_, :].rearrange("p a t -> p (a t)").bitcast(F32), ALU.subtract
                           ).then_inc(hid_lo_ready, 1)
                        dve.sem_inc(t_dve, 2)
                if STAGES[name][0] // STAGES[name][1] > 1:
                    turns = STAGES[name][0] // STAGES[name][1]
                    with nc.vector.Fori(0, turns) as i:
                        step.loop(i, 4)
                        for k in range(4):
                            body(i, k)
                    step.end(turns)

            def relu_ffn(name):
                def body(i, k):
                    ahead(name, i, k)
                    used(name, i, k)
                    n = HID0[name] + k + 1
                    dve.wait_ge(t_act, i * 4 + (TILES[name][1] + k + 1))
                    dve.wait_ge(hid_lo_ready, i * 4 + (n - 1))
                    stt(out=hid_f[:, :], in0=ps[:, (TILES[name][0] + k) % 4, 0:SEQ], scalar=0.0, in1=act_tmp[:, :],
                        op0=ALU.max, op1=ALU.mult).then_inc(hid_product, 1)
                    dve.wait_ge(hid_product, i * 4 + n)
                    dve.wait_ge(hid_hi_ready, i * 4 + n)
                    at_ = bass.ds(i * 4 + k, 1)
                    tt(hid_lo[:, at_, :].rearrange("p a t -> p (a t)"), hid_f[:, :],
                       hid_hi[:, at_, :].rearrange("p a t -> p (a t)").bitcast(F32), ALU.subtract
                       ).then_inc(hid_lo_ready, 1)
                stage_loop(nc.vector, name, body)

            conv_ffn("upA")
            take("dnA", H1A // 4)
            conv_ffn("upB")
            dve.wait_ge(c_dve, CHUNKS["dnB"])
            take("dnB", H1B // 4, add=True)
            dve.wait_ge(c_act, CHUNKS["dnB"] + 4)
            post_norm()
            pre_norm(res, y)

            for k in range(10):
                ahead("v2", 0, k)
                if k % 2:
                    ch = k // 2
                    used("v2", 0, k)
                    nc.vector.tensor_copy(v2[:, 1, ch * SEQ:(ch + 1) * SEQ],
                                          ps[:, 5 + 2 * ((CHUNKS["v2"] + ch) % 2), 0:SEQ]).then_inc(c_dve, 1)
            cos_a, sin_a = cst[:, C_COSA:C_COSA + SEQ], cst[:, C_SINA:C_SINA + SEQ]
            for k in range(26):
                ahead("qk2", 0, k)
                used("qk2", 0, k)
                src = ps[:, (TILES["qk2"][0] + k) % 4, 0:SEQ]
                if 10 <= k < 18 and k % 2:
                    nc.vector.tensor_copy(kb2[:, k - 10, :], src).then_inc(t_dve, 1)
                elif k >= 18 and k % 2:
                    nc.vector.tensor_copy(qb2[:, k - 18, :, ::-1], halves(src)).then_inc(t_dve, 1)
                if 1 <= k <= 10:
                    n = k - 1
                    dve.wait_ge(hn_summed, n + 1)
                    dve.wait_ge(hn_scaled, 2 * n + 2)
                    if n:
                        dve.wait_ge(hn_done, n)
                    tt(hn_a[:, :], hn_x[:, n % 2, :], cos_a, ALU.mult)
                    dve.wait_ge(hn_rooted, n + 1)
                    step(tt(hn_b[:, :], ps[:, 4 + n % 4, SEQ:2 * SEQ], sin_a, ALU.mult))
                    tt(hn_a[:, :], hn_a[:, :], hn_b[:, :], ALU.add)
                    step(nc.vector.reciprocal(hn_r[:, :], hn_r[:, :]))
                    dst = ka2[:, n, :] if n < 2 else qa2[:, n - 2, :, :].rearrange("p a t -> p (a t)")
                    tt(dst, hn_a[:, :], hn_r[:, :], ALU.mult).then_inc(hn_done, 1)
            attend(2)
            take("wo2", 4)
            dve.wait_ge(c_act, CHUNKS["wo2"] + 4)
            dve.wait_ge(c_dve, CHUNKS["wo2"] + 4)
            post_norm()
            pre_norm(res, y)
            relu_ffn("up2a")
            take("dn2a", H2A // 4)
            relu_ffn("up2b")
            dve.wait_ge(c_dve, CHUNKS["dn2b"])
            take("dn2b", H2A // 4, add=True)
            dve.wait_ge(c_act, CHUNKS["dn2b"] + 4)
            dve.wait_ge(pe_hi_ready, 1)
            tt(pe_lo[:, :, :], pe_t[:, :, :], pe_hi[:, :, :].bitcast(F32), ALU.subtract).then_inc(pe_lo_ready, 1)
            post_norm()
            pre_norm(res, y)
            for k in range(2):
                ahead("proj", 0, k)
                for j in range(2):
                    ch = 2 * k + j
                    used("proj", 0, k, j)
                    nc.vector.tensor_copy(emb[:, 1, ch * COLS:(ch + 1) * COLS],
                                          ps[:, 5 + 2 * ((CHUNKS["proj"] + ch) % 2), :]).then_inc(c_dve, 1)
            dve.wait_ge(turned, 8 * counts["norm"])
            dve.wait_ge(c_act, CHUNKS["gate"])
            dve.wait_ge(c_dve, CHUNKS["gate"])
            for k in range(16):
                ahead("gate", 0, k)
                if k % 4 == 3:
                    ch = k // 4
                    dve.wait_ge(c_act, CHUNKS["gate"] + ch + 1)
                    cols = slice(ch * COLS, (ch + 1) * COLS)
                    tt(y[:, :, cols], emb[:, :, cols], sig[:, :, :], ALU.mult).then_inc(c_dve, 1)
            dve.wait_ge(y_squared, 4)
            post_norm()

        @block.gpsimd
        def _(pool):
            dma = nc.gpsimd.dma_start
            tt = nc.gpsimd.tensor_tensor
            dma(cst[:, :], consts).then_inc(consts_in, 16)
            dma(x0[:, :, :], x.rearrange("(t p) d -> p t d", p=P)).then_inc(x_in, 16)

            def load_gain(tile, row, done):
                dma(tile[0:P:32, :], gain_rows[row]).then_inc(done, 16)

            load_gain(gr_pre, 0, pre_in)
            dma(table[0:BUCKETS, :], bucket_table).then_inc(table_in, 16)
            dma(hot[:, :], bucket_hot).then_inc(table_in, 16)
            dma(par[:, :], params).then_inc(consts_in, 16)
            pool.wait_ge(row_bias_out, 1)
            dma(band_dram, row_bias[:, :]).then_inc(band_stored, 16)
            pool.wait_ge(band_stored, 16)

            counts = {"rstd": 0}

            def power():
                n = counts["rstd"]
                counts["rstd"] += 1
                pool.wait_ge(memset_done, 3)
                pool.wait_ge(meaned, n + 1)
                tt(rstd, ms, minus_half[:, 0:2], ALU.pow).then_inc(rstd_ready, 1)

            power()
            pool.wait_ge(c_meaned, 2)
            tt(rstd_c, ss_c, minus_half, ALU.pow).then_inc(c_rstd, 1)

            pool.wait_ge(t_dve, 1)
            dma(kr_b[0:64, :], kr_a[64:128, :]).then_inc(kr_moved, 16)
            pool.wait_ge(t_act, 2)
            dma(ks[64:128, 0:4:2, :], ks[0:64, 0:4:2, :]).then_inc(ks_copied, 16)
            dma(ks[0:64, 1:4:2, :], ks[64:128, 1:4:2, :]).then_inc(ks_copied, 16)
            pool.wait_ge(kr_ready, 1)
            dma(kr[64:128, :], kr[0:64, :]).then_inc(kr_copied, 16)

            pool.wait_ge(g_pre, 1)
            for j in range(N_SWA):
                if j >= 2:
                    pool.wait_ge(minus_max, j - 1)
                for h in range(2):
                    head = 2 * j + h
                    src = bass.AP(tensor=band_dram.tensor, offset=head * BAND, ap=[[1, P], [1, SEQ]])
                    dma(sw_bias[:, j % 2, h, :], src).then_inc(bias_in[j % 2], 16)
            pool.wait_ge(minus_max, N_SWA)
            load_gain(gr_post, 1, post_in)
            load_gain(gr_pre, 2, pre_in)
            pool.wait_ge(weights_used, 2 * UNIT0["wout"])
            dma(res[:, :, :], x.rearrange("(t p) d -> p t d", p=P)).then_inc(res_in, 16)

            def next_gains(post, pre):
                n = counts["post"] = counts.get("post", 0) + 1
                pool.wait_ge(g_post, n)
                load_gain(gr_post, post, post_in)
                if pre is not None:
                    pool.wait_ge(g_pre, n + 1)
                    load_gain(gr_pre, pre, pre_in)

            power()
            power()
            next_gains(3, 4)
            power()
            power()
            next_gains(5, 6)
            pool.wait_ge(weights_used, 2 * UNIT0["v2"])
            nb = cst[:, C_NB:C_NB + 64]
            for j in range(N_B2):
                if j >= 2:
                    pool.wait_ge(minus_max, N_SWA + N_MLA + N_A2 + j - 1)
                for h in range(2):
                    for blk in range(TB):
                        for r in range(2):
                            head = 2 * j + h
                            off = (head * 15 + 7 - (2 * blk + 1 - r)) * RPB_W
                            src = bass.AP(tensor=rpb.tensor, offset=off, ap=[[1, 64], [RPB_W, 4], [1, 64]])
                            dma(nb_bias[64 * r:64 * r + 64, j % 2, h, blk, :].rearrange("p (a b) -> p a b", b=64),
                                src).then_inc(bias_in[j % 2], 16)
                pool.wait_ge(bias_in[j % 2], 16 * (N_SWA + 8 * (j // 2 + 1)))
                v = nb_bias[:, j % 2, :, :, :].rearrange("p h b (a k) -> p (h b a) k", k=64)
                m = nb.rearrange("p (a k) -> p a k", a=1).broadcast_to([P, 16, 64])
                tt(v, v, m, ALU.add).then_inc(bias_masked, 1)
            power()
            power()
            next_gains(7, 8)
            pool.wait_ge(weights_used, 2 * UNIT0["proj"])
            dma(pe_t[:, :, :], p_t).then_inc(pe_in, 16)
            power()
            power()
            pool.wait_ge(g_post, 4)
            load_gain(gr_post, 9, post_in)
            power()
            for tb in range(TB):
                pool.wait_ge(added, 8 + tb + 1)
                dma(out[tb * P:(tb + 1) * P, :], res[:, tb, :]).then_inc(out_done, 16)
            pool.wait_ge(out_done, 32)


def _constants():
    c = np.zeros((P, C_END), np.float32)
    d = np.arange(P)
    c[:, C_ID:C_ID + P] = np.eye(P)
    c[d, C_SWAP + (d ^ 32)] = 1.0
    c[:, C_ONES:C_ONES + P] = 1.0
    inv = (np.float32(10000.0) ** (-np.arange(0, 64, 2, dtype=np.float32) / np.float32(64))).astype(np.float32)
    t = np.arange(SEQ)
    sign = np.where(d % 64 < 32, -1.0, 1.0).astype(np.float32)[:, None]
    ang = t.astype(np.float32)[None, :] * inv[d % 32][:, None]
    c[:, C_COSM:C_COSM + SEQ], c[:, C_SINM:C_SINM + SEQ] = np.cos(ang), np.sin(ang) * sign
    where = np.where(d[:, None] < 64, (t // 64)[None, :], (t % 64)[None, :]).astype(np.float32)
    ang = where * inv[d % 32][:, None]
    c[:, C_COSA:C_COSA + SEQ], c[:, C_SINA:C_SINA + SEQ] = np.cos(ang), np.sin(ang) * sign
    lower = np.where(d[None, :] <= d[:, None], 0.0, NEG)
    c[:, C_CAUSAL + P:C_CAUSAL + SEQ] = lower
    c[:, C_CAUSAL + SEQ:C_CAUSAL + BAND] = lower
    col = 63 - d % 64
    c0 = np.clip(col - 8, 0, 48)[:, None]
    k = np.arange(64)[None, :]
    c[:, C_NB:C_NB + 64] = np.where((k >= c0) & (k < c0 + 16), 0.0, NEG)
    return c


def _bucket_hot():
    hot = np.zeros((BUCKETS + 1, BAND), np.float32)
    for j in range(BAND):
        n = 255 - j
        if not 0 <= n < WINDOW:
            hot[BUCKETS, j] = NEG
            continue
        b = n if n < 16 else min(31, 16 + int(math.log(n / 16) / math.log(8) * 16))
        hot[b, j] = 1.0
    return hot


def _t_units(w):
    k, n = w.shape
    return w.reshape(k // P, P, n // P, P).transpose(2, 1, 0, 3).reshape(n // P, P, UNIT)


def _n_units(w):
    k, n = w.shape
    return w.reshape(k // 512, 4, P, n // COLS, COLS).transpose(3, 0, 2, 1, 4).reshape(-1, P, UNIT)


def _few_t(w, tiles):
    k, n = w.shape
    return w.reshape(k // P, P, n // (tiles * P), tiles, P).transpose(2, 1, 3, 0, 4).reshape(-1, P, UNIT)


def _few_n(w):
    return w.reshape(2, P, -1, 2, COLS).transpose(2, 1, 3, 0, 4).reshape(-1, P, UNIT)


def _values_units(w):
    return w.reshape(2, 8, P, 5, SEQ).transpose(3, 0, 2, 1, 4).reshape(-1, P, UNIT)


def _stream(a):
    w = a["w_in"][0]
    cq, ckv, kr, q_s, k_s, v_s, g = np.split(w, np.cumsum([512, 256, 64, 2048, 256, 256]), axis=1)
    kr_sw = np.concatenate([kr[:, 32:], kr[:, :32]], 1)
    g = _t_units(g)
    om, os_ = _t_units(a["w_o_mla"][0]), _t_units(a["w_o_swa"][0])
    merge = np.stack([g[:16], g[16:], om, os_], 1).reshape(64, P, UNIT)
    qu = a["mla_w_q_up"][0].reshape(512, 16, 192)
    kvu = a["mla_w_kv_up"][0].reshape(256, 16, 256)
    up = a["ffn_w_up"][0]
    pairs = np.stack([_t_units(up[:, :FF1]), _t_units(up[:, FF1:])], 1)
    down = a["ffn_w_down"][0]
    w2 = a["w_in_2"][0]
    qa, ka, va, qb, kb, vb = np.split(w2, np.cumsum([1024, 256, 256, 1024, 1024]), axis=1)
    up2, down2 = _t_units(a["w_up_2"][0]), a["w_down_2"][0]
    parts = [
        _n_units(np.concatenate([cq, ckv, v_s], 1)), _t_units(np.concatenate([kr, kr_sw, k_s], 1)),
        _t_units(q_s),
        _few_t(np.concatenate([qu[:, :, 128:].reshape(512, 1024), qu[:, :, :128].reshape(512, 2048)], 1), 4),
        _few_t(np.ascontiguousarray(kvu[:, :, :128]).reshape(256, 2048), 8),
        _few_n(np.ascontiguousarray(kvu[:, :, 128:]).reshape(256, 2048)),
        merge, _n_units(a["w_out"][0]),
        pairs[:H1A].reshape(-1, P, UNIT), _n_units(down[:H1A * P]),
        pairs[H1A:].reshape(-1, P, UNIT), _n_units(down[H1A * P:]),
        _values_units(np.concatenate([va, vb], 1)), _t_units(np.concatenate([ka, qa, kb, qb], 1)),
        _n_units(a["w_o_2"][0]),
        up2[:H2A], _n_units(down2[:H2A * P]), up2[H2A:], _n_units(down2[H2A * P:]),
        _few_n(a["w_ple_proj_2"][0]), _n_units(a["w_ple_gate_2"][0]),
    ]
    return np.concatenate(parts, 0)


def kernel(**inputs):
    import concourse.bacc as bacc
    from concourse.bass_utils import run_bass_kernel_spmd

    a = {n: np.asarray(v) for n, v in inputs.items()}
    conv = np.concatenate([a["ffn_conv_w"][0], a["ffn_conv_b"]], 0).reshape(4, 44, P).transpose(2, 1, 0).reshape(P, 176)
    params = np.concatenate([
        a["mla_q_norm"][0].reshape(4, P).T, a["mla_kv_norm"][0].reshape(2, P).T,
        a["q_norm_2"][0].reshape(1, P).T, a["k_norm_2"][0].reshape(1, P).T, conv,
        np.broadcast_to(a["swa_sinks"][0], (P, 32))], 1)
    rows = ["norm_mix_pre", "norm_mix_post", "norm_ffn_pre", "norm_ffn_post", "pre_mix_norm_2", "post_mix_norm_2",
            "pre_mlp_norm_2", "post_mlp_norm_2", "pre_ple_norm_2", "post_ple_norm_2"]
    arrays = {
        "stream": _stream(a), "x": a["x"][0], "consts": _constants(), "params": params,
        "gain_rows": np.stack([a[n][0].reshape(4, COLS) for n in rows]),
        "bucket_table": a["rel_bias_table"], "bucket_hot": _bucket_hot(),
        "rpb": np.pad(a["rel_pos_bias_2"][0], ((0, 0), (0, 0), (48, 48))).reshape(-1),
        "p_t": a["p_2"][0, 0].reshape(SEQ, 2, P).transpose(2, 1, 0),
    }
    arrays = {f"in_{n}": np.ascontiguousarray(v) for n, v in arrays.items()}
    nc = bacc.Bacc("TRN2", target_bir_lowering=False, num_devices=1)
    args = [nc.dram_tensor(n, v.shape, F32, kind="ExternalInput").ap() for n, v in arrays.items()]
    args.append(nc.dram_tensor("out_x", (SEQ, D), F32, kind="ExternalOutput").ap())
    program(nc, *args)
    r = run_bass_kernel_spmd(nc, [arrays], core_ids=[0])
    return r.results[0]["out_x"].reshape(1, SEQ, D)
```

```python
import math
from contextlib import ExitStack

import numpy as np

import concourse.bass as bass
from concourse import mybir

F32 = mybir.dt.float32
F32R = mybir.dt.float32r
ALU = mybir.AluOpType
ACT = mybir.ActivationFunctionType
AX_X = mybir.AxisListType.X

P = 128
SEQ = 256
TB = SEQ // P
D = 2048
KT = D // P
EPS = 1e-6
FF1 = 5632
FF2 = 8192
H1A, H1B = 32, FF1 // P - 32
H2A = FF2 // P // 2
MLA_HEADS = 16
SWA_HEADS = 32
WINDOW = 128
BUCKETS = 32
NEG = -1e30
COLS = 512
UNIT = 2048
HALF = UNIT // 2
RAW = 4
SLOTS = 4
LEAD = 2
MLA_SCALE = (128 + 64) ** -0.5
SWA_SCALE = 64 ** -0.5
HEAD_SCALE = 1.0 / math.sqrt(128)
BAND = 3 * P
RPB_W = 31 + 2 * 48

STAGES = {
    "cq": (8, 8), "k1": (3, 3), "qs": (16, 4), "qup": (6, 6), "kvk": (2, 2), "kvv": (2, 2),
    "merge": (64, 4), "wout": (16, 8), "upA": (2 * H1A, 4), "dnA": (H1A, 16), "upB": (2 * H1B, 4),
    "dnB": (H1B, H1B), "v2": (10, 10), "qk2": (26, 26), "wo2": (16, 8), "up2a": (H2A, 4),
    "dn2a": (H2A, 16), "up2b": (H2A, 4), "dn2b": (H2A, 16), "proj": (2, 2), "gate": (16, 16),
}
UNIT0 = {}
_u = 0
for _n, (_c, _) in STAGES.items():
    UNIT0[_n] = _u
    _u += _c
UNITS = _u
TILES = {}
_t = _a = _d = 0
for _n, _c, _ca, _cd in (("k1", 3, 2, 1), ("qs", 16, 8, 8), ("qup", 24, 12, 12), ("kvk", 16, 8, 8),
                         ("merge", 64, 32, 32), ("upA", 2 * H1A, 0, 2 * H1A), ("upB", 2 * H1B, 0, 2 * H1B),
                         ("qk2", 26, 18, 8), ("up2a", H2A, H2A, 0), ("up2b", H2A, H2A, 0)):
    TILES[_n] = (_t, _a, _d)
    _t, _a, _d = (_t + _c + 3) // 4 * 4, _a + _ca, _d + _cd
TILES["end"] = (_t, _a, _d)
CHUNKS = {}
_c = 0
for _n, _k in (("cq", 2), ("kvv", 4), ("wout", 4), ("dnA", 4), ("dnB", 4), ("v2", 5), ("wo2", 4),
               ("dn2a", 4), ("dn2b", 4), ("proj", 4), ("gate", 4)):
    CHUNKS[_n] = _c
    _c += _k
AFTER_NORM = ("cq", "upA", "up2a", "gate")
BANKS_T = (0, 1, 2, 3, 4, 5, 6, 7)
BANKS_N = ((4, 5, 6, 7, 0, 1, 2, 3), (6, 7, 4, 5, 0, 1, 2, 3))
HID0 = {"upA": 0, "upB": H1A, "up2a": H1A + H1B, "up2b": H1A + H1B + H2A}

C_ID, C_SWAP, C_ONES = 0, 128, 256
C_COSM, C_SINM, C_COSA, C_SINA = 384, 640, 896, 1152
C_CAUSAL, C_NB, C_END = 1408, 1536, 1600
G_QN, G_KVN, G_Q2, G_K2, G_CONV, G_SINK, G_PRE = 0, 4, 6, 7, 8, 8 + 44 * 4, 8 + 44 * 4 + 32
PRE_NORMS = 5
G_END = G_PRE + PRE_NORMS * KT

N_SWA, N_MLA, N_A2, N_B2 = SWA_HEADS // 2, MLA_HEADS // 2, 4, 4


def attention_jobs(block):
    if block == 1:
        return [("swa", j) for j in range(N_SWA)] + [("mla", j) for j in range(N_MLA)]
    return [("a2", j) for j in range(N_A2)] + [("b2", j) for j in range(N_B2)]


def score_reads(g):
    return g + 1 if g < N_SWA + N_MLA else g + 1 - N_A2


def stage_loop(engine, name, body):
    units, group = STAGES[name]
    turns = units // group
    if turns > 1:
        with engine.Fori(0, turns) as i:
            for k in range(group):
                body(i, k)
    else:
        for k in range(units):
            body(0, k)


class Steps:

    def __init__(self, engine, sem):
        self.engine, self.sem, self.n, self.i, self.per, self.at = engine, sem, 0, 0, 0, 0

    def loop(self, i, per):
        self.i, self.per, self.at = i, per, 0

    def end(self, turns):
        self.n += self.per * turns
        self.i = self.per = self.at = 0

    def __call__(self, ins):
        ins.then_inc(self.sem, 1)
        if self.per:
            self.at = self.at % self.per + 1
            self.engine.wait_ge(self.sem, self.i * self.per + (self.n + self.at))
        else:
            self.n += 1
            self.engine.wait_ge(self.sem, self.n)


def program(nc, stream, x, consts, params, post_gains, bucket_table, bucket_hot, rpb, p_t, out):
    with ExitStack() as ctx:
        base = (nc.sbuf_base + 63) // 64 * 64
        KB = 1024

        def at(name, kb, shape, dtype=F32):
            return nc.alloc_sbuf_tensor_at(name, shape, dtype, offset=base + int(kb * KB))

        def sem(name):
            return ctx.enter_context(nc.semaphore(name))

        raw = at("raw", 0, [P, RAW, UNIT])
        w_hi = at("w_hi", 32, [P, SLOTS, HALF], F32R)
        w_lo = at("w_lo", 48, [P, SLOTS, HALF], F32R)
        xt_hi = at("xt_hi", 64, [P, KT, SEQ], F32R)
        xt_lo = at("xt_lo", 80, [P, KT, SEQ], F32R)
        qs = at("qs", 96, [P, 16, TB, P])
        qn = at("qn", 112, [P, 16, TB, P])
        kn = at("kn", 128, [P, 16, SEQ])
        v1 = at("v1", 144, [P, TB, D])
        c1 = at("c1", 128, [P, TB, 768])
        c_junk = at("c_junk", 144, [P, TB, 768])
        kr_a = at("kr_a", 112, [P, SEQ])
        kr_b = at("kr_b", 113, [P, SEQ])
        qr = at("qr", 160, [P, 8, SEQ])
        ks = at("ks", 168, [P, 4, SEQ])
        vs = at("vs", 172, [P, TB, 4, 64])
        ct_hi = at("ct_hi", 180, [P, 6, SEQ], F32R)
        ct_lo = at("ct_lo", 186, [P, 6, SEQ], F32R)
        pr1 = at("pr1", 174, [P, 3, 2, BAND])
        pt1 = at("pt1", 183, [P, 2, 2, BAND])
        os_lo = at("os_lo", 96, [P, 16, SEQ], F32R)
        om_lo = at("om_lo", 112, [P, 16, SEQ], F32R)
        om_hi = at("om_hi", 128, [P, 16, SEQ], F32R)
        os_hi = at("os_hi", 144, [P, 16, SEQ], F32R)
        mg_hi = at("mg_hi", 160, [P, 16, SEQ], F32R)
        mg_lo = at("mg_lo", 176, [P, 16, SEQ], F32R)
        y = at("y", 96, [P, TB, D])
        res = at("res", 112, [P, TB, D])
        hid_hi = at("hid_hi", 128, [P, 32, SEQ], F32R)
        hid_lo = at("hid_lo", 160, [P, 32, SEQ], F32R)
        v2 = at("v2", 128, [P, TB, 1280])
        ka2 = at("ka2", 138, [P, 2, SEQ])
        qa2 = at("qa2", 140, [P, 8, TB, P])
        qb2 = at("qb2", 148, [P, 8, TB, P])
        kb2 = at("kb2", 156, [P, 8, SEQ])
        nb_bias = at("nb_bias", 164, [P, 2, 2, 2, SEQ])
        hn_x = at("hn_x", 172, [P, 2, SEQ])
        hn_sq = at("hn_sq", 174, [P, 2, SEQ])
        hn_r = at("hn_r", 176, [P, SEQ])
        hn_a = at("hn_a", 177, [P, SEQ])
        hn_b = at("hn_b", 178, [P, SEQ])
        pr2 = at("pr2", 96, [P, 3, 2, 2, SEQ])
        pt2 = at("pt2", 180, [P, 2, 2, 2, SEQ])
        pe_t = at("pe_t", 199.5, [P, 2, SEQ])
        pe_lo = at("pe_lo", 199.5, [P, 2, SEQ], F32R)
        pe_hi = at("pe_hi", 201.5, [P, 2, SEQ], F32R)
        emb = at("emb", 134, [P, TB, D])
        sig = at("sig", 150, [P, 2, COLS])
        cst = at("cst", 192, [P, C_END])
        par = at("par", 198.25, [P, G_END])
        squares_xt = at("squares_xt", 80, [P, TB, COLS])
        squares_hid = at("squares_hid", 154, [P, TB, COLS])
        yg_xt = at("yg_xt", 64, [P, TB, D])
        yg_hid = at("yg_hid", 128, [P, TB, D])
        yg_gate = at("yg_gate", 160, [P, TB, D])
        gain_xt = at("gain_xt", 84, [P, D])
        gain_hid = at("gain_hid", 176, [P, D])
        conv = at("conv", 203.5, [P, SEQ])
        act_tmp = at("act_tmp", 204.5, [P, SEQ])
        hid_f = at("hid_f", 205.5, [P, SEQ])
        kr = at("kr", 203.5, [P, SEQ])
        sg = at("sg", 203.5, [P, 2, SEQ])
        mg_f = at("mg_f", 205.5, [P, SEQ])
        rope_b = at("rope_b", 205.5, [P, SEQ])
        stat = at("stat", 206.5, [P, 104])
        sw_bias = at("sw_bias", 199.5, [P, 2, 2, SEQ])
        table = at("table", 174, [BUCKETS + 1, 32])
        hot = at("hot", 175, [BUCKETS + 1, BAND])
        row_bias = at("row_bias", 177, [SWA_HEADS, BAND])
        ps = ctx.enter_context(nc.psum_tensor("ps", [P, 8, COLS], F32))
        band_dram = nc.dram_tensor("band_bias", (SWA_HEADS, BAND), F32, kind="Internal").ap()

        ident = cst[:, C_ID:C_ID + P]
        swap = cst[:, C_SWAP:C_SWAP + P]
        ones = cst[:, C_ONES:C_ONES + P]
        sum_parts = stat[:, 0:10].rearrange("p (t c) -> p t c", c=5)
        row_parts = stat[:, 56:62].rearrange("p (t c) -> p t c", c=3)
        rstd = stat[:, 10:12]
        ms = stat[:, 12:14]
        ss_c = stat[:, 14:18]
        rstd_c = stat[:, 18:22]
        minus_half = stat[:, 22:26]
        eps_col = stat[:, 26:27]
        mx = stat[:, 28:40]
        nm = stat[:, 40:48]
        rs = stat[:, 48:56]
        es = stat[:, 96:104]
        minus_sink = stat[:, 64:96]
        sink = par[:, G_SINK:G_SINK + 32]

        raw_loaded = [sem(f"raw_loaded{s}") for s in range(RAW)]
        hi_ready, lo_ready, weights_used = sem("hi_ready"), sem("lo_ready"), sem("weights_used")
        t_act, t_dve, c_act, c_dve = sem("t_act"), sem("t_dve"), sem("c_act"), sem("c_dve")
        consts_in, params_in, res_in, post_in = (sem(n) for n in ("consts_in", "params_in", "res_in", "post_in"))
        x_in = [sem(f"x_in{n}") for n in range(4)]
        memset_done = sem("memset_done")
        added, squared, meaned, rstd_ready, normed = (
            sem(n) for n in ("added", "squared", "meaned", "rstd_ready", "normed"))
        turned, xt_hi_ready, xt_lo_ready = sem("turned"), sem("xt_hi_ready"), sem("xt_lo_ready")
        dve_step, act_step, pool_step = sem("dve_step"), sem("act_step"), sem("pool_step")
        c_meaned, c_rstd, c_scaled, c_turned, ct_hi_ready, ct_lo_ready = (
            sem(n) for n in ("c_meaned", "c_rstd", "c_scaled", "c_turned", "ct_hi_ready", "ct_lo_ready"))
        row_bias_mm, row_bias_out, band_stored, table_in = (
            sem(n) for n in ("row_bias_mm", "row_bias_out", "band_stored", "table_in"))
        kr_moved, kr_ready, kr_copied, ks_copied = (
            sem(n) for n in ("kr_moved", "kr_ready", "kr_copied", "ks_copied"))
        qr_swapped, qr_ready = sem("qr_swapped"), sem("qr_ready")
        bias_in, bias_masked = [sem("bias_in0"), sem("bias_in1")], sem("bias_masked")
        scored, minus_max, exp_done, denom_ready, p_normed, p_turned = (
            sem(n) for n in ("scored", "minus_max", "exp_done", "denom_ready", "p_normed", "p_turned"))
        score_read, sink_exp = sem("score_read"), sem("sink_exp")
        pt_act, pt_dve, pv_done, o_act, o_dve = (sem(n) for n in ("pt_act", "pt_dve", "pv_done", "o_act", "o_dve"))
        om_hi_ready, om_lo_ready, gate_sig, merged, mg_hi_ready, mg_lo_ready = (
            sem(n) for n in ("om_hi_ready", "om_lo_ready", "gate_sig", "merged", "mg_hi_ready", "mg_lo_ready"))
        conved, activated, hid_product, hid_hi_ready, hid_lo_ready = (
            sem(n) for n in ("conved", "activated", "hid_product", "hid_hi_ready", "hid_lo_ready"))
        hn_scaled, hn_summed, hn_rooted, hn_done = (sem(n) for n in ("hn_scaled", "hn_summed", "hn_rooted", "hn_done"))
        pe_in, pe_hi_ready, pe_lo_ready, sig_ready, e_ready = (
            sem(n) for n in ("pe_in", "pe_hi_ready", "pe_lo_ready", "sig_ready", "e_ready"))
        out_done, y_squared = sem("out_done"), sem("y_squared")

        def flat(ap):
            return ap.rearrange("p a b -> p (a b)")

        def halves(ap):
            return ap.rearrange("p (a t) -> p a t", t=P)

        block = ctx.enter_context(nc.Block())

        @block.sync
        def _(sp):
            for n in range(4):
                tb, cols = n // 2, slice((n % 2) * (D // 2), (n % 2 + 1) * (D // 2))
                sp.dma_start(res[:, tb, cols], x[tb * P:(tb + 1) * P, cols]).then_inc(x_in[n], 16)
            for u in range(RAW):
                sp.dma_start(raw[:, u, :], stream[u]).then_inc(raw_loaded[u], 16)
            turns = UNITS // RAW
            with nc.sync.Fori(1, turns) as i:
                for s in range(RAW):
                    sp.wait_ge(lo_ready, i * (2 * RAW) + (2 * (s - RAW) + 2))
                    sp.dma_start(raw[:, s, :], stream[bass.ds(i * RAW + s, 1)].rearrange("u p c -> p (u c)")
                                 ).then_inc(raw_loaded[s], 16)
            for u in range(turns * RAW, UNITS):
                sp.wait_ge(lo_ready, 2 * (u - RAW) + 2)
                sp.dma_start(raw[:, u % RAW, :], stream[u]).then_inc(raw_loaded[u % RAW], 16)
            for n in range(4):
                tb, cols = n // 2, slice((n % 2) * (D // 2), (n % 2 + 1) * (D // 2))
                sp.wait_ge(added, 4 * 4 + n + 1)
                sp.dma_start(out[tb * P:(tb + 1) * P, cols], res[:, tb, cols]).then_inc(out_done, 16)
            sp.wait_ge(out_done, 64)

        @block.tensor
        def _(pe):
            mm = pe.matmul

            def three(dst, lhs, rhs, n_lhs, n_rhs, first, last):
                mm(dst, lhs[0][n_lhs], rhs[0][n_rhs], start=first, stop=False)
                mm(dst, lhs[0][n_lhs], rhs[1][n_rhs], start=False, stop=False)
                return mm(dst, lhs[1][n_lhs], rhs[0][n_rhs], start=False, stop=last)

            def half_at(name, i, k, j):
                u = UNIT0[name] + k
                pe.wait_ge(lo_ready, i * (2 * STAGES[name][1]) + (2 * u + j + 1))
                return (2 * u + j) % SLOTS

            def tile_free(name, i, k, n=0):
                _, a, d = TILES[name]
                if k >= 4 or not isinstance(i, int):
                    if k % 2 == 0:
                        pe.wait_ge(t_act, i * (STAGES[name][1] // 2) + (a + k // 2 - 1))
                    else:
                        pe.wait_ge(t_dve, i * (STAGES[name][1] // 2) + (d + k // 2 - 1))

            def all_tiles_read(name):
                _, a, d = TILES[name]
                pe.wait_ge(t_act, a) if a else None
                pe.wait_ge(t_dve, d) if d else None

            def chunks_read(n):
                if n > 0:
                    pe.wait_ge(c_act, n)
                    pe.wait_ge(c_dve, n)

            def t_stage(name, acts, free):
                t0 = TILES[name][0]

                def body(i, k):
                    free(i, k)
                    for j in range(2):
                        s = half_at(name, i, k, j)
                        wh = w_hi[:, s, :].rearrange("p (c n) -> p c n", n=P)
                        wl = w_lo[:, s, :].rearrange("p (c n) -> p c n", n=P)
                        hi, lo = acts(k)
                        for c in range(8):
                            kt = 8 * j + c
                            if name in AFTER_NORM and k == 0 and kt % 2 == 0:
                                xt_ready(kt + 2)
                            dst = ps[:, (t0 + k) % 4, 0:SEQ]
                            last = three(dst, (wh, wl), (hi, lo), (slice(None), c), (slice(None), kt),
                                         kt == 0, kt == KT - 1)
                        last.then_inc(weights_used, 1)
                stage_loop(nc.tensor, name, body)

            def n_stage(name, per_chunk, hi, lo, ready=None):
                c0 = CHUNKS[name]
                group = STAGES[name][1]

                def body(i, k):
                    ch, g = k // per_chunk, k % per_chunk
                    if g == 0 and (ch >= 1 or not isinstance(i, int)):
                        step = group // per_chunk
                        n = c0 + ch - 1
                        pe.wait_ge(c_act, i * step + n)
                        pe.wait_ge(c_dve, i * step + n)
                    if ready:
                        ready(i, k)
                    for j in range(2):
                        s = half_at(name, i, k, j)
                        for c in range(2):
                            kt = 4 * g + 2 * j + c
                            if name in AFTER_NORM and k < 4 and kt % 2 == 0:
                                xt_ready(max(kt + 2, 4))
                            cols = (slice(None), s, slice(c * COLS, (c + 1) * COLS))
                            for tb in range(TB):
                                dst = ps[:, 4 + 2 * ((c0 + ch) % 2) + tb, :]
                                last = three(dst, (hi, lo), (w_hi, w_lo),
                                             (slice(None), kt, slice(tb * P, (tb + 1) * P)), cols,
                                             kt == 0, kt == 4 * per_chunk - 1)
                        last.then_inc(weights_used, 1)
                chunks_read(c0)
                stage_loop(nc.tensor, name, body)

            counts = {"norm": 0, "job": 0}

            def pre_norm(tiles, chunks, banks):
                e = counts["norm"]
                counts["norm"] += 1
                all_tiles_read(tiles)
                chunks_read(chunks)
                for g in range(8):
                    tb, q = g // 4, g % 4
                    pe.wait_ge(normed, 8 * e + g + 1)
                    for kt in range(4 * q, 4 * q + 4):
                        c = (kt % 2) * SEQ + tb * P
                        last = pe.transpose(ps[:, banks[kt // 2], c:c + P], y[:, tb, kt * P:(kt + 1) * P], ident)
                    last.then_inc(turned, 1)

            def xt_ready(n):
                pe.wait_ge(xt_lo_ready, KT * (counts["norm"] - 1) + n)

            pe.wait_ge(consts_in, 16)
            pre_norm("k1", 0, BANKS_N[0])
            n_stage("cq", 4, xt_hi, xt_lo)

            xt = lambda k: (xt_hi, xt_lo)
            t_stage("k1", xt, lambda i, k: None)
            all_tiles_read("qs")
            t_stage("qs", xt, lambda i, k: tile_free("qs", i, k))

            chunks_read(2)
            pe.wait_ge(table_in, 32)
            mm(ps[0:SWA_HEADS, 7, 0:BAND], table[:, :], hot[:, :], start=True, stop=True).then_inc(row_bias_mm, 1)
            for kt in range(6):
                src = c1[:, :, kt * P:(kt + 1) * P]
                if kt == 0:
                    pe.wait_ge(c_scaled, 4)
                for tb in range(TB):
                    last = pe.transpose(ps[:, 4 + kt // 2, (kt % 2) * SEQ + tb * P:(kt % 2) * SEQ + (tb + 1) * P],
                                        src[:, tb, :], ident)
                if kt % 2:
                    last.then_inc(c_turned, 1)

            all_tiles_read("qup")
            pe.wait_ge(ct_lo_ready, 4)
            for k in range(6):
                for j in range(2):
                    s = half_at("qup", 0, k, j)
                    for tt in range(2):
                        tile = 4 * k + 2 * j + tt
                        tile_free("qup", 0, tile)
                        wh = w_hi[:, s, :].rearrange("p (t c n) -> p t c n", t=2, n=P)
                        wl = w_lo[:, s, :].rearrange("p (t c n) -> p t c n", t=2, n=P)
                        for kt in range(4):
                            last = three(ps[:, (TILES["qup"][0] + tile) % 4, 0:SEQ], (wh, wl), (ct_hi, ct_lo),
                                         (slice(None), tt, kt), (slice(None), kt), kt == 0, kt == 3)
                    last.then_inc(weights_used, 1)
            pe.wait_ge(ct_lo_ready, 6)
            pe.wait_ge(row_bias_out, 1)
            pe.wait_ge(t_act, TILES["qup"][1] + 4)
            pe.wait_ge(t_dve, TILES["qup"][2] + 4)
            for r in range(4):
                last = mm(ps[:, 4 + r, :], swap, flat(qr[:, 2 * r:2 * r + 2, :]), start=True, stop=True)
                last.then_inc(qr_swapped, 1)
            all_tiles_read("kvk")
            for k in range(2):
                for j in range(2):
                    s = half_at("kvk", 0, k, j)
                    for tt in range(4):
                        tile = 8 * k + 4 * j + tt
                        tile_free("kvk", 0, tile)
                        wh = w_hi[:, s, :].rearrange("p (t c n) -> p t c n", t=4, n=P)
                        wl = w_lo[:, s, :].rearrange("p (t c n) -> p t c n", t=4, n=P)
                        for kt in range(2):
                            last = three(ps[:, (TILES["kvk"][0] + tile) % 4, 0:SEQ], (wh, wl), (ct_hi, ct_lo),
                                         (slice(None), tt, kt), (slice(None), 4 + kt), kt == 0, kt == 1)
                    last.then_inc(weights_used, 1)

            def narrow(name, hi, lo, first_kt, chunks=range(4)):
                for ch in chunks:
                    s = half_at(name, 0, ch // 2, ch % 2)
                    chunks_read(CHUNKS[name] + ch - 1)
                    for kt in range(2):
                        for tb in range(TB):
                            dst = ps[:, 4 + 2 * ((CHUNKS[name] + ch) % 2) + tb, :]
                            last = three(dst, (hi, lo), (w_hi, w_lo),
                                         (slice(None), first_kt + kt, slice(tb * P, (tb + 1) * P)),
                                         (slice(None), s, slice(kt * COLS, (kt + 1) * COLS)), kt == 0, kt == 1)
                    last.then_inc(weights_used, 1)

            pe.wait_ge(qr_ready, 8)
            narrow("kvv", ct_hi, ct_lo, 4)

            def attend(blockno):
                jobs = attention_jobs(blockno)
                g0 = counts["job"]
                counts["job"] += len(jobs)

                def scores(n):
                    kind, j = jobs[n]
                    g = g0 + n
                    if n >= 2 and jobs[n - 2][0] == "a2":
                        pe.wait_ge(exp_done, g - 1)
                    elif n >= 2:
                        pe.wait_ge(score_read, score_reads(g - 2))
                    for h in range(2):
                        bank = ps[:, 2 * (g % 2) + h, :]
                        half = slice(64 * h, 64 * h + 64)
                        if kind == "swa":
                            mm(bank[:, 0:SEQ], qs[half, j, 1, :], ks[half, j // 4, :], start=True, stop=True)
                            last = mm(bank[:, SEQ:BAND], qs[half, j, 0, :], ks[half, j // 4, 0:P],
                                      start=True, stop=True)
                        elif kind == "mla":
                            head = 2 * j + h
                            mm(bank[:, 0:SEQ], qn[:, head, 1, :], kn[:, head, :], start=True, stop=False)
                            mm(bank[:, 0:SEQ], qr[half, j, P:SEQ], kr[half, :], start=False, stop=True)
                            mm(bank[:, SEQ:BAND], qn[:, head, 0, :], kn[:, head, 0:P], start=True, stop=False)
                            last = mm(bank[:, SEQ:BAND], qr[half, j, 0:P], kr[half, 0:P], start=False, stop=True)
                        else:
                            head = 2 * j + h
                            q_t, k_t = (qa2, ka2[:, head // 4, :]) if kind == "a2" else (qb2, kb2[:, head, :])
                            for blk in range(TB):
                                last = mm(bank[:, blk * SEQ:(blk + 1) * SEQ], q_t[:, head, blk, :], k_t,
                                          start=True, stop=True)
                    last.then_inc(scored, 1)

                def turn(n):
                    g = g0 + n
                    pe.wait_ge(p_normed, g + 1)
                    if g >= 1:
                        pe.wait_ge(pt_act, g)
                    if blockno == 2 and n >= 1:
                        pe.wait_ge(pt_dve, n)
                    for h in range(2):
                        bank = ps[:, 4 + h, :]
                        if blockno == 1:
                            pr = pr1[:, g % 3, h, :]
                            pe.transpose(bank[:, 0:P], pr[:, SEQ:BAND], ident)
                            pe.transpose(bank[:, P:SEQ], pr[:, 0:P], ident)
                            last = pe.transpose(bank[:, SEQ:BAND], pr[:, P:SEQ], ident)
                        else:
                            for kt in range(2):
                                for blk in range(TB):
                                    c = (2 * kt + blk) * P
                                    last = pe.transpose(bank[:, c:c + P],
                                                        pr2[:, g % 3, h, blk, kt * P:(kt + 1) * P], ident)
                    last.then_inc(p_turned, 1)

                def values(n):
                    kind, j = jobs[n]
                    g = g0 + n
                    pe.wait_ge(pt_act, g + 1)
                    if blockno == 2:
                        pe.wait_ge(pt_dve, n + 1)
                    if g >= 2:
                        pe.wait_ge(o_act, g - 1)
                    if blockno == 2 and n >= 2:
                        pe.wait_ge(o_dve, n - 1)
                    for h in range(2):
                        dst = ps[:, 6 + g % 2, h * SEQ:(h + 1) * SEQ]
                        if blockno == 1:
                            pt = pt1[:, g % 2, h, :]
                            if kind == "swa":
                                dst = ps[64 * h:64 * h + 64, 6 + g % 2, 0:SEQ]
                                v0, v1_ = (vs[:, kt, j // 4, :] for kt in range(2))
                            else:
                                c = (2 * j + h) * P
                                v0, v1_ = (v1[:, kt, c:c + P] for kt in range(2))
                            mm(dst[:, 0:P], v0, pt[:, 0:P], start=True, stop=True)
                            mm(dst[:, P:SEQ], v0, pt[:, P:SEQ], start=True, stop=False)
                            last = mm(dst[:, P:SEQ], v1_, pt[:, SEQ:BAND], start=False, stop=True)
                        else:
                            head = 2 * j + h
                            c = (head // 4) * P if kind == "a2" else SEQ + head * P
                            for kt in range(2):
                                pt = pt2[:, g % 2, h, kt, :]
                                last = mm(dst, v2[:, kt, c:c + P], pt, start=kt == 0, stop=kt == 1)
                    last.then_inc(pv_done, 1)

                scores(0)
                for n in range(len(jobs) + 2):
                    if n + 1 < len(jobs):
                        scores(n + 1)
                    if n >= 2:
                        values(n - 2)
                    if 1 <= n <= len(jobs):
                        turn(n - 1)

            all_tiles_read("merge")
            chunks_read(6)
            pe.wait_ge(kr_copied, 16)
            pe.wait_ge(ks_copied, 32)
            attend(1)

            pe.wait_ge(score_read, N_SWA + N_MLA)
            _, ta, td = TILES["merge"]

            def merge_free(i, k):
                if k == 0:
                    pe.wait_ge(t_act, i * 2 + (ta - 1))
                elif k == 1:
                    pe.wait_ge(t_act, i * 2 + ta)
                elif k == 2:
                    pe.wait_ge(t_dve, i * 2 + (td - 1))
                    pe.wait_ge(om_lo_ready, 8)
                else:
                    pe.wait_ge(t_dve, i * 2 + td)
            operands = [(xt_hi, xt_lo), (xt_hi, xt_lo), (om_hi, om_lo), (os_hi, os_lo)]
            t_stage("merge", lambda k: operands[k], merge_free)
            pe.wait_ge(o_act, N_SWA + N_MLA)
            pe.wait_ge(mg_lo_ready, 16)
            n_stage("wout", 4, mg_hi, mg_lo)

            def ffn(up, down, per_chunk, per_tile):
                all_tiles_read(up)
                if per_tile == 2:
                    def free(i, k):
                        if k >= 4 or not isinstance(i, int):
                            pe.wait_ge(t_dve, i * 4 + (TILES[up][2] + k - 3))
                else:
                    def free(i, k):
                        if k >= 4 or not isinstance(i, int):
                            pe.wait_ge(hid_product, i * 4 + (HID0[up] + k - 3))
                t_stage(up, xt, free)
                pe.wait_ge(hid_lo_ready, HID0[up] + STAGES[up][0] // per_tile)
                n_stage(down, per_chunk, hid_hi, hid_lo)

            pre_norm("upA", CHUNKS["dnA"], BANKS_T)
            ffn("upA", "dnA", H1A // 4, 2)
            ffn("upB", "dnB", H1B // 4, 2)
            pre_norm("qk2", CHUNKS["v2"], BANKS_N[CHUNKS["v2"] % 2])

            for k in range(10):
                ch, g = k // 2, k % 2
                if g == 0:
                    chunks_read(CHUNKS["v2"] + ch - 1)
                for j in range(2):
                    s = half_at("v2", 0, k, j)
                    for c in range(4):
                        kt = 8 * g + 4 * j + c
                        if k < 2 and kt % 2 == 0:
                            xt_ready(max(kt + 2, 4))
                        for tb in range(TB):
                            dst = ps[:, 4 + 2 * ((CHUNKS["v2"] + ch) % 2) + tb, 0:SEQ]
                            last = three(dst, (xt_hi, xt_lo), (w_hi, w_lo),
                                         (slice(None), kt, slice(tb * P, (tb + 1) * P)),
                                         (slice(None), s, slice(c * SEQ, (c + 1) * SEQ)), kt == 0, kt == KT - 1)
                    last.then_inc(weights_used, 1)

            def head_sums(n):
                pe.wait_ge(hn_scaled, 2 * n + 2)
                if n == 0:
                    chunks_read(CHUNKS["v2"] + 5)
                if n >= 4:
                    pe.wait_ge(hn_done, n - 3)
                bank = ps[:, 4 + n % 4, :]
                mm(bank[:, 0:SEQ], ones, hn_sq[:, n % 2, :], start=True, stop=True)
                mm(bank[:, SEQ:2 * SEQ], swap, hn_x[:, n % 2, :], start=True, stop=True).then_inc(hn_summed, 1)

            t0 = TILES["qk2"][0]
            all_tiles_read("qk2")
            for k in range(26):
                if k >= 4:
                    n = k - 4
                    _, ta, td = TILES["qk2"]
                    if n < 10 or n % 2 == 0:
                        pe.wait_ge(t_act, ta + (n + 1 if n < 10 else n // 2 + 6))
                    else:
                        pe.wait_ge(t_dve, td + (n - 9) // 2)
                for j in range(2):
                    s = half_at("qk2", 0, k, j)
                    wh = w_hi[:, s, :].rearrange("p (c n) -> p c n", n=P)
                    wl = w_lo[:, s, :].rearrange("p (c n) -> p c n", n=P)
                    for c in range(8):
                        kt = 8 * j + c
                        last = three(ps[:, (t0 + k) % 4, 0:SEQ], (wh, wl), (xt_hi, xt_lo), (slice(None), c),
                                     (slice(None), kt), kt == 0, kt == KT - 1)
                    last.then_inc(weights_used, 1)
                if 1 <= k <= 10:
                    head_sums(k - 1)

            all_tiles_read("up2a")
            pe.wait_ge(hn_done, 10)
            attend(2)
            jobs = N_SWA + N_MLA + N_A2 + N_B2
            pe.wait_ge(o_act, jobs)
            pe.wait_ge(o_dve, N_A2 + N_B2)
            pe.wait_ge(score_read, score_reads(jobs - 1))
            pe.wait_ge(exp_done, jobs)
            n_stage("wo2", 4, xt_hi, xt_lo)
            pre_norm("up2a", CHUNKS["dn2a"], BANKS_T)
            ffn("up2a", "dn2a", H2A // 4, 1)
            ffn("up2b", "dn2b", H2A // 4, 1)

            pe.wait_ge(pe_lo_ready, 1)
            narrow("proj", pe_hi, pe_lo, 0, (0, 1))
            pre_norm("end", CHUNKS["proj"] + 2, BANKS_N[CHUNKS["proj"] % 2])
            xt_ready(8)
            narrow("proj", pe_hi, pe_lo, 0, (2, 3))
            n_stage("gate", 4, xt_hi, xt_lo)

        @block.scalar
        def _(act):
            activation = nc.scalar.activation

            def split_hi(h, i=0, step=0):
                if h >= 2 * UNITS:
                    return
                slot, u = h % SLOTS, h // 2
                act.wait_ge(raw_loaded[u % RAW], i * (step * 16 // (2 * RAW)) + 16 * (u // RAW + 1))
                if h >= SLOTS or not isinstance(i, int):
                    act.wait_ge(weights_used, i * step + (h - SLOTS + 1))
                activation(w_hi[:, slot, :], raw[:, u % RAW, (h % 2) * HALF:(h % 2 + 1) * HALF], ACT.Copy
                           ).then_inc(hi_ready, 1)

            def ahead(name, i, k):
                h = 2 * (UNIT0[name] + k) + LEAD
                step = 2 * STAGES[name][1]
                split_hi(h, i, step)
                split_hi(h + 1, i, step)

            def used(name, i, k, j=1):
                act.wait_ge(weights_used, i * (2 * STAGES[name][1]) + (2 * (UNIT0[name] + k) + j + 1))

            counts = {"norm": 0, "post": 0, "job": 0}

            def row_squares():
                for n in range(4):
                    tb, half = n // 2, n % 2
                    if counts["post"] == 0:
                        act.wait_ge(x_in[n], 16)
                    else:
                        act.wait_ge(added, 4 * (counts["post"] - 1) + n + 1)
                    cols = slice(half * (D // 2), (half + 1) * (D // 2))
                    activation(y[:, tb, cols], res[:, tb, cols], ACT.Square, scale=D ** -0.5,
                               accum_out=row_parts[:, tb, half:half + 1]).then_inc(squared, 1)

            def turned_hi(banks):
                e = counts["norm"]
                counts["norm"] += 1
                act.wait_ge(params_in, 16)
                for kt in range(KT):
                    act.wait_ge(turned, 8 * e + 4 + kt // 4 + 1)
                    c = G_PRE + e * KT + kt
                    activation(xt_hi[:, kt, :], ps[:, banks[kt // 2], (kt % 2) * SEQ:(kt % 2 + 1) * SEQ], ACT.Copy,
                               scale=par[:, c:c + 1]).then_inc(xt_hi_ready, 1)

            def chunk_squares(name, per_chunk, junk):
                c0 = CHUNKS[name]
                bound = STAGES[name][1] // per_chunk

                def body(i, k):
                    ahead(name, i, k)
                    if k % per_chunk == per_chunk - 1:
                        ch = k // per_chunk
                        act.wait_ge(c_dve, i * bound + (c0 + ch + 1))
                        for tb in range(TB):
                            ins = activation(junk[:, tb, :], y[:, tb, bass.ds(i * (bound * COLS) + ch * COLS, COLS)],
                                             ACT.Square, scale=D ** -0.5,
                                             accum_out=stat[:, bass.ds(i * bound + (tb * 5 + ch), 1)])
                        ins.then_inc(c_act, 1)
                stage_loop(nc.scalar, name, body)

            row_squares()
            turned_hi(BANKS_N[0])
            for h in range(LEAD):
                split_hi(h)

            for k in range(8):
                ahead("cq", 0, k)
                if k == 3 or k == 7:
                    act.wait_ge(c_dve, k // 4 + 1)
                    cols = slice(0, COLS) if k == 3 else slice(COLS, COLS + SEQ)
                    q = 0 if k == 3 else 2
                    for tb in range(TB):
                        ins = activation(c_junk[:, tb, cols], c1[:, tb, cols], ACT.Square,
                                         accum_out=ss_c[:, q + tb:q + tb + 1])
                    ins.then_inc(c_act, 1)
            act.wait_ge(memset_done, 5)
            for k in range(3):
                ahead("k1", 0, k)
                if k >= 1:
                    used("k1", 0, k)
                    activation(ks[0:64, 2 * k - 2, :], ps[0:64, k, 0:SEQ], ACT.Copy)
                    activation(ks[64:128, 2 * k - 1, :], ps[64:128, k, 0:SEQ], ACT.Copy).then_inc(t_act, 1)

            def q_s(i, k):
                ahead("qs", i, k)
                used("qs", i, k)
                if k % 2 == 0:
                    dst = qs[:, bass.ds(i * 4 + k, 1), :, :].rearrange("p o a t -> p (o a) t")
                    activation(dst, halves(ps[:, (TILES["qs"][0] + k) % 4, 0:SEQ])[:, :, ::-1], ACT.Copy).then_inc(t_act, 1)
            stage_loop(nc.scalar, "qs", q_s)
            for kt in range(6):
                act.wait_ge(c_turned, kt // 2 + 1)
                g = par[:, G_QN + kt:G_QN + kt + 1]
                activation(ct_hi[:, kt, :], ps[:, 4 + kt // 2, (kt % 2) * SEQ:(kt % 2 + 1) * SEQ], ACT.Copy,
                           scale=g).then_inc(ct_hi_ready, 1)
            for k in range(6):
                ahead("qup", 0, k)
                for j in range(2):
                    used("qup", 0, k, j)
                    for tt in range(2):
                        tile = 4 * k + 2 * j + tt
                        if tile % 2 == 0:
                            dst = qr[:, tile, :] if tile < 8 else flat(qn[:, tile - 8, :, :])
                            activation(dst, ps[:, (TILES["qup"][0] + tile) % 4, 0:SEQ], ACT.Copy).then_inc(t_act, 1)
            for k in range(2):
                ahead("kvk", 0, k)
                for j in range(2):
                    used("kvk", 0, k, j)
                    for tt in range(4):
                        tile = 8 * k + 4 * j + tt
                        if tile % 2 == 0:
                            activation(kn[:, tile, :], ps[:, (TILES["kvk"][0] + tile) % 4, 0:SEQ], ACT.Copy
                                       ).then_inc(t_act, 1)
            for k in range(2):
                ahead("kvv", 0, k)
                for j in range(2):
                    ch = 2 * k + j
                    used("kvv", 0, k, j)
                    activation(v1[:, 0, ch * COLS:(ch + 1) * COLS], ps[:, 4 + 2 * ((CHUNKS["kvv"] + ch) % 2), :],
                               ACT.Copy).then_inc(c_act, 1)

            def attend(blockno):
                jobs = attention_jobs(blockno)
                g0 = counts["job"]
                counts["job"] += len(jobs)

                def exponentials(n):
                    kind, j = jobs[n]
                    g = g0 + n
                    r = g % 2
                    act.wait_ge(minus_max, g + 1)
                    if kind == "swa":
                        for h in range(2):
                            c = 4 * r + 2 * h
                            last = activation(es[:, c:c + 2], nm[:, c:c + 2], ACT.Exp,
                                              bias=sink[:, 2 * j + h:2 * j + h + 1])
                        last.then_inc(sink_exp, 1)
                    for h in range(2):
                        for blk in range(TB):
                            bias = nm[:, 4 * r + 2 * h + blk:4 * r + 2 * h + blk + 1]
                            total = rs[:, 4 * r + 2 * h + blk:4 * r + 2 * h + blk + 1]
                            if blockno == 1:
                                dst = pr1[:, g % 3, h, 0:SEQ] if blk else pr1[:, g % 3, h, SEQ:BAND]
                            else:
                                dst = pr2[:, g % 3, h, blk, :]
                            if kind == "a2":
                                src, scale = ps[:, 2 * r + h, blk * SEQ:(blk + 1) * SEQ], HEAD_SCALE
                                if h == 0 and blk == 0:
                                    act.wait_ge(p_turned, g - 2)
                            else:
                                src, scale = dst, 1.0
                            last = activation(dst, src, ACT.Exp, bias=bias, scale=scale, accum_out=total)
                    last.then_inc(exp_done, 1)

                def turned_out(n):
                    g = g0 + n
                    act.wait_ge(p_turned, g + 1)
                    if g >= 2:
                        act.wait_ge(pv_done, g - 1)
                    if blockno == 1:
                        activation(pt1[:, g % 2, :, :], ps[:, 4:6, 0:BAND], ACT.Copy).then_inc(pt_act, 1)
                    else:
                        activation(pt2[:, g % 2, 0, :, :].rearrange("p a b -> p (a b)"), ps[:, 4, :], ACT.Copy
                                   ).then_inc(pt_act, 1)

                def outputs(n):
                    kind, j = jobs[n]
                    g = g0 + n
                    act.wait_ge(pv_done, g + 1)
                    src = ps[:, 6 + g % 2, :]
                    if kind == "swa":
                        activation(qs[:, j, :, ::-1], halves(src[:, 0:SEQ]), ACT.Copy).then_inc(o_act, 1)
                    elif kind == "mla":
                        activation(qn[:, 2 * j:2 * j + 2, :, :].rearrange("p h a t -> p (h a t)"), src, ACT.Copy
                                   ).then_inc(o_act, 1)
                    elif kind == "a2":
                        activation(flat(xt_hi[:, 2 * j:2 * j + 2, :]), src, ACT.Copy).then_inc(o_act, 1)
                    else:
                        dst = xt_hi[:, 8 + 2 * j:10 + 2 * j, :].rearrange("p h (a t) -> p (h a) t", t=P)[:, :, ::-1]
                        activation(dst, src.rearrange("p (a t) -> p a t", t=P), ACT.Copy).then_inc(o_act, 1)

                for n in range(len(jobs) + 2):
                    if n >= 2:
                        turned_out(n - 2)
                    if n < len(jobs):
                        exponentials(n)
                    if n >= 2:
                        outputs(n - 2)

            attend(1)
            act.wait_ge(o_act, N_SWA + N_MLA)
            act.wait_ge(pv_done, N_SWA + N_MLA)
            for q in range(4):
                for src, dst in ((qn, om_hi), (qs, os_hi)):
                    activation(flat(dst[:, 4 * q:4 * q + 4, :]),
                               src[:, 4 * q:4 * q + 4, :, :].rearrange("p a b c -> p (a b c)"), ACT.Copy
                               ).then_inc(om_hi_ready, 1)

            def merge(i, k):
                ahead("merge", i, k)
                if k < 2:
                    used("merge", i, k)
                    activation(sg[:, k, :], ps[:, (TILES["merge"][0] + k) % 4, 0:SEQ], ACT.Sigmoid).then_inc(t_act, 1)
                if k == 3:
                    act.wait_ge(merged, i + 1)
                    activation(mg_hi[:, bass.ds(i, 1), :].rearrange("p a t -> p (a t)"), mg_f[:, :], ACT.Copy
                               ).then_inc(mg_hi_ready, 1)
            stage_loop(nc.scalar, "merge", merge)
            chunk_squares("wout", 4, squares_hid)
            counts["post"] += 1
            row_squares()
            turned_hi(BANKS_T)

            def plain(name):
                stage_loop(nc.scalar, name, lambda i, k: ahead(name, i, k))

            def conv_ffn(name):
                def body(i, k):
                    ahead(name, i, k)
                    if k % 2:
                        n = i * 2 + (HID0[name] + k // 2 + 1)
                        act.wait_ge(conved, n)
                        activation(act_tmp[:, :], conv[:, :], ACT.Gelu_apprx_tanh).then_inc(activated, 1)
                        act.wait_ge(hid_product, n)
                        activation(hid_hi[:, bass.ds(i * 2 + k // 2, 1), :].rearrange("p a t -> p (a t)"),
                                   hid_f[:, :], ACT.Copy).then_inc(hid_hi_ready, 1)
                act.wait_ge(weights_used, 2 * UNIT0[name])
                stage_loop(nc.scalar, name, body)

            def relu_ffn(name):
                def body(i, k):
                    ahead(name, i, k)
                    used(name, i, k)
                    n = HID0[name] + k
                    act.wait_ge(hid_product, i * 4 + n)
                    act.wait_ge(hid_hi_ready, i * 4 + n)
                    activation(act_tmp[:, :], ps[:, (TILES[name][0] + k) % 4, 0:SEQ], ACT.Relu).then_inc(t_act, 1)
                    act.wait_ge(t_act, i * 4 + (TILES[name][1] + k + 1))
                    activation(hid_hi[:, bass.ds(i * 4 + k, 1), :].rearrange("p a t -> p (a t)"),
                               act_tmp[:, :], ACT.Square).then_inc(hid_hi_ready, 1)
                act.wait_ge(weights_used, 2 * UNIT0[name])
                stage_loop(nc.scalar, name, body)

            def down(name, per_chunk):
                def body(i, k):
                    ahead(name, i, k)
                    if k % per_chunk == per_chunk - 1:
                        used(name, i, k)
                        act.wait_ge(c_dve, i * (STAGES[name][1] // per_chunk) + (CHUNKS[name] + k // per_chunk + 1))
                        act.sem_inc(c_act, 1)
                stage_loop(nc.scalar, name, body)

            conv_ffn("upA")
            down("dnA", H1A // 4)
            conv_ffn("upB")
            chunk_squares("dnB", H1B // 4, squares_xt)
            counts["post"] += 1
            row_squares()
            turned_hi(BANKS_N[CHUNKS["v2"] % 2])

            for k in range(10):
                ahead("v2", 0, k)
                if k % 2:
                    ch = k // 2
                    used("v2", 0, k)
                    activation(v2[:, 0, ch * SEQ:(ch + 1) * SEQ],
                               ps[:, 4 + 2 * ((CHUNKS["v2"] + ch) % 2), 0:SEQ], ACT.Copy).then_inc(c_act, 1)
            for k in range(26):
                ahead("qk2", 0, k)
                used("qk2", 0, k)
                src = ps[:, (TILES["qk2"][0] + k) % 4, 0:SEQ]
                if k < 10:
                    if k >= 2:
                        act.wait_ge(hn_done, k - 1)
                        act.wait_ge(hn_summed, k - 1)
                    g = par[:, G_K2:G_K2 + 1] if k < 2 else par[:, G_Q2:G_Q2 + 1]
                    activation(hn_x[:, k % 2, :], src, ACT.Copy, scale=g).then_inc(hn_scaled, 1)
                    activation(hn_sq[:, k % 2, :], src, ACT.Square).then_inc(hn_scaled, 1)
                    act.wait_ge(hn_scaled, 2 * k + 2)
                    act.sem_inc(t_act, 1)
                elif k < 18 and k % 2 == 0:
                    activation(kb2[:, k - 10, :], src, ACT.Copy).then_inc(t_act, 1)
                elif k % 2 == 0:
                    activation(qb2[:, k - 18, :, ::-1], halves(src), ACT.Copy).then_inc(t_act, 1)
                if 1 <= k <= 10:
                    n = k - 1
                    act.wait_ge(hn_summed, n + 1)
                    if n >= 1:
                        act.wait_ge(hn_done, n)
                    activation(hn_r[:, :], ps[:, 4 + n % 4, 0:SEQ], ACT.Sqrt, scale=1.0 / P, bias=eps_col
                               ).then_inc(hn_rooted, 1)
            act.wait_ge(weights_used, 2 * UNIT0["wo2"])
            attend(2)
            chunk_squares("wo2", 4, squares_hid)
            counts["post"] += 1
            row_squares()
            turned_hi(BANKS_T)
            relu_ffn("up2a")
            down("dn2a", H2A // 4)
            relu_ffn("up2b")
            act.wait_ge(pe_in, 16)
            activation(pe_hi[:, :, :], pe_t[:, :, :], ACT.Copy).then_inc(pe_hi_ready, 1)
            chunk_squares("dn2b", H2A // 4, squares_xt)
            counts["post"] += 1
            for k in range(2):
                if k:
                    row_squares()
                    ahead("proj", 0, 0)
                    turned_hi(BANKS_N[CHUNKS["proj"] % 2])
                    ahead("proj", 0, 1)
                for j in range(2):
                    ch = 2 * k + j
                    used("proj", 0, k, j)
                    activation(emb[:, 0, ch * COLS:(ch + 1) * COLS], ps[:, 4 + 2 * ((CHUNKS["proj"] + ch) % 2), :],
                               ACT.Copy).then_inc(c_act, 1)
            def gated_squares(ch):
                act.wait_ge(c_dve, CHUNKS["gate"] + ch + 1)
                if ch:
                    act.wait_ge(y_squared, ch)
                for tb in range(TB):
                    last = activation(squares_hid[:, tb, :], y[:, tb, ch * COLS:(ch + 1) * COLS], ACT.Square,
                                      scale=D ** -0.5, accum_out=sum_parts[:, tb, ch:ch + 1])
                last.then_inc(y_squared, 1)

            for k in range(16):
                ahead("gate", 0, k)
                if k % 4 == 3:
                    ch = k // 4
                    if ch:
                        gated_squares(ch - 1)
                    used("gate", 0, k)
                    for tb in range(TB):
                        last = activation(sig[:, tb, :], ps[:, 4 + 2 * ((CHUNKS["gate"] + ch) % 2) + tb, :],
                                          ACT.Sigmoid)
                    last.then_inc(c_act, 1)
            gated_squares(3)

        @block.vector
        def _(dve):
            tt, ts, stt = nc.vector.tensor_tensor, nc.vector.tensor_scalar, nc.vector.scalar_tensor_tensor
            step = Steps(dve, dve_step)

            def split_lo(h, i=0, stp=0):
                if h >= 2 * UNITS:
                    return
                slot, u = h % SLOTS, h // 2
                dve.wait_ge(hi_ready, i * stp + (h + 1))
                tt(w_lo[:, slot, :], raw[:, u % RAW, (h % 2) * HALF:(h % 2 + 1) * HALF],
                   w_hi[:, slot, :].bitcast(F32), ALU.subtract).then_inc(lo_ready, 1)

            def ahead(name, i, k):
                h = 2 * (UNIT0[name] + k) + LEAD
                stp = 2 * STAGES[name][1]
                split_lo(h, i, stp)
                split_lo(h + 1, i, stp)

            def used(name, i, k, j=1):
                dve.wait_ge(weights_used, i * (2 * STAGES[name][1]) + (2 * (UNIT0[name] + k) + j + 1))

            counts = {"norm": 0, "post": 0, "job": 0, "rstd": 0}

            def mean_square(dst, parts):
                nc.vector.tensor_reduce(dst, parts, AX_X, ALU.add).then_inc(meaned, 1)
                counts["rstd"] += 1

            def post_norm(yg):
                counts["post"] += 1
                dve.wait_ge(rstd_ready, counts["rstd"])
                mean_square(ms[:, :], sum_parts)
                dve.wait_ge(rstd_ready, counts["rstd"])
                dve.wait_ge(res_in, 16)
                for tb in range(TB):
                    for half in range(2):
                        cols = slice(half * (D // 2), (half + 1) * (D // 2))
                        stt(out=res[:, tb, cols], in0=yg[:, tb, cols], scalar=rstd[:, tb:tb + 1], in1=res[:, tb, cols],
                            op0=ALU.mult, op1=ALU.add).then_inc(added, 1)

            def pre_norm():
                e = counts["norm"]
                counts["norm"] += 1

                def quarter(tb, q):
                    cols = slice(q * COLS, (q + 1) * COLS)
                    ts(y[:, tb, cols], res[:, tb, cols], rstd[:, tb:tb + 1], None, ALU.mult).then_inc(normed, 1)

                dve.wait_ge(squared, 4 * e + 2)
                mean_square(ms[:, 0:1], row_parts[:, 0:1, :])
                dve.wait_ge(rstd_ready, counts["rstd"])
                for q in range(4):
                    quarter(0, q)
                dve.wait_ge(squared, 4 * e + 4)
                mean_square(ms[:, 1:2], row_parts[:, 1:2, :])
                dve.wait_ge(rstd_ready, counts["rstd"])
                for q in range(4):
                    quarter(1, q)
                return e

            def turned_lo(banks, e):
                for kt in range(KT):
                    dve.wait_ge(xt_hi_ready, KT * e + kt // 2 * 2 + 2)
                    c = G_PRE + e * KT + kt
                    stt(out=xt_lo[:, kt, :], in0=ps[:, banks[kt // 2], (kt % 2) * SEQ:(kt % 2 + 1) * SEQ],
                        scalar=par[:, c:c + 1], in1=xt_hi[:, kt, :].bitcast(F32), op0=ALU.mult, op1=ALU.subtract
                        ).then_inc(xt_lo_ready, 1)

            nc.vector.memset(minus_half, -0.5).then_inc(memset_done, 1)
            nc.vector.memset(eps_col, EPS).then_inc(memset_done, 1)
            nc.vector.memset(table[BUCKETS:BUCKETS + 1, :], 1.0).then_inc(memset_done, 1)
            nc.vector.memset(sum_parts[:, :, 4:5], EPS).then_inc(memset_done, 1)
            nc.vector.memset(row_parts[:, :, 2:3], EPS).then_inc(memset_done, 1)
            dve.wait_ge(memset_done, 5)
            dve.wait_ge(params_in, 16)
            turned_lo(BANKS_N[0], pre_norm())
            for h in range(LEAD):
                split_lo(h)

            for k in range(8):
                ahead("cq", 0, k)
                if k == 3:
                    used("cq", 0, k)
                    nc.vector.tensor_copy(c1[:, :, 0:COLS], ps[:, 4:6, :]).then_inc(c_dve, 1)
                if k == 7:
                    used("cq", 0, k)
                    nc.vector.tensor_copy(vs.rearrange("p t h d -> p t (h d)"), ps[:, 6:8, SEQ:COLS])
                    nc.vector.tensor_copy(c1[:, :, COLS:COLS + SEQ], ps[:, 6:8, 0:SEQ]).then_inc(c_dve, 1)
            dve.wait_ge(c_act, 2)
            ts(ss_c[:, 0:2], ss_c[:, 0:2], 1.0 / 512, EPS, ALU.mult, ALU.add).then_inc(c_meaned, 1)
            ts(ss_c[:, 2:4], ss_c[:, 2:4], 1.0 / 256, EPS, ALU.mult, ALU.add).then_inc(c_meaned, 1)
            cos_m, sin_m = cst[:, C_COSM:C_COSM + SEQ], cst[:, C_SINM:C_SINM + SEQ]
            for k in range(3):
                ahead("k1", 0, k)
                if k == 0:
                    used("k1", 0, k)
                    tt(kr_a[0:64, :], ps[0:64, 0, 0:SEQ], cos_m[0:64, :], ALU.mult)
                    tt(kr_a[64:128, :], ps[64:128, 0, 0:SEQ], sin_m[64:128, :], ALU.mult).then_inc(t_dve, 1)
                if k == 1:
                    dve.wait_ge(c_rstd, 1)
                    dve.wait_ge(c_dve, 2)
                    for q, cols in ((0, slice(0, COLS)), (2, slice(COLS, COLS + SEQ))):
                        for tb in range(TB):
                            ts(c1[:, tb, cols], c1[:, tb, cols], rstd_c[:, q + tb:q + tb + 1], None, ALU.mult
                               ).then_inc(c_scaled, 1)

            def q_s(i, k):
                ahead("qs", i, k)
                used("qs", i, k)
                if k % 2:
                    dst = qs[:, bass.ds(i * 4 + k, 1), :, :].rearrange("p o a t -> p (o a) t")
                    nc.vector.tensor_copy(dst, halves(ps[:, (TILES["qs"][0] + k) % 4, 0:SEQ])[:, :, ::-1]).then_inc(t_dve, 1)
            stage_loop(nc.vector, "qs", q_s)
            dve.wait_ge(row_bias_mm, 1)
            nc.vector.tensor_copy(row_bias[:, :], ps[0:SWA_HEADS, 7, 0:BAND]).then_inc(row_bias_out, 1)
            dve.wait_ge(kr_moved, 16)
            tt(kr[0:64, :], kr_a[0:64, :], kr_b[0:64, :], ALU.add).then_inc(kr_ready, 1)
            ts(minus_sink, sink, -1.0, None, ALU.mult)
            for kt in range(6):
                dve.wait_ge(ct_hi_ready, kt // 2 * 2 + 2)
                g = par[:, G_QN + kt:G_QN + kt + 1]
                stt(out=ct_lo[:, kt, :], in0=ps[:, 4 + kt // 2, (kt % 2) * SEQ:(kt % 2 + 1) * SEQ], scalar=g,
                    in1=ct_hi[:, kt, :].bitcast(F32), op0=ALU.mult, op1=ALU.subtract).then_inc(ct_lo_ready, 1)
            for k in range(6):
                ahead("qup", 0, k)
                for j in range(2):
                    used("qup", 0, k, j)
                    for tl in range(2):
                        tile = 4 * k + 2 * j + tl
                        if tile % 2:
                            dst = qr[:, tile, :] if tile < 8 else flat(qn[:, tile - 8, :, :])
                            nc.vector.tensor_copy(dst, ps[:, (TILES["qup"][0] + tile) % 4, 0:SEQ]).then_inc(t_dve, 1)
            for k in range(2):
                ahead("kvk", 0, k)
                for j in range(2):
                    used("kvk", 0, k, j)
                    for tl in range(4):
                        tile = 8 * k + 4 * j + tl
                        if tile % 2:
                            nc.vector.tensor_copy(kn[:, tile, :], ps[:, (TILES["kvk"][0] + tile) % 4, 0:SEQ]
                                                  ).then_inc(t_dve, 1)
            dve.wait_ge(t_act, TILES["qup"][1] + 4)
            for r in range(4):
                dve.wait_ge(qr_swapped, r + 1)
                for c in range(2):
                    tile, src = 2 * r + c, ps[:, 4 + r, c * SEQ:(c + 1) * SEQ]
                    if tile:
                        dve.wait_ge(qr_ready, tile)
                    tt(rope_b[:, :], src, sin_m, ALU.mult)
                    step(tt(qr[:, tile, :], qr[:, tile, :], cos_m, ALU.mult))
                    tt(qr[:, tile, :], qr[:, tile, :], rope_b[:, :], ALU.add).then_inc(qr_ready, 1)
            for k in range(2):
                ahead("kvv", 0, k)
                for j in range(2):
                    ch = 2 * k + j
                    used("kvv", 0, k, j)
                    nc.vector.tensor_copy(v1[:, 1, ch * COLS:(ch + 1) * COLS],
                                          ps[:, 5 + 2 * ((CHUNKS["kvv"] + ch) % 2), :]).then_inc(c_dve, 1)

            def attend(blockno):
                jobs = attention_jobs(blockno)
                g0 = counts["job"]
                counts["job"] += len(jobs)

                def maxima(n):
                    kind, j = jobs[n]
                    g = g0 + n
                    r = g % 2
                    dve.wait_ge(scored, g + 1)
                    m = nm[:, 4 * r:4 * r + 4]
                    if kind == "a2":
                        mm_ = mx[:, 6 * r:6 * r + 4]
                        step(nc.vector.tensor_reduce(mm_, ps[:, 2 * r:2 * r + 2, :].rearrange("p h (b k) -> p h b k", k=SEQ),
                                                     AX_X, ALU.max))
                        ts(m, mm_, -HEAD_SCALE, None, ALU.mult).then_inc(minus_max, 1)
                        return
                    if g >= 3:
                        dve.wait_ge(p_turned, g - 2)
                    banks = ps[:, 2 * r:2 * r + 2, :]
                    if kind == "b2":
                        dve.wait_ge(bias_masked, j + 1)
                        pr = pr2[:, g % 3, :, :, :].rearrange("p h b k -> p (h b) k")
                        stt(out=pr2[:, g % 3, :, :, :].rearrange("p h b k -> p h (b k)"), in0=banks, scalar=HEAD_SCALE,
                            in1=nb_bias[:, j % 2, :, :, :].rearrange("p h b k -> p h (b k)"),
                            op0=ALU.mult, op1=ALU.add).then_inc(score_read, 1)
                        dve.wait_ge(score_read, score_reads(g))
                        mm_ = mx[:, 6 * r:6 * r + 4]
                        step(nc.vector.tensor_reduce(mm_, pr, AX_X, ALU.max))
                        ts(m, mm_, -1.0, None, ALU.mult).then_inc(minus_max, 1)
                        return
                    pr = pr1[:, g % 3, :, :]
                    if kind == "swa":
                        dve.wait_ge(bias_in[j % 2], 16 * (2 * (j // 2) + 2))
                        b = sw_bias[:, j % 2, :, :]
                        stt(out=pr[:, :, 0:SEQ], in0=banks[:, :, 0:SEQ], scalar=SWA_SCALE, in1=b,
                            op0=ALU.mult, op1=ALU.add)
                        last = stt(out=pr[:, :, SEQ:BAND], in0=banks[:, :, SEQ:BAND], scalar=SWA_SCALE,
                                   in1=b[:, :, P:SEQ], op0=ALU.mult, op1=ALU.add)
                    else:
                        ts(pr[:, :, 0:P], banks[:, :, 0:P], MLA_SCALE, None, ALU.mult)
                        causal = cst[:, C_CAUSAL:C_CAUSAL + P].rearrange("p (a k) -> p a k", a=1).broadcast_to([P, 2, P])
                        for h in range(2):
                            last = stt(out=pr[:, h, P:BAND].rearrange("p (s k) -> p s k", k=P),
                                       in0=banks[:, h, P:BAND].rearrange("p (s k) -> p s k", k=P),
                                       scalar=MLA_SCALE, in1=causal, op0=ALU.mult, op1=ALU.add)
                    last.then_inc(score_read, 1)
                    dve.wait_ge(score_read, score_reads(g))
                    m6 = mx[:, 6 * r:6 * r + 6]
                    step(nc.vector.tensor_reduce(m6, pr.rearrange("p h (s k) -> p (h s) k", k=P), AX_X, ALU.max))
                    m6 = m6.rearrange("p (h s) -> p h s", s=3)
                    step(tt(m6[:, :, 1:2], m6[:, :, 0:1], m6[:, :, 1:2], ALU.max))
                    mv = m6[:, :, 2:0:-1]
                    mo = m.rearrange("p (h b) -> p h b", b=2)
                    if kind == "mla":
                        ts(mo, mv, -1.0, None, ALU.mult).then_inc(minus_max, 1)
                    else:
                        ms_ = minus_sink[:, 2 * j:2 * j + 2].rearrange("p (h b) -> p h b", b=1).broadcast_to([P, 2, 2])
                        stt(out=mo, in0=mv, scalar=-1.0, in1=ms_, op0=ALU.mult, op1=ALU.min).then_inc(minus_max, 1)

                def denominators(n):
                    kind, j = jobs[n]
                    g = g0 + n
                    r = g % 2
                    dve.wait_ge(exp_done, g + 1)
                    t = rs[:, 4 * r:4 * r + 4]
                    if kind == "swa":
                        dve.wait_ge(sink_exp, n + 1)
                        step(tt(t, t, es[:, 4 * r:4 * r + 4], ALU.add))
                    step(nc.vector.reciprocal(t, t))
                    for h in range(2):
                        for blk in range(TB):
                            d = t[:, 2 * h + blk:2 * h + blk + 1]
                            if blockno == 1:
                                pr = pr1[:, g % 3, h, 0:SEQ] if blk else pr1[:, g % 3, h, SEQ:BAND]
                            else:
                                pr = pr2[:, g % 3, h, blk, :]
                            last = ts(pr, pr, d, None, ALU.mult)
                    last.then_inc(p_normed, 1)

                def turned_out(n):
                    g = g0 + n
                    dve.wait_ge(p_turned, g + 1)
                    if g >= 2:
                        dve.wait_ge(pv_done, g - 1)
                    nc.vector.tensor_copy(pt2[:, g % 2, 1, :, :].rearrange("p a b -> p (a b)"), ps[:, 5, :]
                                          ).then_inc(pt_dve, 1)

                def outputs(n):
                    kind, j = jobs[n]
                    g = g0 + n
                    dve.wait_ge(pv_done, g + 1)
                    src = ps[:, 6 + g % 2, :]
                    if kind == "a2":
                        dve.wait_ge(o_act, g + 1)
                        tt(flat(xt_lo[:, 2 * j:2 * j + 2, :]), src, flat(xt_hi[:, 2 * j:2 * j + 2, :]).bitcast(F32),
                           ALU.subtract).then_inc(o_dve, 1)
                    else:
                        dve.wait_ge(o_act, g + 1)

                        def rev(t):
                            return t[:, 8 + 2 * j:10 + 2 * j, :].rearrange("p h (a t) -> p (h a) t", t=P)[:, :, ::-1]
                        tt(rev(xt_lo), src.rearrange("p (a t) -> p a t", t=P), rev(xt_hi).bitcast(F32),
                           ALU.subtract).then_inc(o_dve, 1)

                for n in range(len(jobs) + 3):
                    if n < len(jobs):
                        maxima(n)
                    if blockno == 2 and 2 <= n < len(jobs) + 2:
                        turned_out(n - 2)
                    if blockno == 2 and n >= 3:
                        outputs(n - 3)
                    if 1 <= n <= len(jobs):
                        denominators(n - 1)

            attend(1)
            for q in range(4):
                for c, (src, hi, lo) in enumerate(((qn, om_hi, om_lo), (qs, os_hi, os_lo))):
                    dve.wait_ge(om_hi_ready, 2 * q + c + 1)
                    tt(flat(lo[:, 4 * q:4 * q + 4, :]), src[:, 4 * q:4 * q + 4, :, :].rearrange("p a b c -> p (a b c)"),
                       flat(hi[:, 4 * q:4 * q + 4, :]).bitcast(F32), ALU.subtract).then_inc(om_lo_ready, 1)

            _, ta, td = TILES["merge"]

            def merge(i, k):
                ahead("merge", i, k)
                if k >= 2:
                    used("merge", i, k)
                    dve.wait_ge(t_act, i * 2 + (ta + k - 1))
                    tt(sg[:, k - 2, :], ps[:, (TILES["merge"][0] + k) % 4, 0:SEQ], sg[:, k - 2, :], ALU.mult
                       ).then_inc(t_dve, 1)
                if k == 3:
                    dve.wait_ge(t_dve, i * 2 + (td + 2))
                    tt(mg_f[:, :], sg[:, 0, :], sg[:, 1, :], ALU.add).then_inc(merged, 1)
                    dve.wait_ge(merged, i + 1)
                    dve.wait_ge(mg_hi_ready, i + 1)
                    tt(mg_lo[:, bass.ds(i, 1), :].rearrange("p a t -> p (a t)"), mg_f[:, :],
                       mg_hi[:, bass.ds(i, 1), :].rearrange("p a t -> p (a t)").bitcast(F32), ALU.subtract
                       ).then_inc(mg_lo_ready, 1)
            stage_loop(nc.vector, "merge", merge)

            def take(name, per_chunk, add=False, yg=None, gain=None):
                c0 = CHUNKS[name]
                chunks = STAGES[name][1] // per_chunk
                if yg is not None:
                    dve.wait_ge(post_in, 16 * (counts["post"] + 1))

                def body(i, k):
                    ahead(name, i, k)
                    if k % per_chunk == per_chunk - 1:
                        ch = k // per_chunk
                        used(name, i, k)
                        b = 4 + 2 * ((c0 + ch) % 2)
                        cols = bass.ds(i * (chunks * COLS) + ch * COLS, COLS)
                        if add:
                            tt(y[:, :, cols], ps[:, b:b + 2, :], y[:, :, cols], ALU.add).then_inc(c_dve, 1)
                        else:
                            nc.vector.tensor_copy(y[:, :, cols], ps[:, b:b + 2, :]).then_inc(c_dve, 1)
                        if yg is not None:
                            dve.wait_ge(c_dve, i * chunks + (c0 + ch + 1))
                            g = gain[:, cols].rearrange("p (a c) -> p a c", a=1).broadcast_to([P, TB, COLS])
                            tt(yg[:, :, cols], y[:, :, cols], g, ALU.mult)
                stage_loop(nc.vector, name, body)

            take("wout", 4, yg=yg_hid, gain=gain_xt)
            dve.wait_ge(c_act, CHUNKS["wout"] + 4)
            post_norm(yg_hid)
            turned_lo(BANKS_T, pre_norm())

            def conv_ffn(name):
                g0 = 0 if name == "upA" else H1A

                def body(i, k):
                    ahead(name, i, k)
                    if k % 2:
                        n = i * 2 + (HID0[name] + k // 2 + 1)
                        used(name, i, k)
                        a = ps[:, (TILES[name][0] + k - 1) % 4, 0:SEQ]
                        b = ps[:, (TILES[name][0] + k) % 4, 0:SEQ]

                        def w(c):
                            return par[:, bass.ds(i * 8 + (G_CONV + 4 * (g0 + k // 2) + c), 1)]
                        step(ts(conv[:, :], a, w(2), w(3), ALU.mult, ALU.add))
                        step(stt(out=conv[:, 1:SEQ], in0=a[:, 0:SEQ - 1], scalar=w(1), in1=conv[:, 1:SEQ],
                                 op0=ALU.mult, op1=ALU.add))
                        stt(out=conv[:, 2:SEQ], in0=a[:, 0:SEQ - 2], scalar=w(0), in1=conv[:, 2:SEQ],
                            op0=ALU.mult, op1=ALU.add).then_inc(conved, 1)
                        dve.wait_ge(activated, n)
                        tt(hid_f[:, :], b, act_tmp[:, :], ALU.mult).then_inc(hid_product, 1)
                        dve.wait_ge(hid_product, n)
                        dve.wait_ge(hid_hi_ready, n)
                        at_ = bass.ds(i * 2 + k // 2, 1)
                        tt(hid_lo[:, at_, :].rearrange("p a t -> p (a t)"), hid_f[:, :],
                           hid_hi[:, at_, :].rearrange("p a t -> p (a t)").bitcast(F32), ALU.subtract
                           ).then_inc(hid_lo_ready, 1)
                        dve.sem_inc(t_dve, 2)
                if STAGES[name][0] // STAGES[name][1] > 1:
                    turns = STAGES[name][0] // STAGES[name][1]
                    with nc.vector.Fori(0, turns) as i:
                        step.loop(i, 4)
                        for k in range(4):
                            body(i, k)
                    step.end(turns)

            def relu_ffn(name):
                def body(i, k):
                    ahead(name, i, k)
                    used(name, i, k)
                    n = HID0[name] + k + 1
                    dve.wait_ge(t_act, i * 4 + (TILES[name][1] + k + 1))
                    dve.wait_ge(hid_lo_ready, i * 4 + (n - 1))
                    stt(out=hid_f[:, :], in0=ps[:, (TILES[name][0] + k) % 4, 0:SEQ], scalar=0.0, in1=act_tmp[:, :],
                        op0=ALU.max, op1=ALU.mult).then_inc(hid_product, 1)
                    dve.wait_ge(hid_product, i * 4 + n)
                    dve.wait_ge(hid_hi_ready, i * 4 + n)
                    at_ = bass.ds(i * 4 + k, 1)
                    tt(hid_lo[:, at_, :].rearrange("p a t -> p (a t)"), hid_f[:, :],
                       hid_hi[:, at_, :].rearrange("p a t -> p (a t)").bitcast(F32), ALU.subtract
                       ).then_inc(hid_lo_ready, 1)
                stage_loop(nc.vector, name, body)

            conv_ffn("upA")
            take("dnA", H1A // 4)
            conv_ffn("upB")
            dve.wait_ge(c_dve, CHUNKS["dnB"])
            take("dnB", H1B // 4, add=True, yg=yg_xt, gain=gain_xt)
            dve.wait_ge(c_act, CHUNKS["dnB"] + 4)
            post_norm(yg_xt)
            turned_lo(BANKS_N[CHUNKS["v2"] % 2], pre_norm())

            for k in range(10):
                ahead("v2", 0, k)
                if k % 2:
                    ch = k // 2
                    used("v2", 0, k)
                    nc.vector.tensor_copy(v2[:, 1, ch * SEQ:(ch + 1) * SEQ],
                                          ps[:, 5 + 2 * ((CHUNKS["v2"] + ch) % 2), 0:SEQ]).then_inc(c_dve, 1)
            cos_a, sin_a = cst[:, C_COSA:C_COSA + SEQ], cst[:, C_SINA:C_SINA + SEQ]
            for k in range(26):
                ahead("qk2", 0, k)
                used("qk2", 0, k)
                src = ps[:, (TILES["qk2"][0] + k) % 4, 0:SEQ]
                if 10 <= k < 18 and k % 2:
                    nc.vector.tensor_copy(kb2[:, k - 10, :], src).then_inc(t_dve, 1)
                elif k >= 18 and k % 2:
                    nc.vector.tensor_copy(qb2[:, k - 18, :, ::-1], halves(src)).then_inc(t_dve, 1)
                if 1 <= k <= 10:
                    n = k - 1
                    dve.wait_ge(hn_summed, n + 1)
                    dve.wait_ge(hn_scaled, 2 * n + 2)
                    if n:
                        dve.wait_ge(hn_done, n)
                    tt(hn_a[:, :], hn_x[:, n % 2, :], cos_a, ALU.mult)
                    dve.wait_ge(hn_rooted, n + 1)
                    step(tt(hn_b[:, :], ps[:, 4 + n % 4, SEQ:2 * SEQ], sin_a, ALU.mult))
                    tt(hn_a[:, :], hn_a[:, :], hn_b[:, :], ALU.add)
                    step(nc.vector.reciprocal(hn_r[:, :], hn_r[:, :]))
                    dst = ka2[:, n, :] if n < 2 else qa2[:, n - 2, :, :].rearrange("p a t -> p (a t)")
                    tt(dst, hn_a[:, :], hn_r[:, :], ALU.mult).then_inc(hn_done, 1)
            attend(2)
            take("wo2", 4, yg=yg_hid, gain=gain_hid)
            dve.wait_ge(c_act, CHUNKS["wo2"] + 4)
            post_norm(yg_hid)
            turned_lo(BANKS_T, pre_norm())
            relu_ffn("up2a")
            take("dn2a", H2A // 4)
            relu_ffn("up2b")
            dve.wait_ge(c_dve, CHUNKS["dn2b"])
            dve.wait_ge(pe_hi_ready, 1)
            tt(pe_lo[:, :, :], pe_t[:, :, :], pe_hi[:, :, :].bitcast(F32), ALU.subtract).then_inc(pe_lo_ready, 1)
            take("dn2b", H2A // 4, add=True, yg=yg_xt, gain=gain_xt)
            dve.wait_ge(c_act, CHUNKS["dn2b"] + 4)
            post_norm(yg_xt)
            for k in range(2):
                if k:
                    e = pre_norm()
                    ahead("proj", 0, 0)
                    turned_lo(BANKS_N[CHUNKS["proj"] % 2], e)
                    ahead("proj", 0, 1)
                for j in range(2):
                    ch = 2 * k + j
                    used("proj", 0, k, j)
                    nc.vector.tensor_copy(emb[:, 1, ch * COLS:(ch + 1) * COLS],
                                          ps[:, 5 + 2 * ((CHUNKS["proj"] + ch) % 2), :]).then_inc(c_dve, 1)
            dve.wait_ge(c_act, CHUNKS["gate"])
            dve.wait_ge(c_dve, CHUNKS["gate"])
            dve.wait_ge(post_in, 16 * 5)
            for k in range(16):
                ahead("gate", 0, k)
                if k % 4 == 3:
                    ch = k // 4
                    dve.wait_ge(c_act, CHUNKS["gate"] + ch + 1)
                    cols = slice(ch * COLS, (ch + 1) * COLS)
                    tt(y[:, :, cols], emb[:, :, cols], sig[:, :, :], ALU.mult).then_inc(c_dve, 1)
                    dve.wait_ge(c_dve, CHUNKS["gate"] + ch + 1)
                    g = gain_hid[:, cols].rearrange("p (a c) -> p a c", a=1).broadcast_to([P, TB, COLS])
                    tt(yg_gate[:, :, cols], y[:, :, cols], g, ALU.mult)
            dve.wait_ge(y_squared, 4)
            post_norm(yg_gate)

        @block.gpsimd
        def _(pool):
            dma = nc.gpsimd.dma_start
            tt = nc.gpsimd.tensor_tensor
            dma(cst[:, :], consts).then_inc(consts_in, 16)

            dma(par[:, :], params).then_inc(params_in, 16)

            def load_gains(tile, norm, stage):
                pool.wait_ge(weights_used, 2 * UNIT0[stage] + 1)
                src = bass.AP(tensor=post_gains.tensor, offset=norm * D, ap=[[0, P], [1, D]])
                dma(tile[:, :], src).then_inc(post_in, 16)

            dma(table[0:BUCKETS, :], bucket_table).then_inc(table_in, 16)
            dma(hot[:, :], bucket_hot).then_inc(table_in, 16)

            counts = {"rstd": 0}

            def power(tbs=slice(0, 2)):
                counts["rstd"] += 1
                pool.wait_ge(meaned, counts["rstd"])
                tt(rstd[:, tbs], ms[:, tbs], minus_half[:, tbs], ALU.pow).then_inc(rstd_ready, 1)

            def pre_powers():
                power(slice(0, 1))
                power(slice(1, 2))

            pool.wait_ge(memset_done, 5)
            pre_powers()
            pool.wait_ge(c_meaned, 2)
            tt(rstd_c, ss_c, minus_half, ALU.pow).then_inc(c_rstd, 1)

            pool.wait_ge(t_dve, 1)
            dma(kr_b[0:64, :], kr_a[64:128, :]).then_inc(kr_moved, 16)
            pool.wait_ge(t_act, 2)
            dma(ks[64:128, 0:4:2, :], ks[0:64, 0:4:2, :]).then_inc(ks_copied, 16)
            dma(ks[0:64, 1:4:2, :], ks[64:128, 1:4:2, :]).then_inc(ks_copied, 16)
            pool.wait_ge(kr_ready, 1)
            dma(kr[64:128, :], kr[0:64, :]).then_inc(kr_copied, 16)
            pool.wait_ge(row_bias_out, 1)
            dma(band_dram, row_bias[:, :]).then_inc(band_stored, 16)
            pool.wait_ge(band_stored, 16)

            for j in range(N_SWA):
                if j >= 2:
                    pool.wait_ge(minus_max, j - 1)
                for h in range(2):
                    head = 2 * j + h
                    src = bass.AP(tensor=band_dram.tensor, offset=head * BAND, ap=[[1, P], [1, SEQ]])
                    dma(sw_bias[:, j % 2, h, :], src).then_inc(bias_in[j % 2], 16)
            load_gains(gain_xt, 0, "wout")
            dma(res[:, :, :], x.rearrange("(t p) d -> p t d", p=P)).then_inc(res_in, 16)
            power()
            pre_powers()
            load_gains(gain_xt, 1, "dnB")
            power()
            pre_powers()
            pool.wait_ge(weights_used, 2 * UNIT0["v2"])
            nb = cst[:, C_NB:C_NB + 64]
            for j in range(N_B2):
                if j >= 2:
                    pool.wait_ge(minus_max, N_SWA + N_MLA + N_A2 + j - 1)
                for h in range(2):
                    for blk in range(TB):
                        for r in range(2):
                            head = 2 * j + h
                            off = (head * 15 + 7 - (2 * blk + 1 - r)) * RPB_W
                            src = bass.AP(tensor=rpb.tensor, offset=off, ap=[[1, 64], [RPB_W, 4], [1, 64]])
                            dma(nb_bias[64 * r:64 * r + 64, j % 2, h, blk, :].rearrange("p (a b) -> p a b", b=64),
                                src).then_inc(bias_in[j % 2], 16)
                pool.wait_ge(bias_in[j % 2], 16 * (N_SWA + 8 * (j // 2 + 1)))
                v = nb_bias[:, j % 2, :, :, :].rearrange("p h b (a k) -> p (h b a) k", k=64)
                m = nb.rearrange("p (a k) -> p a k", a=1).broadcast_to([P, 16, 64])
                tt(v, v, m, ALU.add).then_inc(bias_masked, 1)
            dma(pe_t[:, :, :], p_t).then_inc(pe_in, 16)
            load_gains(gain_hid, 2, "wo2")
            power()
            pre_powers()
            load_gains(gain_xt, 3, "dn2b")
            power()
            pre_powers()
            load_gains(gain_hid, 4, "gate")
            power()


def _constants():
    c = np.zeros((P, C_END), np.float32)
    d = np.arange(P)
    c[:, C_ID:C_ID + P] = np.eye(P)
    c[d, C_SWAP + (d ^ 32)] = 1.0
    c[:, C_ONES:C_ONES + P] = 1.0
    inv = (np.float32(10000.0) ** (-np.arange(0, 64, 2, dtype=np.float32) / np.float32(64))).astype(np.float32)
    t = np.arange(SEQ)
    sign = np.where(d % 64 < 32, -1.0, 1.0).astype(np.float32)[:, None]
    ang = t.astype(np.float32)[None, :] * inv[d % 32][:, None]
    c[:, C_COSM:C_COSM + SEQ], c[:, C_SINM:C_SINM + SEQ] = np.cos(ang), np.sin(ang) * sign
    where = np.where(d[:, None] < 64, (t // 64)[None, :], (t % 64)[None, :]).astype(np.float32)
    ang = where * inv[d % 32][:, None]
    c[:, C_COSA:C_COSA + SEQ], c[:, C_SINA:C_SINA + SEQ] = np.cos(ang), np.sin(ang) * sign
    lower = np.where(d[None, :] <= d[:, None], 0.0, NEG)
    c[:, C_CAUSAL:C_CAUSAL + P] = lower
    col = 63 - d % 64
    c0 = np.clip(col - 8, 0, 48)[:, None]
    k = np.arange(64)[None, :]
    c[:, C_NB:C_NB + 64] = np.where((k >= c0) & (k < c0 + 16), 0.0, NEG)
    return c


def _bucket_hot():
    hot = np.zeros((BUCKETS + 1, BAND), np.float32)
    for j in range(BAND):
        n = 255 - j
        if not 0 <= n < WINDOW:
            hot[BUCKETS, j] = NEG
            continue
        b = n if n < 16 else min(31, 16 + int(math.log(n / 16) / math.log(8) * 16))
        hot[b, j] = 1.0
    return hot


def _t_units(w):
    k, n = w.shape
    return w.reshape(k // P, P, n // P, P).transpose(2, 1, 0, 3).reshape(n // P, P, UNIT)


def _n_units(w):
    k, n = w.shape
    return w.reshape(k // 512, 4, P, n // COLS, COLS).transpose(3, 0, 2, 1, 4).reshape(-1, P, UNIT)


def _few_t(w, tiles):
    k, n = w.shape
    return w.reshape(k // P, P, n // (tiles * P), tiles, P).transpose(2, 1, 3, 0, 4).reshape(-1, P, UNIT)


def _few_n(w):
    return w.reshape(2, P, -1, 2, COLS).transpose(2, 1, 3, 0, 4).reshape(-1, P, UNIT)


def _values_units(w):
    return w.reshape(2, 8, P, 5, SEQ).transpose(3, 0, 2, 1, 4).reshape(-1, P, UNIT)


def _stream(a):
    w = a["w_in"][0]
    cq, ckv, kr, q_s, k_s, v_s, g = np.split(w, np.cumsum([512, 256, 64, 2048, 256, 256]), axis=1)
    kr_sw = np.concatenate([kr[:, 32:], kr[:, :32]], 1)
    g = _t_units(g)
    om, os_ = _t_units(a["w_o_mla"][0]), _t_units(a["w_o_swa"][0])
    merge = np.stack([g[:16], g[16:], om, os_], 1).reshape(64, P, UNIT)
    qu = a["mla_w_q_up"][0].reshape(512, 16, 192)
    kvu = a["mla_w_kv_up"][0].reshape(256, 16, 256)
    up = a["ffn_w_up"][0]
    pairs = np.stack([_t_units(up[:, :FF1]), _t_units(up[:, FF1:])], 1)
    down = a["ffn_w_down"][0]
    w2 = a["w_in_2"][0]
    qa, ka, va, qb, kb, vb = np.split(w2, np.cumsum([1024, 256, 256, 1024, 1024]), axis=1)
    up2, down2 = _t_units(a["w_up_2"][0]), a["w_down_2"][0]
    parts = [
        _n_units(np.concatenate([cq, ckv, v_s], 1)), _t_units(np.concatenate([kr, kr_sw, k_s], 1)),
        _t_units(q_s),
        _few_t(np.concatenate([qu[:, :, 128:].reshape(512, 1024), qu[:, :, :128].reshape(512, 2048)], 1), 4),
        _few_t(np.ascontiguousarray(kvu[:, :, :128]).reshape(256, 2048), 8),
        _few_n(np.ascontiguousarray(kvu[:, :, 128:]).reshape(256, 2048)),
        merge, _n_units(a["w_out"][0]),
        pairs[:H1A].reshape(-1, P, UNIT), _n_units(down[:H1A * P]),
        pairs[H1A:].reshape(-1, P, UNIT), _n_units(down[H1A * P:]),
        _values_units(np.concatenate([va, vb], 1)), _t_units(np.concatenate([ka, qa, kb, qb], 1)),
        _n_units(a["w_o_2"][0]),
        up2[:H2A], _n_units(down2[:H2A * P]), up2[H2A:], _n_units(down2[H2A * P:]),
        _few_n(a["w_ple_proj_2"][0]), _n_units(a["w_ple_gate_2"][0]),
    ]
    return np.concatenate(parts, 0)


def kernel(**inputs):
    import concourse.bacc as bacc
    from concourse.bass_utils import run_bass_kernel_spmd

    a = {n: np.asarray(v) for n, v in inputs.items()}
    conv = np.concatenate([a["ffn_conv_w"][0], a["ffn_conv_b"]], 0).reshape(4, 44, P).transpose(2, 1, 0).reshape(P, 176)
    params = np.concatenate([
        a["mla_q_norm"][0].reshape(4, P).T, a["mla_kv_norm"][0].reshape(2, P).T,
        a["q_norm_2"][0].reshape(1, P).T, a["k_norm_2"][0].reshape(1, P).T, conv,
        np.broadcast_to(a["swa_sinks"][0], (P, 32))]
        + [a[n][0].reshape(KT, P).T for n in ("norm_mix_pre", "norm_ffn_pre", "pre_mix_norm_2", "pre_mlp_norm_2",
                                              "pre_ple_norm_2")], 1)
    post = ["norm_mix_post", "norm_ffn_post", "post_mix_norm_2", "post_mlp_norm_2", "post_ple_norm_2"]
    arrays = {
        "stream": _stream(a), "x": a["x"][0], "consts": _constants(), "params": params,
        "post_gains": np.stack([a[n][0] for n in post]),
        "bucket_table": a["rel_bias_table"], "bucket_hot": _bucket_hot(),
        "rpb": np.pad(a["rel_pos_bias_2"][0], ((0, 0), (0, 0), (48, 48))).reshape(-1),
        "p_t": a["p_2"][0, 0].reshape(SEQ, 2, P).transpose(2, 1, 0),
    }
    arrays = {f"in_{n}": np.ascontiguousarray(v) for n, v in arrays.items()}
    nc = bacc.Bacc("TRN2", target_bir_lowering=False, num_devices=1)
    args = [nc.dram_tensor(n, v.shape, F32, kind="ExternalInput").ap() for n, v in arrays.items()]
    args.append(nc.dram_tensor("out_x", (SEQ, D), F32, kind="ExternalOutput").ap())
    program(nc, *args)
    r = run_bass_kernel_spmd(nc, [arrays], core_ids=[0])
    return r.results[0]["out_x"].reshape(1, SEQ, D)
```

```python
import math
from contextlib import ExitStack

import numpy as np

import concourse.bass as bass
from concourse import mybir

F32 = mybir.dt.float32
F32R = mybir.dt.float32r
ALU = mybir.AluOpType
ACT = mybir.ActivationFunctionType
AX_X = mybir.AxisListType.X

P = 128
SEQ = 256
TB = SEQ // P
D = 2048
KT = D // P
EPS = 1e-6
FF1 = 5632
FF2 = 8192
H1A, H1B = 32, FF1 // P - 32
H2A = FF2 // P // 2
MLA_HEADS = 16
SWA_HEADS = 32
WINDOW = 128
BUCKETS = 32
NEG = -1e30
COLS = 512
UNIT = 2048
HALF = UNIT // 2
RAW = 4
SLOTS = 4
LEAD = 4
MLA_SCALE = (128 + 64) ** -0.5
SWA_SCALE = 64 ** -0.5
HEAD_SCALE = 1.0 / math.sqrt(128)
BAND = 3 * P
RPB_W = 31 + 2 * 48

STAGES = {
    "cq": (8, 8), "k1": (3, 3), "qs": (16, 4), "qup": (6, 6), "kvk": (2, 2), "kvv": (2, 2),
    "gate0": (2, 2), "merge": (56, 8), "mergeZ": (6, 6), "wout": (16, 8),
    "upA": (2 * H1A, 4), "dnA": (H1A, 16), "upB": (2 * H1B, 4), "dnB": (H1B, H1B),
    "v2": (10, 10), "qk2": (26, 26), "wo2": (16, 16), "up2a": (H2A, 4),
    "dn2a": (H2A, 16), "up2b": (H2A, 4), "dn2b": (H2A, 16), "proj": (2, 2), "gate": (16, 16),
}
UNIT0 = {}
_u = 0
for _n, (_c, _) in STAGES.items():
    UNIT0[_n] = _u
    _u += _c
UNITS = _u
TILES = {}
_t = _a = _d = 0
for _n, _c, _ca, _cd in (("k1", 3, 2, 2), ("qs", 16, 8, 8), ("qup", 24, 12, 12), ("kvk", 16, 16, 0),
                         ("gate0", 2, 2, 0), ("merge", 56, 28, 28), ("mergeZ", 6, 2, 4),
                         ("upA", 2 * H1A, 0, 2 * H1A), ("upB", 2 * H1B, 0, 2 * H1B),
                         ("qk2", 26, 18, 8), ("up2a", H2A, H2A, 0), ("up2b", H2A, H2A, 0)):
    TILES[_n] = (_t, _a, _d)
    _t, _a, _d = (_t + _c + 3) // 4 * 4, _a + _ca, _d + _cd
TILES["end"] = (_t, _a, _d)
MERGE = {
    "gate0": [("gate", 0, 0), ("gate", 0, 1)],
    "merge": [("gate", 1, 0), ("gate", 1, 1), ("out", 0, 1), ("out", 0, 0),
              ("gate", 2, 0), ("gate", 2, 1), ("out", 1, 1), ("out", 1, 0)],
    "mergeZ": [("gate", 1, 0), ("gate", 1, 1), ("out", 0, 1), ("out", 0, 0), ("out", 1, 1), ("out", 1, 0)],
}
MERGE_TILE0 = {"gate0": 0, "merge": 0, "mergeZ": 14}
CHUNKS = {}
_c = 0
for _n, _k in (("cq", 2), ("kvv", 4), ("wout", 4), ("dnA", 4), ("dnB", 4), ("v2", 5), ("wo2", 4),
               ("dn2a", 4), ("dn2b", 4), ("proj", 4), ("gate", 4)):
    CHUNKS[_n] = _c
    _c += _k
AFTER_NORM = ("cq", "upA", "up2a", "gate")
BANKS_T = (0, 1, 2, 3, 4, 5, 6, 7)
BANKS_N = ((4, 5, 6, 7, 0, 1, 2, 3), (6, 7, 4, 5, 0, 1, 2, 3))
HID0 = {"upA": 0, "upB": H1A, "up2a": H1A + H1B, "up2b": H1A + H1B + H2A}

C_ID, C_SWAP, C_ONES = 0, 128, 256
C_COSM, C_SINM, C_COSA, C_SINA = 384, 640, 896, 1152
C_CAUSAL, C_NB, C_END = 1408, 1536, 1600
G_QN, G_KVN, G_Q2, G_K2, G_CONV, G_SINK, G_PRE = 0, 4, 6, 7, 8, 8 + 44 * 4, 8 + 44 * 4 + 32
PRE_NORMS = 5
G_END = G_PRE + PRE_NORMS * KT

N_SWA, N_MLA, N_A2, N_B2 = SWA_HEADS // 2, MLA_HEADS // 2, 4, 4


def attention_jobs(block):
    if block == 1:
        return [("swa", j) for j in range(N_SWA)] + [("mla", j) for j in range(N_MLA)]
    return [("a2", j) for j in range(N_A2)] + [("b2", j) for j in range(N_B2)]


def score_pair(block, g):
    return 2 * (g % 2) if block == 1 else 6 - 2 * (g % 2)


TURN_BANK, VALUE_BANK = {1: 4, 2: 0}, {1: 6, 2: 2}


def score_reads(g):
    return g + 1 if g < N_SWA + N_MLA else g + 1 - N_A2


def stage_loop(engine, name, body, peel=False):
    units, group = STAGES[name]
    turns = units // group
    looped = 0 if turns == 1 else turns - 1 if peel else turns
    if looped:
        with engine.Fori(0, looped) as i:
            for k in range(group):
                body(i, k)
    for i in range(looped, turns):
        for k in range(group):
            body(i, k)


def is_last(name, i, k):
    units, group = STAGES[name]
    return isinstance(i, int) and i * group + k == units - 1


class Steps:

    def __init__(self, engine, sem):
        self.engine, self.sem, self.n, self.i, self.per, self.at = engine, sem, 0, 0, 0, 0

    def loop(self, i, per):
        self.i, self.per, self.at = i, per, 0

    def end(self, turns):
        self.n += self.per * turns
        self.i = self.per = self.at = 0

    def __call__(self, ins):
        ins.then_inc(self.sem, 1)
        if self.per:
            self.at = self.at % self.per + 1
            self.engine.wait_ge(self.sem, self.i * self.per + (self.n + self.at))
        else:
            self.n += 1
            self.engine.wait_ge(self.sem, self.n)


def program(nc, stream, x, consts, params, post_gains, bucket_table, bucket_hot, rpb, p_t, out):
    with ExitStack() as ctx:
        base = (nc.sbuf_base + 63) // 64 * 64
        KB = 1024

        def at(name, kb, shape, dtype=F32):
            return nc.alloc_sbuf_tensor_at(name, shape, dtype, offset=base + int(kb * KB))

        def sem(name):
            return ctx.enter_context(nc.semaphore(name))

        raw = at("raw", 0, [P, RAW, UNIT])
        w_hi = at("w_hi", 32, [P, SLOTS, HALF], F32R)
        w_lo = at("w_lo", 48, [P, SLOTS, HALF], F32R)
        xt_hi = at("xt_hi", 64, [P, KT, SEQ], F32R)
        xt_lo = at("xt_lo", 80, [P, KT, SEQ], F32R)
        qs = at("qs", 96, [P, 16, TB, P])
        qn = at("qn", 112, [P, 16, TB, P])
        kn = at("kn", 128, [P, 16, SEQ])
        v1 = at("v1", 144, [P, TB, D])
        c1 = at("c1", 128, [P, TB, 768])
        c_junk = at("c_junk", 144, [P, TB, 768])
        kr_a = at("kr_a", 112, [P, SEQ])
        kr_b = at("kr_b", 113, [P, SEQ])
        qr = at("qr", 160, [P, 8, SEQ])
        ks = at("ks", 168, [P, 4, SEQ])
        vs = at("vs", 172, [P, TB, 4, 64])
        ct_hi = at("ct_hi", 180, [P, 6, SEQ], F32R)
        ct_lo = at("ct_lo", 186, [P, 6, SEQ], F32R)
        pr1 = at("pr1", 174, [P, 3, 2, BAND])
        pt1 = at("pt1", 183, [P, 2, 2, BAND])
        os_lo = at("os_lo", 96, [P, 16, SEQ], F32R)
        om_lo = at("om_lo", 112, [P, 16, SEQ], F32R)
        os_hi = at("os_hi", 128, [P, 16, SEQ], F32R)
        om_hi = at("om_hi", 144, [P, 16, SEQ], F32R)
        mg_hi = at("mg_hi", 160, [P, 16, SEQ], F32R)
        mg_lo = at("mg_lo", 176, [P, 16, SEQ], F32R)
        y = at("y", 96, [P, TB, D])
        res = at("res", 112, [P, TB, D])
        hid_hi = at("hid_hi", 128, [P, 32, SEQ], F32R)
        hid_lo = at("hid_lo", 160, [P, 32, SEQ], F32R)
        v2 = at("v2", 128, [P, TB, 1280])
        ka2 = at("ka2", 138, [P, 2, SEQ])
        qa2 = at("qa2", 140, [P, 8, TB, P])
        qb2 = at("qb2", 148, [P, 8, TB, P])
        kb2 = at("kb2", 156, [P, 8, SEQ])
        nb_bias = [at(f"nb_bias{j}", kb, [P, 2, 2, SEQ]) for j, kb in enumerate((164, 168, 188, 108))]
        hn_x = at("hn_x", 172, [P, 2, SEQ])
        hn_sq = at("hn_sq", 174, [P, 2, SEQ])
        hn_r = at("hn_r", 176, [P, SEQ])
        hn_a = at("hn_a", 177, [P, SEQ])
        hn_b = at("hn_b", 178, [P, SEQ])
        pr2 = at("pr2", 96, [P, 3, 2, 2, SEQ])
        pt2 = at("pt2", 180, [P, 2, 2, 2, SEQ])
        pe_t = at("pe_t", 199.5, [P, 2, SEQ])
        pe_lo = at("pe_lo", 199.5, [P, 2, SEQ], F32R)
        pe_hi = at("pe_hi", 201.5, [P, 2, SEQ], F32R)
        emb = at("emb", 134, [P, TB, D])
        sig = at("sig", 150, [P, 2, COLS])
        cst = at("cst", 192, [P, C_END])
        par = at("par", 198.25, [P, G_END])
        squares_xt = at("squares_xt", 80, [P, TB, COLS])
        squares_hid = at("squares_hid", 154, [P, TB, COLS])
        yg_xt = at("yg_xt", 64, [P, TB, D])
        yg_hid = at("yg_hid", 128, [P, TB, D])
        yg_gate = at("yg_gate", 160, [P, TB, D])
        gain_xt = at("gain_xt", 84, [P, D])
        gain_hid = at("gain_hid", 176, [P, D])
        conv = at("conv", 203.5, [P, SEQ])
        act_tmp = at("act_tmp", 204.5, [P, SEQ])
        hid_f = at("hid_f", 205.5, [P, SEQ])
        kr = at("kr", 203.5, [P, SEQ])
        sg = at("sg", 199.5, [P, 2, 2, SEQ])
        mg_f = at("mg_f", 205.5, [P, SEQ])
        rope_b = at("rope_b", 205.5, [P, SEQ])
        stat = at("stat", 206.5, [P, 108])
        sw_bias = at("sw_bias", 199.5, [P, 2, 2, SEQ])
        table = at("table", 174, [BUCKETS + 1, 32])
        hot = at("hot", 175, [BUCKETS + 1, BAND])
        row_bias = at("row_bias", 177, [SWA_HEADS, BAND])
        ps = ctx.enter_context(nc.psum_tensor("ps", [P, 8, COLS], F32))
        band_dram = nc.dram_tensor("band_bias", (SWA_HEADS, BAND), F32, kind="Internal").ap()

        ident = cst[:, C_ID:C_ID + P]
        swap = cst[:, C_SWAP:C_SWAP + P]
        ones = cst[:, C_ONES:C_ONES + P]
        sum_parts = stat[:, 0:10].rearrange("p (t c) -> p t c", c=5)
        row_parts = stat[:, 56:62].rearrange("p (t c) -> p t c", c=3)
        rstd = stat[:, 10:12]
        ms = stat[:, 24:28]
        rstd_post = stat[:, 12:14]
        ss_c = stat[:, 14:18]
        rstd_c = stat[:, 18:22]
        minus_half = stat[:, 104:108]
        eps_col = stat[:, 22:23]
        mx = stat[:, 28:40]
        nm = stat[:, 40:48]
        rs = stat[:, 48:56]
        es = stat[:, 96:104]
        minus_sink = stat[:, 64:96]
        sink = par[:, G_SINK:G_SINK + 32]

        raw_loaded = [sem(f"raw_loaded{s}") for s in range(RAW)]
        hi_ready, lo_ready, weights_used = sem("hi_ready"), sem("lo_ready"), sem("weights_used")
        t_act, t_dve, c_act, c_dve = sem("t_act"), sem("t_dve"), sem("c_act"), sem("c_dve")
        consts_in, params_in, res_in, post_in = (sem(n) for n in ("consts_in", "params_in", "res_in", "post_in"))
        x_in = [sem(f"x_in{n}") for n in range(4)]
        memset_done = sem("memset_done")
        block0_taken, block0_sig = sem("block0_taken"), sem("block0_sig")
        added, squared, meaned, rstd_ready, normed = (
            sem(n) for n in ("added", "squared", "meaned", "rstd_ready", "normed"))
        turned, xt_hi_ready, xt_lo_ready = sem("turned"), sem("xt_hi_ready"), sem("xt_lo_ready")
        dve_step = sem("dve_step")
        c_meaned, c_rstd, c_scaled, c_turned, ct_hi_ready, ct_lo_ready = (
            sem(n) for n in ("c_meaned", "c_rstd", "c_scaled", "c_turned", "ct_hi_ready", "ct_lo_ready"))
        row_bias_mm, row_bias_out, band_stored, table_in = (
            sem(n) for n in ("row_bias_mm", "row_bias_out", "band_stored", "table_in"))
        kr_moved, kr_ready, kr_copied, ks_copied = (
            sem(n) for n in ("kr_moved", "kr_ready", "kr_copied", "ks_copied"))
        qr_swapped, qr_ready = sem("qr_swapped"), sem("qr_ready")
        bias_in, bias_masked = [sem("bias_in0"), sem("bias_in1")], sem("bias_masked")
        scored, minus_max, exp_done, p_normed, p_turned = (
            sem(n) for n in ("scored", "minus_max", "exp_done", "p_normed", "p_turned"))
        score_read, sink_exp = sem("score_read"), sem("sink_exp")
        pt_act, pv_done, o_act, o_dve = (sem(n) for n in ("pt_act", "pv_done", "o_act", "o_dve"))
        os_hi_ready, os_lo_ready, om_hi_ready, om_lo_ready, merged, mg_hi_ready, mg_lo_ready = (
            sem(n) for n in ("os_hi_ready", "os_lo_ready", "om_hi_ready", "om_lo_ready", "merged", "mg_hi_ready",
                             "mg_lo_ready"))
        conved, activated, hid_product, hid_hi_ready, hid_lo_ready = (
            sem(n) for n in ("conved", "activated", "hid_product", "hid_hi_ready", "hid_lo_ready"))
        hn_scaled, hn_summed, hn_rooted, hn_done = (sem(n) for n in ("hn_scaled", "hn_summed", "hn_rooted", "hn_done"))
        pe_in, pe_hi_ready, pe_lo_ready = (sem(n) for n in ("pe_in", "pe_hi_ready", "pe_lo_ready"))
        out_done, y_squared = sem("out_done"), sem("y_squared")

        def flat(ap):
            return ap.rearrange("p a b -> p (a b)")

        def halves(ap):
            return ap.rearrange("p (a t) -> p a t", t=P)

        block = ctx.enter_context(nc.Block())

        @block.sync
        def _(sp):
            for n in range(4):
                tb, cols = n // 2, slice((n % 2) * (D // 2), (n % 2 + 1) * (D // 2))
                sp.dma_start(res[:, tb, cols], x[tb * P:(tb + 1) * P, cols]).then_inc(x_in[n], 16)
            for u in range(RAW):
                sp.dma_start(raw[:, u, :], stream[u]).then_inc(raw_loaded[u], 16)
            turns = UNITS // RAW
            with nc.sync.Fori(1, turns) as i:
                for s in range(RAW):
                    sp.wait_ge(lo_ready, i * (2 * RAW) + (2 * (s - RAW) + 2))
                    sp.dma_start(raw[:, s, :], stream[bass.ds(i * RAW + s, 1)].rearrange("u p c -> p (u c)")
                                 ).then_inc(raw_loaded[s], 16)
            for u in range(turns * RAW, UNITS):
                sp.wait_ge(lo_ready, 2 * (u - RAW) + 2)
                sp.dma_start(raw[:, u % RAW, :], stream[u]).then_inc(raw_loaded[u % RAW], 16)
            for n in range(4):
                tb, cols = n // 2, slice((n % 2) * (D // 2), (n % 2 + 1) * (D // 2))
                sp.wait_ge(added, 4 * 4 + n + 1)
                sp.dma_start(out[tb * P:(tb + 1) * P, cols], res[:, tb, cols]).then_inc(out_done, 16)
            sp.wait_ge(out_done, 64)

        @block.tensor
        def _(pe):
            mm = pe.matmul

            def three(dst, lhs, rhs, n_lhs, n_rhs, first, last):
                mm(dst, lhs[0][n_lhs], rhs[0][n_rhs], start=first, stop=False)
                mm(dst, lhs[0][n_lhs], rhs[1][n_rhs], start=False, stop=False)
                return mm(dst, lhs[1][n_lhs], rhs[0][n_rhs], start=False, stop=last)

            def half_at(name, i, k, j):
                u = UNIT0[name] + k
                pe.wait_ge(lo_ready, i * (2 * STAGES[name][1]) + (2 * u + j + 1))
                return (2 * u + j) % SLOTS

            def tile_free(name, i, k):
                _, a, d = TILES[name]
                if k >= 4 or not isinstance(i, int):
                    if k % 2 == 0:
                        pe.wait_ge(t_act, i * (STAGES[name][1] // 2) + (a + k // 2 - 1))
                    else:
                        pe.wait_ge(t_dve, i * (STAGES[name][1] // 2) + (d + k // 2 - 1))

            def all_tiles_read(name):
                _, a, d = TILES[name]
                pe.wait_ge(t_act, a) if a else None
                pe.wait_ge(t_dve, d) if d else None

            def chunks_read(n):
                if n > 0:
                    pe.wait_ge(c_act, n)
                    pe.wait_ge(c_dve, n)

            def t_stage(name, acts, free):
                stage_loop(nc.tensor, name, t_body(name, acts, free))

            def t_body(name, acts, free):
                t0 = TILES[name][0]

                def body(i, k):
                    free(i, k)
                    for j in range(2):
                        s = half_at(name, i, k, j)
                        wh = w_hi[:, s, :].rearrange("p (c n) -> p c n", n=P)
                        wl = w_lo[:, s, :].rearrange("p (c n) -> p c n", n=P)
                        hi, lo = acts(k)
                        for c in range(8):
                            kt = 8 * j + c
                            if name in AFTER_NORM and k == 0 and kt % 2 == 0:
                                xt_ready(kt + 2)
                            dst = ps[:, (t0 + k) % 4, 0:SEQ]
                            last = three(dst, (wh, wl), (hi, lo), (slice(None), c), (slice(None), kt),
                                         kt == 0, kt == KT - 1)
                        last.then_inc(weights_used, 1)
                return body

            def n_stage(name, per_chunk, hi, lo, operand=None):
                chunks_read(CHUNKS[name])
                stage_loop(nc.tensor, name, n_body(name, per_chunk, hi, lo, operand=operand))

            def n_body(name, per_chunk, hi, lo, ready=None, operand=None):
                c0 = CHUNKS[name]
                group = STAGES[name][1]

                def body(i, k):
                    ch, g = k // per_chunk, k % per_chunk
                    if g == 0 and (ch >= 1 or not isinstance(i, int)):
                        step = group // per_chunk
                        n = c0 + ch - 1
                        pe.wait_ge(c_act, i * step + n)
                        pe.wait_ge(c_dve, i * step + n)
                    if ready:
                        ready(i, k)
                    for j in range(2):
                        s = half_at(name, i, k, j)
                        for c in range(2):
                            kt = 4 * g + 2 * j + c
                            if operand and k < per_chunk:
                                operand(kt)
                            if name in AFTER_NORM and k < 4 and kt % 2 == 0:
                                xt_ready(max(kt + 2, 4))
                            cols = (slice(None), s, slice(c * COLS, (c + 1) * COLS))
                            for tb in range(TB):
                                dst = ps[:, 4 + 2 * ((c0 + ch) % 2) + tb, :]
                                last = three(dst, (hi, lo), (w_hi, w_lo),
                                             (slice(None), kt, slice(tb * P, (tb + 1) * P)), cols,
                                             kt == 0, kt == 4 * per_chunk - 1)
                        last.then_inc(weights_used, 1)
                return body

            counts = {"norm": 0, "job": 0}

            def pre_norm(tiles, chunks, banks):
                e = counts["norm"]
                counts["norm"] += 1
                all_tiles_read(tiles)
                chunks_read(chunks)
                for g in range(8):
                    tb, q = g // 4, g % 4
                    pe.wait_ge(normed, 8 * e + g + 1)
                    for kt in range(4 * q, 4 * q + 4):
                        c = (kt % 2) * SEQ + tb * P
                        last = pe.transpose(ps[:, banks[kt // 2], c:c + P], y[:, tb, kt * P:(kt + 1) * P], ident)
                    last.then_inc(turned, 1)

            def xt_ready(n):
                pe.wait_ge(xt_lo_ready, KT * (counts["norm"] - 1) + n)

            pe.wait_ge(consts_in, 16)
            pre_norm("k1", 0, BANKS_N[0])
            n_stage("cq", 4, xt_hi, xt_lo)

            xt = lambda k: (xt_hi, xt_lo)
            t_stage("k1", xt, lambda i, k: None)
            chunks_read(2)
            pe.wait_ge(table_in, 32)
            mm(ps[0:SWA_HEADS, 7, 0:BAND], table[:, :], hot[:, :], start=True, stop=True).then_inc(row_bias_mm, 1)
            for kt in range(6):
                src = c1[:, :, kt * P:(kt + 1) * P]
                if kt == 0:
                    pe.wait_ge(c_scaled, 4)
                for tb in range(TB):
                    last = pe.transpose(ps[:, 4 + kt // 2, (kt % 2) * SEQ + tb * P:(kt % 2) * SEQ + (tb + 1) * P],
                                        src[:, tb, :], ident)
                if kt % 2:
                    last.then_inc(c_turned, 1)

            all_tiles_read("qs")
            t_stage("qs", xt, lambda i, k: tile_free("qs", i, k))

            all_tiles_read("qup")
            pe.wait_ge(ct_lo_ready, 4)
            for k in range(6):
                for j in range(2):
                    s = half_at("qup", 0, k, j)
                    for tt in range(2):
                        tile = 4 * k + 2 * j + tt
                        tile_free("qup", 0, tile)
                        wh = w_hi[:, s, :].rearrange("p (t c n) -> p t c n", t=2, n=P)
                        wl = w_lo[:, s, :].rearrange("p (t c n) -> p t c n", t=2, n=P)
                        for kt in range(4):
                            last = three(ps[:, (TILES["qup"][0] + tile) % 4, 0:SEQ], (wh, wl), (ct_hi, ct_lo),
                                         (slice(None), tt, kt), (slice(None), kt), kt == 0, kt == 3)
                    last.then_inc(weights_used, 1)
            pe.wait_ge(ct_lo_ready, 6)
            pe.wait_ge(row_bias_out, 1)
            pe.wait_ge(t_act, TILES["qup"][1] + 4)
            pe.wait_ge(t_dve, TILES["qup"][2] + 4)
            for r in range(4):
                last = mm(ps[:, 4 + r, :], swap, flat(qr[:, 2 * r:2 * r + 2, :]), start=True, stop=True)
                last.then_inc(qr_swapped, 1)
            all_tiles_read("kvk")
            for k in range(2):
                for j in range(2):
                    s = half_at("kvk", 0, k, j)
                    for tt in range(4):
                        tile = 8 * k + 4 * j + tt
                        if tile >= 4:
                            pe.wait_ge(t_act, TILES["kvk"][1] + tile - 3)
                        wh = w_hi[:, s, :].rearrange("p (t c n) -> p t c n", t=4, n=P)
                        wl = w_lo[:, s, :].rearrange("p (t c n) -> p t c n", t=4, n=P)
                        for kt in range(2):
                            last = three(ps[:, (TILES["kvk"][0] + tile) % 4, 0:SEQ], (wh, wl), (ct_hi, ct_lo),
                                         (slice(None), tt, kt), (slice(None), 4 + kt), kt == 0, kt == 1)
                    last.then_inc(weights_used, 1)

            def narrow(name, hi, lo, first_kt, chunks=range(4)):
                for ch in chunks:
                    s = half_at(name, 0, ch // 2, ch % 2)
                    chunks_read(CHUNKS[name] + ch - 1)
                    for kt in range(2):
                        for tb in range(TB):
                            dst = ps[:, 4 + 2 * ((CHUNKS[name] + ch) % 2) + tb, :]
                            last = three(dst, (hi, lo), (w_hi, w_lo),
                                         (slice(None), first_kt + kt, slice(tb * P, (tb + 1) * P)),
                                         (slice(None), s, slice(kt * COLS, (kt + 1) * COLS)), kt == 0, kt == 1)
                    last.then_inc(weights_used, 1)

            pe.wait_ge(qr_ready, 4)
            narrow("kvv", ct_hi, ct_lo, 4, (0,))
            pe.wait_ge(qr_ready, 8)
            narrow("kvv", ct_hi, ct_lo, 4, (1, 2, 3))

            def attend(blockno, between):
                jobs = attention_jobs(blockno)
                g0 = counts["job"]
                counts["job"] += len(jobs)

                def scores(n):
                    kind, j = jobs[n]
                    g = g0 + n
                    if n >= 2 and jobs[n - 2][0] == "a2":
                        pe.wait_ge(exp_done, g - 1)
                    elif n >= 2:
                        pe.wait_ge(score_read, score_reads(g - 2))
                    for h in range(2):
                        bank = ps[:, score_pair(blockno, g) + h, :]
                        half = slice(64 * h, 64 * h + 64)
                        if kind == "swa":
                            mm(bank[:, 0:SEQ], qs[half, j, 1, :], ks[half, j // 4, :], start=True, stop=True)
                            last = mm(bank[:, SEQ:BAND], qs[half, j, 0, :], ks[half, j // 4, 0:P],
                                      start=True, stop=True)
                        elif kind == "mla":
                            head = 2 * j + h
                            mm(bank[:, 0:SEQ], qn[:, head, 1, :], kn[:, head, :], start=True, stop=False)
                            mm(bank[:, 0:SEQ], qr[half, j, P:SEQ], kr[half, :], start=False, stop=True)
                            mm(bank[:, SEQ:BAND], qn[:, head, 0, :], kn[:, head, 0:P], start=True, stop=False)
                            last = mm(bank[:, SEQ:BAND], qr[half, j, 0:P], kr[half, 0:P], start=False, stop=True)
                        else:
                            head = 2 * j + h
                            q_t, k_t = (qa2, ka2[:, head // 4, :]) if kind == "a2" else (qb2, kb2[:, head, :])
                            for blk in range(TB):
                                last = mm(bank[:, blk * SEQ:(blk + 1) * SEQ], q_t[:, head, blk, :], k_t,
                                          start=True, stop=True)
                    last.then_inc(scored, 1)

                def turn(n):
                    g = g0 + n
                    pe.wait_ge(p_normed, g + 1)
                    if g >= 1:
                        pe.wait_ge(pt_act, g)
                    for h in range(2):
                        bank = ps[:, TURN_BANK[blockno] + h, :]
                        if blockno == 1:
                            pr = pr1[:, g % 3, h, :]
                            pe.transpose(bank[:, 0:P], pr[:, SEQ:BAND], ident)
                            pe.transpose(bank[:, P:SEQ], pr[:, 0:P], ident)
                            last = pe.transpose(bank[:, SEQ:BAND], pr[:, P:SEQ], ident)
                        else:
                            for kt in range(2):
                                for blk in range(TB):
                                    c = (2 * kt + blk) * P
                                    last = pe.transpose(bank[:, c:c + P],
                                                        pr2[:, g % 3, h, blk, kt * P:(kt + 1) * P], ident)
                    last.then_inc(p_turned, 1)

                def values(n):
                    kind, j = jobs[n]
                    g = g0 + n
                    pe.wait_ge(pt_act, g + 1)
                    if g >= 2:
                        pe.wait_ge(o_act, g - 1)
                    if blockno == 2 and n >= 2:
                        pe.wait_ge(o_dve, n - 1)
                    for h in range(2):
                        dst = ps[:, VALUE_BANK[blockno] + g % 2, h * SEQ:(h + 1) * SEQ]
                        if blockno == 1:
                            pt = pt1[:, g % 2, h, :]
                            if kind == "swa":
                                dst = ps[64 * h:64 * h + 64, 6 + g % 2, 0:SEQ]
                                v0, v1_ = (vs[:, kt, j // 4, :] for kt in range(2))
                            else:
                                c = (2 * j + h) * P
                                v0, v1_ = (v1[:, kt, c:c + P] for kt in range(2))
                            mm(dst[:, 0:P], v0, pt[:, 0:P], start=True, stop=True)
                            mm(dst[:, P:SEQ], v0, pt[:, P:SEQ], start=True, stop=False)
                            last = mm(dst[:, P:SEQ], v1_, pt[:, SEQ:BAND], start=False, stop=True)
                        else:
                            head = 2 * j + h
                            c = (head // 4) * P if kind == "a2" else SEQ + head * P
                            for kt in range(2):
                                pt = pt2[:, g % 2, h, kt, :]
                                last = mm(dst, v2[:, kt, c:c + P], pt, start=kt == 0, stop=kt == 1)
                    last.then_inc(pv_done, 1)

                scores(0)
                for n in range(len(jobs) + 2):
                    if n + 1 < len(jobs):
                        scores(n + 1)
                    if n >= 2:
                        values(n - 2)
                    if 1 <= n <= len(jobs):
                        turn(n - 1)
                    for work in between.get(n - len(jobs) + 1, ()):
                        work()

            def merge(name):
                _, ta, td = TILES[name]
                ahead_of = {kind: [sum(u[0] == kind for u in MERGE[name][:k]) for k in range(len(MERGE[name]))]
                            for kind in ("gate", "out")}
                operands = [(om_hi, om_lo), (os_hi, os_lo)]

                def free(i, k):
                    kind, _, branch = MERGE[name][k]
                    if name == "gate0":
                        pe.wait_ge(score_read, N_SWA + N_MLA - 1)
                    elif kind == "gate":
                        pe.wait_ge(t_act, i * 4 + (ta + ahead_of["gate"][k] - 1))
                    else:
                        if name == "mergeZ" and k >= 4:
                            pe.wait_ge(t_act, ta + k - 3)
                        elif td + ahead_of["out"][k] > 1 or not isinstance(i, int):
                            n = td + ahead_of["out"][k] - 1
                            pe.wait_ge(t_dve, i * 4 + n)
                        pe.wait_ge(om_lo_ready if branch == 0 else os_lo_ready, 4)
                return t_body(name, lambda k: (xt_hi, xt_lo) if MERGE[name][k][0] == "gate"
                              else operands[MERGE[name][k][2]], free)

            all_tiles_read("gate0")
            chunks_read(6)
            pe.wait_ge(kr_copied, 16)
            pe.wait_ge(ks_copied, 32)
            gate0 = merge("gate0")
            attend(1, {0: [lambda: gate0(0, 0)], 1: [lambda: gate0(0, 1)]})

            pe.wait_ge(score_read, N_SWA + N_MLA)
            for name in ("merge", "mergeZ"):
                stage_loop(nc.tensor, name, merge(name))
            pe.wait_ge(o_act, N_SWA + N_MLA)
            n_stage("wout", 4, mg_hi, mg_lo, lambda kt: pe.wait_ge(mg_lo_ready, kt + 1))

            def ffn(up, down, per_chunk, per_tile):
                all_tiles_read(up)
                if per_tile == 2:
                    def free(i, k):
                        if k >= 4 or not isinstance(i, int):
                            pe.wait_ge(t_dve, i * 4 + (TILES[up][2] + k - 3))
                else:
                    def free(i, k):
                        if k >= 4 or not isinstance(i, int):
                            pe.wait_ge(hid_product, i * 4 + (HID0[up] + k - 3))
                t_stage(up, xt, free)
                tiles = STAGES[up][0] // per_tile

                def hidden(kt):
                    if kt == 0 or kt >= tiles - 4:
                        pe.wait_ge(hid_lo_ready, HID0[up] + max(kt + 1, tiles - 4))
                n_stage(down, per_chunk, hid_hi, hid_lo, hidden)

            pre_norm("upA", CHUNKS["dnA"], BANKS_T)
            ffn("upA", "dnA", H1A // 4, 2)
            ffn("upB", "dnB", H1B // 4, 2)
            pre_norm("qk2", CHUNKS["v2"], BANKS_N[CHUNKS["v2"] % 2])

            for k in range(10):
                ch, g = k // 2, k % 2
                if g == 0:
                    chunks_read(CHUNKS["v2"] + ch - 1)
                for j in range(2):
                    s = half_at("v2", 0, k, j)
                    for c in range(4):
                        kt = 8 * g + 4 * j + c
                        if k < 2 and kt % 2 == 0:
                            xt_ready(max(kt + 2, 4))
                        for tb in range(TB):
                            dst = ps[:, 4 + 2 * ((CHUNKS["v2"] + ch) % 2) + tb, 0:SEQ]
                            last = three(dst, (xt_hi, xt_lo), (w_hi, w_lo),
                                         (slice(None), kt, slice(tb * P, (tb + 1) * P)),
                                         (slice(None), s, slice(c * SEQ, (c + 1) * SEQ)), kt == 0, kt == KT - 1)
                    last.then_inc(weights_used, 1)

            def head_sums(n):
                pe.wait_ge(hn_scaled, 2 * n + 2)
                if n == 0:
                    chunks_read(CHUNKS["v2"] + 5)
                if n >= 4:
                    pe.wait_ge(hn_done, n - 3)
                bank = ps[:, 4 + n % 4, :]
                mm(bank[:, 0:SEQ], ones, hn_sq[:, n % 2, :], start=True, stop=True)
                mm(bank[:, SEQ:2 * SEQ], swap, hn_x[:, n % 2, :], start=True, stop=True).then_inc(hn_summed, 1)

            t0 = TILES["qk2"][0]
            all_tiles_read("qk2")
            for k in range(26):
                if k >= 4:
                    n = k - 4
                    _, ta, td = TILES["qk2"]
                    if n < 10 or n % 2 == 0:
                        pe.wait_ge(t_act, ta + (n + 1 if n < 10 else n // 2 + 6))
                    else:
                        pe.wait_ge(t_dve, td + (n - 9) // 2)
                for j in range(2):
                    s = half_at("qk2", 0, k, j)
                    wh = w_hi[:, s, :].rearrange("p (c n) -> p c n", n=P)
                    wl = w_lo[:, s, :].rearrange("p (c n) -> p c n", n=P)
                    for c in range(8):
                        kt = 8 * j + c
                        last = three(ps[:, (t0 + k) % 4, 0:SEQ], (wh, wl), (xt_hi, xt_lo), (slice(None), c),
                                     (slice(None), kt), kt == 0, kt == KT - 1)
                    last.then_inc(weights_used, 1)
                if 1 <= k <= 10:
                    head_sums(k - 1)

            all_tiles_read("up2a")
            pe.wait_ge(hn_done, 10)
            jobs = N_SWA + N_MLA + N_A2 + N_B2

            def heads_ready(i, k):
                if k < 4:
                    pe.wait_ge(o_act, N_SWA + N_MLA + 2 * k + 2)
                    pe.wait_ge(o_dve, 2 * k + 2)
                if k == 0:
                    pe.wait_ge(score_read, score_reads(jobs - 2))
                if k == 4:
                    pe.wait_ge(score_read, score_reads(jobs - 1))
            wo2 = n_body("wo2", 4, xt_hi, xt_lo, heads_ready)
            attend(2, {0: [lambda: wo2(0, 0)], 1: [lambda: wo2(0, 1)]})
            for k in range(2, STAGES["wo2"][0]):
                wo2(0, k)
            pre_norm("up2a", CHUNKS["dn2a"], BANKS_T)
            ffn("up2a", "dn2a", H2A // 4, 1)
            ffn("up2b", "dn2b", H2A // 4, 1)

            pe.wait_ge(pe_lo_ready, 1)
            narrow("proj", pe_hi, pe_lo, 0, (0, 1))
            pre_norm("end", CHUNKS["proj"] + 2, BANKS_N[CHUNKS["proj"] % 2])
            xt_ready(8)
            narrow("proj", pe_hi, pe_lo, 0, (2, 3))
            n_stage("gate", 4, xt_hi, xt_lo)

        @block.scalar
        def _(act):
            activation = nc.scalar.activation

            def split_hi(h, i=0, step=0):
                if h >= 2 * UNITS:
                    return
                slot, u = h % SLOTS, h // 2
                act.wait_ge(raw_loaded[u % RAW], i * (step * 16 // (2 * RAW)) + 16 * (u // RAW + 1))
                if h >= SLOTS or not isinstance(i, int):
                    act.wait_ge(weights_used, i * step + (h - SLOTS + 1))
                activation(w_hi[:, slot, :], raw[:, u % RAW, (h % 2) * HALF:(h % 2 + 1) * HALF], ACT.Copy
                           ).then_inc(hi_ready, 1)

            def ahead_half(name, i, k, j):
                split_hi(2 * (UNIT0[name] + k) + j + LEAD, i, 2 * STAGES[name][1])

            def ahead(name, i, k):
                for j in range(2):
                    ahead_half(name, i, k, j)

            def used(name, i, k, j=1):
                act.wait_ge(weights_used, i * (2 * STAGES[name][1]) + (2 * (UNIT0[name] + k) + j + 1))

            counts = {"norm": 0, "post": 0, "job": 0}

            def row_squares(after=None):
                for n in range(4):
                    tb, half = n // 2, n % 2
                    if counts["post"] == 0:
                        act.wait_ge(x_in[n], 16)
                    else:
                        act.wait_ge(added, 4 * (counts["post"] - 1) + n + 1)
                    cols = slice(half * (D // 2), (half + 1) * (D // 2))
                    activation(y[:, tb, cols], res[:, tb, cols], ACT.Square, scale=D ** -0.5,
                               accum_out=row_parts[:, tb, half:half + 1]).then_inc(squared, 1)
                if after:
                    ahead(after, 0, STAGES[after][0] - 1)

            def turned_hi(banks):
                e = counts["norm"]
                counts["norm"] += 1
                act.wait_ge(params_in, 16)
                for kt in range(KT):
                    act.wait_ge(turned, 8 * e + 4 + kt // 4 + 1)
                    c = G_PRE + e * KT + kt
                    activation(xt_hi[:, kt, :], ps[:, banks[kt // 2], (kt % 2) * SEQ:(kt % 2 + 1) * SEQ], ACT.Copy,
                               scale=par[:, c:c + 1]).then_inc(xt_hi_ready, 1)

            def chunk_squares(name, per_chunk, junk, begun=0):
                c0 = CHUNKS[name]
                bound = STAGES[name][1] // per_chunk

                def body(i, k):
                    if k >= begun and not is_last(name, i, k):
                        ahead(name, i, k)
                    if k % per_chunk == per_chunk - 1:
                        ch = k // per_chunk
                        for tb in range(TB):
                            if tb == 0:
                                act.wait_ge(block0_taken, i * bound + (4 * counts["post"] + ch + 1))
                            else:
                                act.wait_ge(c_dve, i * bound + (c0 + ch + 1))
                            ins = activation(junk[:, tb, :], y[:, tb, bass.ds(i * (bound * COLS) + ch * COLS, COLS)],
                                             ACT.Square, scale=D ** -0.5,
                                             accum_out=stat[:, bass.ds(i * bound + (tb * 5 + ch), 1)])
                        ins.then_inc(c_act, 1)
                stage_loop(nc.scalar, name, body, peel=True)

            row_squares()
            for h in range(2):
                split_hi(h)
            turned_hi(BANKS_N[0])
            for h in range(2, LEAD):
                split_hi(h)

            for k in range(8):
                ahead("cq", 0, k)
                if k == 3 or k == 7:
                    act.wait_ge(c_dve, k // 4 + 1)
                    cols = slice(0, COLS) if k == 3 else slice(COLS, COLS + SEQ)
                    q = 0 if k == 3 else 2
                    for tb in range(TB):
                        ins = activation(c_junk[:, tb, cols], c1[:, tb, cols], ACT.Square,
                                         accum_out=ss_c[:, q + tb:q + tb + 1])
                    ins.then_inc(c_act, 1)
            act.wait_ge(memset_done, 5)
            for k in range(3):
                ahead("k1", 0, k)
                if k >= 1:
                    used("k1", 0, k)
                    activation(ks[0:64, 2 * k - 2, :], ps[0:64, k, 0:SEQ], ACT.Copy)
                    activation(ks[64:128, 2 * k - 1, :], ps[64:128, k, 0:SEQ], ACT.Copy).then_inc(t_act, 1)

            def q_s(i, k):
                ahead("qs", i, k)
                used("qs", i, k)
                if k % 2 == 0:
                    dst = qs[:, bass.ds(i * 4 + k, 1), :, :].rearrange("p o a t -> p (o a) t")
                    activation(dst, halves(ps[:, (TILES["qs"][0] + k) % 4, 0:SEQ])[:, :, ::-1], ACT.Copy
                               ).then_inc(t_act, 1)
            for kt in range(6):
                act.wait_ge(c_turned, kt // 2 + 1)
                g = par[:, G_QN + kt:G_QN + kt + 1]
                activation(ct_hi[:, kt, :], ps[:, 4 + kt // 2, (kt % 2) * SEQ:(kt % 2 + 1) * SEQ], ACT.Copy,
                           scale=g).then_inc(ct_hi_ready, 1)
            stage_loop(nc.scalar, "qs", q_s)
            for k in range(6):
                for j in range(2):
                    used("qup", 0, k, j)
                    for tt in range(2):
                        tile = 4 * k + 2 * j + tt
                        if tile % 2 == 0:
                            dst = qr[:, tile, :] if tile < 8 else flat(qn[:, tile - 8, :, :])
                            activation(dst, ps[:, (TILES["qup"][0] + tile) % 4, 0:SEQ], ACT.Copy).then_inc(t_act, 1)
                    ahead_half("qup", 0, k, j)
            for k in range(2):
                for j in range(2):
                    used("kvk", 0, k, j)
                    for tt in range(4):
                        tile = 8 * k + 4 * j + tt
                        activation(kn[:, tile, :], ps[:, (TILES["kvk"][0] + tile) % 4, 0:SEQ], ACT.Copy
                                   ).then_inc(t_act, 1)
                    ahead_half("kvk", 0, k, j)
            for k in range(2):
                for j in range(2):
                    ch = 2 * k + j
                    used("kvv", 0, k, j)
                    activation(v1[:, 0, ch * COLS:(ch + 1) * COLS], ps[:, 4 + 2 * ((CHUNKS["kvv"] + ch) % 2), :],
                               ACT.Copy).then_inc(c_act, 1)
                    ahead_half("kvv", 0, k, j)

            def attend(blockno, between):
                jobs = attention_jobs(blockno)
                g0 = counts["job"]
                counts["job"] += len(jobs)

                def exponentials(n):
                    kind, j = jobs[n]
                    g = g0 + n
                    r = g % 2
                    act.wait_ge(minus_max, g + 1)
                    if kind == "swa":
                        for h in range(2):
                            c = 4 * r + 2 * h
                            last = activation(es[:, c:c + 2], nm[:, c:c + 2], ACT.Exp,
                                              bias=sink[:, 2 * j + h:2 * j + h + 1])
                        last.then_inc(sink_exp, 1)
                    for h in range(2):
                        for blk in range(TB):
                            bias = nm[:, 4 * r + 2 * h + blk:4 * r + 2 * h + blk + 1]
                            total = rs[:, 4 * r + 2 * h + blk:4 * r + 2 * h + blk + 1]
                            if blockno == 1:
                                dst = pr1[:, g % 3, h, 0:SEQ] if blk else pr1[:, g % 3, h, SEQ:BAND]
                            else:
                                dst = pr2[:, g % 3, h, blk, :]
                            if kind == "a2":
                                src, scale = ps[:, score_pair(blockno, g) + h, blk * SEQ:(blk + 1) * SEQ], HEAD_SCALE
                                if h == 0 and blk == 0:
                                    act.wait_ge(p_turned, g - 2)
                            else:
                                src, scale = dst, 1.0
                            last = activation(dst, src, ACT.Exp, bias=bias, scale=scale, accum_out=total)
                    last.then_inc(exp_done, 1)

                def turned_out(n):
                    g = g0 + n
                    act.wait_ge(p_turned, g + 1)
                    if g >= 2:
                        act.wait_ge(pv_done, g - 1)
                    if blockno == 1:
                        activation(pt1[:, g % 2, :, :], ps[:, 4:6, 0:BAND], ACT.Copy).then_inc(pt_act, 1)
                    else:
                        activation(pt2[:, g % 2, :, :, :].rearrange("p h a b -> p h (a b)"), ps[:, 0:2, :], ACT.Copy
                                   ).then_inc(pt_act, 1)

                def outputs(n):
                    kind, j = jobs[n]
                    g = g0 + n
                    act.wait_ge(pv_done, g + 1)
                    src = ps[:, VALUE_BANK[blockno] + g % 2, :]
                    if kind == "swa":
                        activation(qs[:, j, :, ::-1], halves(src[:, 0:SEQ]), ACT.Copy).then_inc(o_act, 1)
                    elif kind == "mla":
                        activation(qn[:, 2 * j:2 * j + 2, :, :].rearrange("p h a t -> p (h a t)"), src, ACT.Copy
                                   ).then_inc(o_act, 1)
                    elif kind == "a2":
                        activation(flat(xt_hi[:, 2 * j:2 * j + 2, :]), src, ACT.Copy).then_inc(o_act, 1)
                    else:
                        dst = xt_hi[:, 8 + 2 * j:10 + 2 * j, :].rearrange("p h (a t) -> p (h a) t", t=P)[:, :, ::-1]
                        activation(dst, src.rearrange("p (a t) -> p a t", t=P), ACT.Copy).then_inc(o_act, 1)

                for n in range(len(jobs) + 2):
                    if n >= 2:
                        turned_out(n - 2)
                    if n < len(jobs):
                        exponentials(n)
                    if n >= 2:
                        outputs(n - 2)
                    for work in between.get(n - len(jobs) + 1, ()):
                        work()

            def outputs_hi(src, dst, q, done):
                activation(flat(dst[:, 4 * q:4 * q + 4, :]),
                           src[:, 4 * q:4 * q + 4, :, :].rearrange("p a b c -> p (a b c)"), ACT.Copy).then_inc(done, 1)

            def os_hi_part(qq):
                act.wait_ge(scored, N_SWA + N_MLA)
                act.wait_ge(o_act, N_SWA)
                for q in qq:
                    outputs_hi(qs, os_hi, q, os_hi_ready)

            def merge(name):
                _, ta, td = TILES[name]

                def body(i, k):
                    ahead(name, i, k)
                    kind, place, branch = MERGE[name][k]
                    tile = MERGE_TILE0[name] + place
                    if kind == "gate":
                        used(name, i, k)
                        if tile >= 2:
                            act.wait_ge(merged, i * 2 + (tile - 1))
                        activation(sg[:, place % 2, branch, :], ps[:, (TILES[name][0] + k) % 4, 0:SEQ], ACT.Sigmoid
                                   ).then_inc(t_act, 1)
                    elif branch == 0:
                        act.wait_ge(merged, i * 2 + (tile + 1))
                        dst = mg_hi[:, bass.ds(i * 2 + tile, 1), :]
                        activation(dst.rearrange("p a t -> p (a t)"), mg_f[:, :], ACT.Copy).then_inc(mg_hi_ready, 1)
                return body
            gate0 = merge("gate0")
            attend(1, {0: [lambda: os_hi_part((0, 1))], 1: [lambda: gate0(0, 0), lambda: os_hi_part((2, 3))],
                       2: [lambda: gate0(0, 1)]})
            act.wait_ge(o_act, N_SWA + N_MLA)
            act.wait_ge(pv_done, N_SWA + N_MLA)
            for q in range(4):
                outputs_hi(qn, om_hi, q, om_hi_ready)
            for name in ("merge", "mergeZ"):
                stage_loop(nc.scalar, name, merge(name))
            chunk_squares("wout", 4, squares_hid)
            counts["post"] += 1
            row_squares("wout")
            turned_hi(BANKS_T)

            def conv_ffn(name):
                def body(i, k):
                    ahead(name, i, k)
                    if k % 2:
                        n = i * 2 + (HID0[name] + k // 2 + 1)
                        act.wait_ge(conved, n)
                        activation(act_tmp[:, :], conv[:, :], ACT.Gelu_apprx_tanh).then_inc(activated, 1)
                        act.wait_ge(hid_product, n)
                        activation(hid_hi[:, bass.ds(i * 2 + k // 2, 1), :].rearrange("p a t -> p (a t)"),
                                   hid_f[:, :], ACT.Copy).then_inc(hid_hi_ready, 1)
                act.wait_ge(weights_used, 2 * UNIT0[name])
                stage_loop(nc.scalar, name, body)

            def relu_ffn(name):
                def body(i, k):
                    ahead(name, i, k)
                    used(name, i, k)
                    n = HID0[name] + k
                    act.wait_ge(hid_product, i * 4 + n)
                    act.wait_ge(hid_hi_ready, i * 4 + n)
                    activation(act_tmp[:, :], ps[:, (TILES[name][0] + k) % 4, 0:SEQ], ACT.Relu).then_inc(t_act, 1)
                    act.wait_ge(t_act, i * 4 + (TILES[name][1] + k + 1))
                    activation(hid_hi[:, bass.ds(i * 4 + k, 1), :].rearrange("p a t -> p (a t)"),
                               act_tmp[:, :], ACT.Square).then_inc(hid_hi_ready, 1)
                act.wait_ge(weights_used, 2 * UNIT0[name])
                stage_loop(nc.scalar, name, body)

            def down(name, per_chunk):
                def body(i, k):
                    ahead(name, i, k)
                    if k % per_chunk == per_chunk - 1:
                        used(name, i, k)
                        act.wait_ge(c_dve, i * (STAGES[name][1] // per_chunk) + (CHUNKS[name] + k // per_chunk + 1))
                        act.sem_inc(c_act, 1)
                stage_loop(nc.scalar, name, body)

            conv_ffn("upA")
            down("dnA", H1A // 4)
            conv_ffn("upB")
            chunk_squares("dnB", H1B // 4, squares_xt)
            counts["post"] += 1
            row_squares("dnB")
            turned_hi(BANKS_N[CHUNKS["v2"] % 2])

            for k in range(10):
                ahead("v2", 0, k)
                if k % 2:
                    ch = k // 2
                    used("v2", 0, k)
                    activation(v2[:, 0, ch * SEQ:(ch + 1) * SEQ],
                               ps[:, 4 + 2 * ((CHUNKS["v2"] + ch) % 2), 0:SEQ], ACT.Copy).then_inc(c_act, 1)
            for k in range(26):
                ahead("qk2", 0, k)
                used("qk2", 0, k)
                src = ps[:, (TILES["qk2"][0] + k) % 4, 0:SEQ]
                if k < 10:
                    if k >= 2:
                        act.wait_ge(hn_done, k - 1)
                        act.wait_ge(hn_summed, k - 1)
                    g = par[:, G_K2:G_K2 + 1] if k < 2 else par[:, G_Q2:G_Q2 + 1]
                    activation(hn_x[:, k % 2, :], src, ACT.Copy, scale=g).then_inc(hn_scaled, 1)
                    activation(hn_sq[:, k % 2, :], src, ACT.Square).then_inc(hn_scaled, 1)
                    act.wait_ge(hn_scaled, 2 * k + 2)
                    act.sem_inc(t_act, 1)
                elif k < 18 and k % 2 == 0:
                    activation(kb2[:, k - 10, :], src, ACT.Copy).then_inc(t_act, 1)
                elif k % 2 == 0:
                    activation(qb2[:, k - 18, :, ::-1], halves(src), ACT.Copy).then_inc(t_act, 1)
                if 1 <= k <= 10:
                    n = k - 1
                    act.wait_ge(hn_summed, n + 1)
                    if n >= 1:
                        act.wait_ge(hn_done, n)
                    activation(hn_r[:, :], ps[:, 4 + n % 4, 0:SEQ], ACT.Sqrt, scale=1.0 / P, bias=eps_col
                               ).then_inc(hn_rooted, 1)
            act.wait_ge(weights_used, 2 * UNIT0["wo2"])
            attend(2, {1: [lambda: ahead("wo2", 0, 0)], 2: [lambda: ahead("wo2", 0, 1)]})
            chunk_squares("wo2", 4, squares_hid, begun=2)
            counts["post"] += 1
            row_squares("wo2")
            turned_hi(BANKS_T)
            relu_ffn("up2a")
            down("dn2a", H2A // 4)
            relu_ffn("up2b")
            act.wait_ge(pe_in, 16)
            activation(pe_hi[:, :, :], pe_t[:, :, :], ACT.Copy).then_inc(pe_hi_ready, 1)
            chunk_squares("dn2b", H2A // 4, squares_xt)
            counts["post"] += 1
            for k in range(2):
                if k:
                    row_squares("dn2b")
                    turned_hi(BANKS_N[CHUNKS["proj"] % 2])
                    ahead("proj", 0, 0)
                for j in range(2):
                    ch = 2 * k + j
                    used("proj", 0, k, j)
                    activation(emb[:, 0, ch * COLS:(ch + 1) * COLS], ps[:, 4 + 2 * ((CHUNKS["proj"] + ch) % 2), :],
                               ACT.Copy).then_inc(c_act, 1)
                    if k:
                        ahead_half("proj", 0, k, j)
            def gated_squares(ch):
                if ch:
                    act.wait_ge(y_squared, ch)
                for tb in range(TB):
                    if tb == 0:
                        act.wait_ge(block0_taken, 4 * counts["post"] + ch + 1)
                    else:
                        act.wait_ge(c_dve, CHUNKS["gate"] + ch + 1)
                    last = activation(squares_hid[:, tb, :], y[:, tb, ch * COLS:(ch + 1) * COLS], ACT.Square,
                                      scale=D ** -0.5, accum_out=sum_parts[:, tb, ch:ch + 1])
                last.then_inc(y_squared, 1)

            for k in range(16):
                ahead("gate", 0, k)
                if k % 4 == 3:
                    ch = k // 4
                    if ch:
                        gated_squares(ch - 1)
                    used("gate", 0, k)
                    for tb, done in ((0, block0_sig), (1, c_act)):
                        activation(sig[:, tb, :], ps[:, 4 + 2 * ((CHUNKS["gate"] + ch) % 2) + tb, :], ACT.Sigmoid
                                   ).then_inc(done, 1)
            gated_squares(3)

        @block.vector
        def _(dve):
            tt, ts, stt = nc.vector.tensor_tensor, nc.vector.tensor_scalar, nc.vector.scalar_tensor_tensor
            step = Steps(dve, dve_step)

            def split_lo(h, i=0, stp=0):
                if h >= 2 * UNITS:
                    return
                slot, u = h % SLOTS, h // 2
                dve.wait_ge(hi_ready, i * stp + (h + 1))
                tt(w_lo[:, slot, :], raw[:, u % RAW, (h % 2) * HALF:(h % 2 + 1) * HALF],
                   w_hi[:, slot, :].bitcast(F32), ALU.subtract).then_inc(lo_ready, 1)

            def ahead_half(name, i, k, j):
                split_lo(2 * (UNIT0[name] + k) + j + LEAD, i, 2 * STAGES[name][1])

            def ahead(name, i, k):
                for j in range(2):
                    ahead_half(name, i, k, j)

            def used(name, i, k, j=1):
                dve.wait_ge(weights_used, i * (2 * STAGES[name][1]) + (2 * (UNIT0[name] + k) + j + 1))

            counts = {"norm": 0, "post": 0, "job": 0, "rstd": 0}

            def mean_square(dst, parts):
                nc.vector.tensor_reduce(dst, parts, AX_X, ALU.add).then_inc(meaned, 1)
                counts["rstd"] += 1

            def post_norm(yg):
                counts["post"] += 1
                dve.wait_ge(rstd_ready, counts["rstd"])
                mean_square(ms[:, 2:4], sum_parts)
                dve.wait_ge(rstd_ready, counts["rstd"])
                dve.wait_ge(res_in, 16)

                def rows(n):
                    tb, cols = n // 2, slice((n % 2) * (D // 2), (n % 2 + 1) * (D // 2))
                    stt(out=res[:, tb, cols], in0=yg[:, tb, cols], scalar=rstd_post[:, tb:tb + 1],
                        in1=res[:, tb, cols], op0=ALU.mult, op1=ALU.add).then_inc(added, 1)
                for n in range(3):
                    rows(n)
                return rows

            def pre_norm(last_rows=None, after=None):
                e = counts["norm"]
                counts["norm"] += 1

                def quarter(tb, q):
                    cols = slice(q * COLS, (q + 1) * COLS)
                    ts(y[:, tb, cols], res[:, tb, cols], rstd[:, tb:tb + 1], None, ALU.mult).then_inc(normed, 1)

                dve.wait_ge(squared, 4 * e + 2)
                mean_square(ms[:, 0:1], row_parts[:, 0:1, :])
                if last_rows:
                    last_rows(3)
                dve.wait_ge(rstd_ready, counts["rstd"])
                for q in range(4):
                    quarter(0, q)
                    if q == 1:
                        dve.wait_ge(squared, 4 * e + 4)
                        mean_square(ms[:, 1:2], row_parts[:, 1:2, :])
                dve.wait_ge(rstd_ready, counts["rstd"])
                for q in range(4):
                    quarter(1, q)
                if after:
                    ahead(after, 0, STAGES[after][0] - 1)
                return e

            def turned_lo(banks, e):
                for kt in range(KT):
                    dve.wait_ge(xt_hi_ready, KT * e + kt // 2 * 2 + 2)
                    c = G_PRE + e * KT + kt
                    stt(out=xt_lo[:, kt, :], in0=ps[:, banks[kt // 2], (kt % 2) * SEQ:(kt % 2 + 1) * SEQ],
                        scalar=par[:, c:c + 1], in1=xt_hi[:, kt, :].bitcast(F32), op0=ALU.mult, op1=ALU.subtract
                        ).then_inc(xt_lo_ready, 1)

            nc.vector.memset(minus_half, -0.5).then_inc(memset_done, 1)
            nc.vector.memset(eps_col, EPS).then_inc(memset_done, 1)
            nc.vector.memset(table[BUCKETS:BUCKETS + 1, :], 1.0).then_inc(memset_done, 1)
            nc.vector.memset(sum_parts[:, :, 4:5], EPS).then_inc(memset_done, 1)
            nc.vector.memset(row_parts[:, :, 2:3], EPS).then_inc(memset_done, 1)
            dve.wait_ge(memset_done, 5)
            dve.wait_ge(params_in, 16)
            e = pre_norm()
            for h in range(2):
                split_lo(h)
            turned_lo(BANKS_N[0], e)
            for h in range(2, LEAD):
                split_lo(h)

            for k in range(8):
                ahead("cq", 0, k)
                if k == 3:
                    used("cq", 0, k)
                    nc.vector.tensor_copy(c1[:, :, 0:COLS], ps[:, 4:6, :]).then_inc(c_dve, 1)
                if k == 7:
                    used("cq", 0, k)
                    nc.vector.tensor_copy(vs.rearrange("p t h d -> p t (h d)"), ps[:, 6:8, SEQ:COLS])
                    nc.vector.tensor_copy(c1[:, :, COLS:COLS + SEQ], ps[:, 6:8, 0:SEQ]).then_inc(c_dve, 1)
            dve.wait_ge(c_act, 2)
            ts(ss_c[:, 0:2], ss_c[:, 0:2], 1.0 / 512, EPS, ALU.mult, ALU.add).then_inc(c_meaned, 1)
            ts(ss_c[:, 2:4], ss_c[:, 2:4], 1.0 / 256, EPS, ALU.mult, ALU.add).then_inc(c_meaned, 1)
            cos_m, sin_m = cst[:, C_COSM:C_COSM + SEQ], cst[:, C_SINM:C_SINM + SEQ]
            for k in range(3):
                ahead("k1", 0, k)
                if k == 0:
                    used("k1", 0, k)
                    tt(kr_a[0:64, :], ps[0:64, 0, 0:SEQ], cos_m[0:64, :], ALU.mult).then_inc(t_dve, 1)
                    tt(kr_a[64:128, :], ps[64:128, 0, 0:SEQ], sin_m[64:128, :], ALU.mult).then_inc(t_dve, 1)
                if k == 1:
                    dve.wait_ge(c_rstd, 1)
                    dve.wait_ge(c_dve, 2)
                    for q, cols in ((0, slice(0, COLS)), (2, slice(COLS, COLS + SEQ))):
                        for tb in range(TB):
                            ts(c1[:, tb, cols], c1[:, tb, cols], rstd_c[:, q + tb:q + tb + 1], None, ALU.mult
                               ).then_inc(c_scaled, 1)

            def q_s(i, k):
                ahead("qs", i, k)
                used("qs", i, k)
                if k % 2:
                    dst = qs[:, bass.ds(i * 4 + k, 1), :, :].rearrange("p o a t -> p (o a) t")
                    nc.vector.tensor_copy(dst, halves(ps[:, (TILES["qs"][0] + k) % 4, 0:SEQ])[:, :, ::-1]
                                          ).then_inc(t_dve, 1)
            dve.wait_ge(row_bias_mm, 1)
            nc.vector.tensor_copy(row_bias[:, :], ps[0:SWA_HEADS, 7, 0:BAND]).then_inc(row_bias_out, 1)
            for kt in range(6):
                dve.wait_ge(ct_hi_ready, kt // 2 * 2 + 2)
                g = par[:, G_QN + kt:G_QN + kt + 1]
                stt(out=ct_lo[:, kt, :], in0=ps[:, 4 + kt // 2, (kt % 2) * SEQ:(kt % 2 + 1) * SEQ], scalar=g,
                    in1=ct_hi[:, kt, :].bitcast(F32), op0=ALU.mult, op1=ALU.subtract).then_inc(ct_lo_ready, 1)
            stage_loop(nc.vector, "qs", q_s)
            dve.wait_ge(kr_moved, 16)
            tt(kr[0:64, :], kr_a[0:64, :], kr_b[0:64, :], ALU.add).then_inc(kr_ready, 1)
            ts(minus_sink, sink, -1.0, None, ALU.mult)
            for k in range(6):
                for j in range(2):
                    used("qup", 0, k, j)
                    for tl in range(2):
                        tile = 4 * k + 2 * j + tl
                        if tile % 2:
                            dst = qr[:, tile, :] if tile < 8 else flat(qn[:, tile - 8, :, :])
                            nc.vector.tensor_copy(dst, ps[:, (TILES["qup"][0] + tile) % 4, 0:SEQ]).then_inc(t_dve, 1)
                    ahead_half("qup", 0, k, j)
            def rope(r):
                dve.wait_ge(qr_swapped, r + 1)
                for c in range(2):
                    tile, src = 2 * r + c, ps[:, 4 + r, c * SEQ:(c + 1) * SEQ]
                    if tile:
                        dve.wait_ge(qr_ready, tile)
                    tt(rope_b[:, :], src, sin_m, ALU.mult)
                    step(tt(qr[:, tile, :], qr[:, tile, :], cos_m, ALU.mult))
                    tt(qr[:, tile, :], qr[:, tile, :], rope_b[:, :], ALU.add).then_inc(qr_ready, 1)

            dve.wait_ge(t_act, TILES["qup"][1] + 4)
            for k in range(2):
                for j in range(2):
                    rope(2 * k + j)
                    ahead_half("kvk", 0, k, j)
            for k in range(2):
                for j in range(2):
                    ch = 2 * k + j
                    used("kvv", 0, k, j)
                    nc.vector.tensor_copy(v1[:, 1, ch * COLS:(ch + 1) * COLS],
                                          ps[:, 5 + 2 * ((CHUNKS["kvv"] + ch) % 2), :]).then_inc(c_dve, 1)
                    ahead_half("kvv", 0, k, j)

            def attend(blockno, between):
                jobs = attention_jobs(blockno)
                g0 = counts["job"]
                counts["job"] += len(jobs)

                def maxima(n):
                    kind, j = jobs[n]
                    g = g0 + n
                    r = g % 2
                    dve.wait_ge(scored, g + 1)
                    m = nm[:, 4 * r:4 * r + 4]
                    if kind == "a2":
                        mm_ = mx[:, 6 * r:6 * r + 4]
                        both = ps[:, score_pair(2, g):score_pair(2, g) + 2, :]
                        step(nc.vector.tensor_reduce(mm_, both.rearrange("p h (b k) -> p h b k", k=SEQ), AX_X, ALU.max))
                        ts(m, mm_, -HEAD_SCALE, None, ALU.mult).then_inc(minus_max, 1)
                        return
                    if g >= 3:
                        dve.wait_ge(p_turned, g - 2)
                    banks = ps[:, score_pair(blockno, g):score_pair(blockno, g) + 2, :]
                    if kind == "b2":
                        dve.wait_ge(bias_masked, j + 1)
                        pr = pr2[:, g % 3, :, :, :].rearrange("p h b k -> p (h b) k")
                        stt(out=pr2[:, g % 3, :, :, :].rearrange("p h b k -> p h (b k)"), in0=banks, scalar=HEAD_SCALE,
                            in1=nb_bias[j].rearrange("p h b k -> p h (b k)"),
                            op0=ALU.mult, op1=ALU.add).then_inc(score_read, 1)
                        dve.wait_ge(score_read, score_reads(g))
                        mm_ = mx[:, 6 * r:6 * r + 4]
                        step(nc.vector.tensor_reduce(mm_, pr, AX_X, ALU.max))
                        ts(m, mm_, -1.0, None, ALU.mult).then_inc(minus_max, 1)
                        return
                    pr = pr1[:, g % 3, :, :]
                    if kind == "swa":
                        dve.wait_ge(bias_in[j % 2], 16 * (2 * (j // 2) + 2))
                        b = sw_bias[:, j % 2, :, :]
                        stt(out=pr[:, :, 0:SEQ], in0=banks[:, :, 0:SEQ], scalar=SWA_SCALE, in1=b,
                            op0=ALU.mult, op1=ALU.add)
                        last = stt(out=pr[:, :, SEQ:BAND], in0=banks[:, :, SEQ:BAND], scalar=SWA_SCALE,
                                   in1=b[:, :, P:SEQ], op0=ALU.mult, op1=ALU.add)
                    else:
                        ts(pr[:, :, 0:P], banks[:, :, 0:P], MLA_SCALE, None, ALU.mult)
                        causal = cst[:, C_CAUSAL:C_CAUSAL + P].rearrange("p (a k) -> p a k", a=1)
                        causal = causal.broadcast_to([P, 2, P])
                        for h in range(2):
                            last = stt(out=pr[:, h, P:BAND].rearrange("p (s k) -> p s k", k=P),
                                       in0=banks[:, h, P:BAND].rearrange("p (s k) -> p s k", k=P),
                                       scalar=MLA_SCALE, in1=causal, op0=ALU.mult, op1=ALU.add)
                    last.then_inc(score_read, 1)
                    dve.wait_ge(score_read, score_reads(g))
                    m6 = mx[:, 6 * r:6 * r + 6]
                    step(nc.vector.tensor_reduce(m6, pr.rearrange("p h (s k) -> p (h s) k", k=P), AX_X, ALU.max))
                    m6 = m6.rearrange("p (h s) -> p h s", s=3)
                    step(tt(m6[:, :, 1:2], m6[:, :, 0:1], m6[:, :, 1:2], ALU.max))
                    mv = m6[:, :, 2:0:-1]
                    mo = m.rearrange("p (h b) -> p h b", b=2)
                    if kind == "mla":
                        ts(mo, mv, -1.0, None, ALU.mult).then_inc(minus_max, 1)
                    else:
                        ms_ = minus_sink[:, 2 * j:2 * j + 2].rearrange("p (h b) -> p h b", b=1).broadcast_to([P, 2, 2])
                        stt(out=mo, in0=mv, scalar=-1.0, in1=ms_, op0=ALU.mult, op1=ALU.min).then_inc(minus_max, 1)

                def denominators(n):
                    kind, j = jobs[n]
                    g = g0 + n
                    r = g % 2
                    dve.wait_ge(exp_done, g + 1)
                    t = rs[:, 4 * r:4 * r + 4]
                    if kind == "swa":
                        dve.wait_ge(sink_exp, n + 1)
                        step(tt(t, t, es[:, 4 * r:4 * r + 4], ALU.add))
                    step(nc.vector.reciprocal(t, t))
                    for h in range(2):
                        for blk in range(TB):
                            d = t[:, 2 * h + blk:2 * h + blk + 1]
                            if blockno == 1:
                                pr = pr1[:, g % 3, h, 0:SEQ] if blk else pr1[:, g % 3, h, SEQ:BAND]
                            else:
                                pr = pr2[:, g % 3, h, blk, :]
                            last = ts(pr, pr, d, None, ALU.mult)
                    last.then_inc(p_normed, 1)

                def outputs(n):
                    kind, j = jobs[n]
                    g = g0 + n
                    dve.wait_ge(pv_done, g + 1)
                    src = ps[:, VALUE_BANK[blockno] + g % 2, :]
                    if kind == "a2":
                        dve.wait_ge(o_act, g + 1)
                        tt(flat(xt_lo[:, 2 * j:2 * j + 2, :]), src, flat(xt_hi[:, 2 * j:2 * j + 2, :]).bitcast(F32),
                           ALU.subtract).then_inc(o_dve, 1)
                    else:
                        dve.wait_ge(o_act, g + 1)

                        def rev(t):
                            return t[:, 8 + 2 * j:10 + 2 * j, :].rearrange("p h (a t) -> p (h a) t", t=P)[:, :, ::-1]
                        tt(rev(xt_lo), src.rearrange("p (a t) -> p a t", t=P), rev(xt_hi).bitcast(F32),
                           ALU.subtract).then_inc(o_dve, 1)

                for n in range(len(jobs) + 3):
                    if n < len(jobs):
                        maxima(n)
                    if blockno == 2 and n >= 3:
                        outputs(n - 3)
                    if 1 <= n <= len(jobs):
                        denominators(n - 1)
                    for work in between.get(n - len(jobs) + 1, ()):
                        work()

            def outputs_lo(src, hi, lo, hi_done, done, q):
                dve.wait_ge(hi_done, q + 1)
                tt(flat(lo[:, 4 * q:4 * q + 4, :]), src[:, 4 * q:4 * q + 4, :, :].rearrange("p a b c -> p (a b c)"),
                   flat(hi[:, 4 * q:4 * q + 4, :]).bitcast(F32), ALU.subtract).then_inc(done, 1)

            def os_lo_part(qq):
                for q in qq:
                    outputs_lo(qs, os_hi, os_lo, os_hi_ready, os_lo_ready, q)

            attend(1, {1: [lambda: ahead("gate0", 0, 0), lambda: os_lo_part((0, 1)), lambda: os_lo_part((2, 3)),
                           lambda: ahead("gate0", 0, 1)]})
            for q in range(4):
                outputs_lo(qn, om_hi, om_lo, om_hi_ready, om_lo_ready, q)

            def merge(name):
                _, ta, td = TILES[name]
                outs = [sum(u[0] == "out" for u in MERGE[name][:k]) for k in range(len(MERGE[name]))]

                def body(i, k):
                    ahead(name, i, k)
                    kind, place, branch = MERGE[name][k]
                    tile = MERGE_TILE0[name] + place
                    if kind == "gate":
                        return
                    used(name, i, k)
                    dve.wait_ge(t_act, i * 4 + (TILES["gate0"][1] + 2 * tile + 2))
                    g = sg[:, place % 2, branch, :]
                    tt(g, ps[:, (TILES[name][0] + k) % 4, 0:SEQ], g, ALU.mult).then_inc(t_dve, 1)
                    if branch:
                        return
                    dve.wait_ge(t_dve, i * 4 + (td + outs[k] + 1))
                    if isinstance(i, int) or tile:
                        dve.wait_ge(mg_lo_ready, i * 2 + tile)
                    tt(mg_f[:, :], sg[:, place % 2, 0, :], sg[:, place % 2, 1, :], ALU.add).then_inc(merged, 1)
                    dve.wait_ge(merged, i * 2 + (tile + 1))
                    dve.wait_ge(mg_hi_ready, i * 2 + (tile + 1))
                    at_ = bass.ds(i * 2 + tile, 1)
                    tt(mg_lo[:, at_, :].rearrange("p a t -> p (a t)"), mg_f[:, :],
                       mg_hi[:, at_, :].rearrange("p a t -> p (a t)").bitcast(F32), ALU.subtract
                       ).then_inc(mg_lo_ready, 1)
                return body
            for name in ("merge", "mergeZ"):
                stage_loop(nc.vector, name, merge(name))

            def take(name, per_chunk, add=False, yg=None, gain=None, begun=0):
                c0 = CHUNKS[name]
                chunks = STAGES[name][1] // per_chunk
                if yg is not None:
                    dve.wait_ge(post_in, 16 * (counts["post"] + 1))

                def body(i, k):
                    if k >= begun and not (yg is not None and is_last(name, i, k)):
                        ahead(name, i, k)
                    if k % per_chunk == per_chunk - 1:
                        ch = k // per_chunk
                        used(name, i, k)
                        b = 4 + 2 * ((c0 + ch) % 2)
                        cols = bass.ds(i * (chunks * COLS) + ch * COLS, COLS)
                        for tbs, done in ((slice(0, 1), block0_taken), (slice(1, 2), c_dve)) if yg is not None else (
                                (slice(0, 2), c_dve),):
                            src = ps[:, b + tbs.start:b + tbs.stop, :]
                            if add:
                                tt(y[:, tbs, cols], src, y[:, tbs, cols], ALU.add).then_inc(done, 1)
                            else:
                                nc.vector.tensor_copy(y[:, tbs, cols], src).then_inc(done, 1)
                        if yg is not None:
                            dve.wait_ge(c_dve, i * chunks + (c0 + ch + 1))
                            g = gain[:, cols].rearrange("p (a c) -> p a c", a=1).broadcast_to([P, TB, COLS])
                            tt(yg[:, :, cols], y[:, :, cols], g, ALU.mult)
                stage_loop(nc.vector, name, body, peel=yg is not None)

            take("wout", 4, yg=yg_hid, gain=gain_xt)
            dve.wait_ge(c_act, CHUNKS["wout"] + 4)
            turned_lo(BANKS_T, pre_norm(post_norm(yg_hid), "wout"))

            def conv_ffn(name):
                g0 = 0 if name == "upA" else H1A

                def body(i, k):
                    ahead(name, i, k)
                    if k % 2:
                        n = i * 2 + (HID0[name] + k // 2 + 1)
                        used(name, i, k)
                        a = ps[:, (TILES[name][0] + k - 1) % 4, 0:SEQ]
                        b = ps[:, (TILES[name][0] + k) % 4, 0:SEQ]

                        def w(c):
                            return par[:, bass.ds(i * 8 + (G_CONV + 4 * (g0 + k // 2) + c), 1)]
                        step(ts(conv[:, :], a, w(2), w(3), ALU.mult, ALU.add))
                        step(stt(out=conv[:, 1:SEQ], in0=a[:, 0:SEQ - 1], scalar=w(1), in1=conv[:, 1:SEQ],
                                 op0=ALU.mult, op1=ALU.add))
                        stt(out=conv[:, 2:SEQ], in0=a[:, 0:SEQ - 2], scalar=w(0), in1=conv[:, 2:SEQ],
                            op0=ALU.mult, op1=ALU.add).then_inc(conved, 1)
                        dve.wait_ge(activated, n)
                        tt(hid_f[:, :], b, act_tmp[:, :], ALU.mult).then_inc(hid_product, 1)
                        dve.wait_ge(hid_product, n)
                        dve.wait_ge(hid_hi_ready, n)
                        at_ = bass.ds(i * 2 + k // 2, 1)
                        tt(hid_lo[:, at_, :].rearrange("p a t -> p (a t)"), hid_f[:, :],
                           hid_hi[:, at_, :].rearrange("p a t -> p (a t)").bitcast(F32), ALU.subtract
                           ).then_inc(hid_lo_ready, 1)
                        dve.sem_inc(t_dve, 2)
                if STAGES[name][0] // STAGES[name][1] > 1:
                    turns = STAGES[name][0] // STAGES[name][1]
                    with nc.vector.Fori(0, turns) as i:
                        step.loop(i, 4)
                        for k in range(4):
                            body(i, k)
                    step.end(turns)

            def relu_ffn(name):
                def body(i, k):
                    ahead(name, i, k)
                    used(name, i, k)
                    n = HID0[name] + k + 1
                    dve.wait_ge(t_act, i * 4 + (TILES[name][1] + k + 1))
                    dve.wait_ge(hid_lo_ready, i * 4 + (n - 1))
                    stt(out=hid_f[:, :], in0=ps[:, (TILES[name][0] + k) % 4, 0:SEQ], scalar=0.0, in1=act_tmp[:, :],
                        op0=ALU.max, op1=ALU.mult).then_inc(hid_product, 1)
                    dve.wait_ge(hid_product, i * 4 + n)
                    dve.wait_ge(hid_hi_ready, i * 4 + n)
                    at_ = bass.ds(i * 4 + k, 1)
                    tt(hid_lo[:, at_, :].rearrange("p a t -> p (a t)"), hid_f[:, :],
                       hid_hi[:, at_, :].rearrange("p a t -> p (a t)").bitcast(F32), ALU.subtract
                       ).then_inc(hid_lo_ready, 1)
                stage_loop(nc.vector, name, body)

            conv_ffn("upA")
            take("dnA", H1A // 4)
            conv_ffn("upB")
            dve.wait_ge(c_dve, CHUNKS["dnB"])
            take("dnB", H1B // 4, add=True, yg=yg_xt, gain=gain_xt)
            dve.wait_ge(c_act, CHUNKS["dnB"] + 4)
            turned_lo(BANKS_N[CHUNKS["v2"] % 2], pre_norm(post_norm(yg_xt), "dnB"))

            for k in range(10):
                ahead("v2", 0, k)
                if k % 2:
                    ch = k // 2
                    used("v2", 0, k)
                    nc.vector.tensor_copy(v2[:, 1, ch * SEQ:(ch + 1) * SEQ],
                                          ps[:, 5 + 2 * ((CHUNKS["v2"] + ch) % 2), 0:SEQ]).then_inc(c_dve, 1)
            cos_a, sin_a = cst[:, C_COSA:C_COSA + SEQ], cst[:, C_SINA:C_SINA + SEQ]
            for k in range(26):
                ahead("qk2", 0, k)
                used("qk2", 0, k)
                src = ps[:, (TILES["qk2"][0] + k) % 4, 0:SEQ]
                if 10 <= k < 18 and k % 2:
                    nc.vector.tensor_copy(kb2[:, k - 10, :], src).then_inc(t_dve, 1)
                elif k >= 18 and k % 2:
                    nc.vector.tensor_copy(qb2[:, k - 18, :, ::-1], halves(src)).then_inc(t_dve, 1)
                if 1 <= k <= 10:
                    n = k - 1
                    dve.wait_ge(hn_summed, n + 1)
                    dve.wait_ge(hn_scaled, 2 * n + 2)
                    if n:
                        dve.wait_ge(hn_done, n)
                    tt(hn_a[:, :], hn_x[:, n % 2, :], cos_a, ALU.mult)
                    dve.wait_ge(hn_rooted, n + 1)
                    step(tt(hn_b[:, :], ps[:, 4 + n % 4, SEQ:2 * SEQ], sin_a, ALU.mult))
                    tt(hn_a[:, :], hn_a[:, :], hn_b[:, :], ALU.add)
                    step(nc.vector.reciprocal(hn_r[:, :], hn_r[:, :]))
                    dst = ka2[:, n, :] if n < 2 else qa2[:, n - 2, :, :].rearrange("p a t -> p (a t)")
                    tt(dst, hn_a[:, :], hn_r[:, :], ALU.mult).then_inc(hn_done, 1)
            attend(2, {1: [lambda: ahead("wo2", 0, 0)], 2: [lambda: ahead("wo2", 0, 1)]})
            take("wo2", 4, yg=yg_hid, gain=gain_hid, begun=2)
            dve.wait_ge(c_act, CHUNKS["wo2"] + 4)
            turned_lo(BANKS_T, pre_norm(post_norm(yg_hid), "wo2"))
            relu_ffn("up2a")
            take("dn2a", H2A // 4)
            relu_ffn("up2b")
            dve.wait_ge(c_dve, CHUNKS["dn2b"])
            dve.wait_ge(pe_hi_ready, 1)
            tt(pe_lo[:, :, :], pe_t[:, :, :], pe_hi[:, :, :].bitcast(F32), ALU.subtract).then_inc(pe_lo_ready, 1)
            take("dn2b", H2A // 4, add=True, yg=yg_xt, gain=gain_xt)
            dve.wait_ge(c_act, CHUNKS["dn2b"] + 4)
            last_rows = post_norm(yg_xt)
            for k in range(2):
                if k:
                    turned_lo(BANKS_N[CHUNKS["proj"] % 2], pre_norm(last_rows, "dn2b"))
                    ahead("proj", 0, 0)
                for j in range(2):
                    ch = 2 * k + j
                    used("proj", 0, k, j)
                    nc.vector.tensor_copy(emb[:, 1, ch * COLS:(ch + 1) * COLS],
                                          ps[:, 5 + 2 * ((CHUNKS["proj"] + ch) % 2), :]).then_inc(c_dve, 1)
                    if k:
                        ahead_half("proj", 0, k, j)
            dve.wait_ge(c_act, CHUNKS["gate"])
            dve.wait_ge(c_dve, CHUNKS["gate"])
            dve.wait_ge(post_in, 16 * 5)
            for k in range(16):
                ahead("gate", 0, k)
                if k % 4 == 3:
                    ch = k // 4
                    cols = slice(ch * COLS, (ch + 1) * COLS)
                    dve.wait_ge(block0_sig, ch + 1)
                    tt(y[:, 0, cols], emb[:, 0, cols], sig[:, 0, :], ALU.mult).then_inc(block0_taken, 1)
                    dve.wait_ge(c_act, CHUNKS["gate"] + ch + 1)
                    tt(y[:, 1, cols], emb[:, 1, cols], sig[:, 1, :], ALU.mult).then_inc(c_dve, 1)
                    dve.wait_ge(c_dve, CHUNKS["gate"] + ch + 1)
                    g = gain_hid[:, cols].rearrange("p (a c) -> p a c", a=1).broadcast_to([P, TB, COLS])
                    tt(yg_gate[:, :, cols], y[:, :, cols], g, ALU.mult)
            dve.wait_ge(y_squared, 4)
            post_norm(yg_gate)(3)

        @block.gpsimd
        def _(pool):
            dma = nc.gpsimd.dma_start
            tt = nc.gpsimd.tensor_tensor
            dma(cst[:, :], consts).then_inc(consts_in, 16)

            dma(par[:, :], params).then_inc(params_in, 16)

            def load_gains(tile, norm, stage, unit=0):
                pool.wait_ge(weights_used, 2 * (UNIT0[stage] + unit) + 1)
                src = bass.AP(tensor=post_gains.tensor, offset=norm * D, ap=[[0, P], [1, D]])
                dma(tile[:, :], src).then_inc(post_in, 16)

            dma(table[0:BUCKETS, :], bucket_table).then_inc(table_in, 16)
            dma(hot[:, :], bucket_hot).then_inc(table_in, 16)

            counts = {"rstd": 0}

            def power(dst=rstd_post, tbs=slice(2, 4)):
                counts["rstd"] += 1
                pool.wait_ge(meaned, counts["rstd"])
                tt(dst, ms[:, tbs], minus_half[:, tbs], ALU.pow).then_inc(rstd_ready, 1)

            def pre_powers():
                power(rstd[:, 0:1], slice(0, 1))
                power(rstd[:, 1:2], slice(1, 2))

            pool.wait_ge(memset_done, 5)
            pre_powers()
            pool.wait_ge(c_meaned, 2)
            tt(rstd_c, ss_c, minus_half, ALU.pow).then_inc(c_rstd, 1)

            pool.wait_ge(t_dve, 2)
            dma(kr_b[0:64, :], kr_a[64:128, :]).then_inc(kr_moved, 16)
            pool.wait_ge(t_act, 2)
            dma(ks[64:128, 0:4:2, :], ks[0:64, 0:4:2, :]).then_inc(ks_copied, 16)
            dma(ks[0:64, 1:4:2, :], ks[64:128, 1:4:2, :]).then_inc(ks_copied, 16)
            pool.wait_ge(kr_ready, 1)
            dma(kr[64:128, :], kr[0:64, :]).then_inc(kr_copied, 16)
            pool.wait_ge(row_bias_out, 1)
            dma(band_dram, row_bias[:, :]).then_inc(band_stored, 16)
            pool.wait_ge(band_stored, 16)

            for j in range(N_SWA):
                if j >= 2:
                    pool.wait_ge(minus_max, j - 1)
                for h in range(2):
                    head = 2 * j + h
                    src = bass.AP(tensor=band_dram.tensor, offset=head * BAND, ap=[[1, P], [1, SEQ]])
                    dma(sw_bias[:, j % 2, h, :], src).then_inc(bias_in[j % 2], 16)
            load_gains(gain_xt, 0, "wout")
            dma(res[:, :, :], x.rearrange("(t p) d -> p t d", p=P)).then_inc(res_in, 16)
            power()
            pre_powers()
            load_gains(gain_xt, 1, "dnB")
            power()
            pre_powers()
            pool.wait_ge(weights_used, 2 * UNIT0["v2"] + 1)
            nb = cst[:, C_NB:C_NB + 64]
            for j in range(N_B2):
                for h in range(2):
                    for blk in range(TB):
                        for r in range(2):
                            head = 2 * j + h
                            off = (head * 15 + 7 - (2 * blk + 1 - r)) * RPB_W
                            src = bass.AP(tensor=rpb.tensor, offset=off, ap=[[1, 64], [RPB_W, 4], [1, 64]])
                            dma(nb_bias[j][64 * r:64 * r + 64, h, blk, :].rearrange("p (a b) -> p a b", b=64),
                                src).then_inc(bias_in[j % 2], 16)
                pool.wait_ge(bias_in[j % 2], 16 * (N_SWA + 8 * (j // 2 + 1)))
                v = nb_bias[j].rearrange("p h b (a k) -> p (h b a) k", k=64)
                m = nb.rearrange("p (a k) -> p a k", a=1).broadcast_to([P, 16, 64])
                tt(v, v, m, ALU.add).then_inc(bias_masked, 1)
            dma(pe_t[:, :, :], p_t).then_inc(pe_in, 16)
            load_gains(gain_hid, 2, "wo2", 2)
            power()
            pre_powers()
            load_gains(gain_xt, 3, "dn2b")
            power()
            pre_powers()
            load_gains(gain_hid, 4, "gate")
            power()


def _constants():
    c = np.zeros((P, C_END), np.float32)
    d = np.arange(P)
    c[:, C_ID:C_ID + P] = np.eye(P)
    c[d, C_SWAP + (d ^ 32)] = 1.0
    c[:, C_ONES:C_ONES + P] = 1.0
    inv = (np.float32(10000.0) ** (-np.arange(0, 64, 2, dtype=np.float32) / np.float32(64))).astype(np.float32)
    t = np.arange(SEQ)
    sign = np.where(d % 64 < 32, -1.0, 1.0).astype(np.float32)[:, None]
    ang = t.astype(np.float32)[None, :] * inv[d % 32][:, None]
    c[:, C_COSM:C_COSM + SEQ], c[:, C_SINM:C_SINM + SEQ] = np.cos(ang), np.sin(ang) * sign
    where = np.where(d[:, None] < 64, (t // 64)[None, :], (t % 64)[None, :]).astype(np.float32)
    ang = where * inv[d % 32][:, None]
    c[:, C_COSA:C_COSA + SEQ], c[:, C_SINA:C_SINA + SEQ] = np.cos(ang), np.sin(ang) * sign
    lower = np.where(d[None, :] <= d[:, None], 0.0, NEG)
    c[:, C_CAUSAL:C_CAUSAL + P] = lower
    col = 63 - d % 64
    c0 = np.clip(col - 8, 0, 48)[:, None]
    k = np.arange(64)[None, :]
    c[:, C_NB:C_NB + 64] = np.where((k >= c0) & (k < c0 + 16), 0.0, NEG)
    return c


def _bucket_hot():
    hot = np.zeros((BUCKETS + 1, BAND), np.float32)
    for j in range(BAND):
        n = 255 - j
        if not 0 <= n < WINDOW:
            hot[BUCKETS, j] = NEG
            continue
        b = n if n < 16 else min(31, 16 + int(math.log(n / 16) / math.log(8) * 16))
        hot[b, j] = 1.0
    return hot


def _t_units(w):
    k, n = w.shape
    return w.reshape(k // P, P, n // P, P).transpose(2, 1, 0, 3).reshape(n // P, P, UNIT)


def _n_units(w):
    k, n = w.shape
    return w.reshape(k // 512, 4, P, n // COLS, COLS).transpose(3, 0, 2, 1, 4).reshape(-1, P, UNIT)


def _few_t(w, tiles):
    k, n = w.shape
    return w.reshape(k // P, P, n // (tiles * P), tiles, P).transpose(2, 1, 3, 0, 4).reshape(-1, P, UNIT)


def _few_n(w):
    return w.reshape(2, P, -1, 2, COLS).transpose(2, 1, 3, 0, 4).reshape(-1, P, UNIT)


def _values_units(w):
    return w.reshape(2, 8, P, 5, SEQ).transpose(3, 0, 2, 1, 4).reshape(-1, P, UNIT)


def _stream(a):
    w = a["w_in"][0]
    cq, ckv, kr, q_s, k_s, v_s, g = np.split(w, np.cumsum([512, 256, 64, 2048, 256, 256]), axis=1)
    kr_sw = np.concatenate([kr[:, 32:], kr[:, :32]], 1)
    g = _t_units(g)
    om, os_ = _t_units(a["w_o_mla"][0]), _t_units(a["w_o_swa"][0])
    gates, outs = (g[:16], g[16:]), (om, os_)
    order = [(kind, MERGE_TILE0[name] + turn * 2 + place, branch) for name in ("gate0", "merge", "mergeZ")
             for turn in range(STAGES[name][0] // STAGES[name][1]) for kind, place, branch in MERGE[name]]
    merge = np.stack([(gates if kind == "gate" else outs)[branch][tile] for kind, tile, branch in order])
    qu = a["mla_w_q_up"][0].reshape(512, 16, 192)
    kvu = a["mla_w_kv_up"][0].reshape(256, 16, 256)
    up = a["ffn_w_up"][0]
    pairs = np.stack([_t_units(up[:, :FF1]), _t_units(up[:, FF1:])], 1)
    down = a["ffn_w_down"][0]
    w2 = a["w_in_2"][0]
    qa, ka, va, qb, kb, vb = np.split(w2, np.cumsum([1024, 256, 256, 1024, 1024]), axis=1)
    up2, down2 = _t_units(a["w_up_2"][0]), a["w_down_2"][0]
    parts = [
        _n_units(np.concatenate([cq, ckv, v_s], 1)), _t_units(np.concatenate([kr, kr_sw, k_s], 1)),
        _t_units(q_s),
        _few_t(np.concatenate([qu[:, :, 128:].reshape(512, 1024), qu[:, :, :128].reshape(512, 2048)], 1), 4),
        _few_t(np.ascontiguousarray(kvu[:, :, :128]).reshape(256, 2048), 8),
        _few_n(np.ascontiguousarray(kvu[:, :, 128:]).reshape(256, 2048)),
        merge, _n_units(a["w_out"][0]),
        pairs[:H1A].reshape(-1, P, UNIT), _n_units(down[:H1A * P]),
        pairs[H1A:].reshape(-1, P, UNIT), _n_units(down[H1A * P:]),
        _values_units(np.concatenate([va, vb], 1)), _t_units(np.concatenate([ka, qa, kb, qb], 1)),
        _n_units(a["w_o_2"][0]),
        up2[:H2A], _n_units(down2[:H2A * P]), up2[H2A:], _n_units(down2[H2A * P:]),
        _few_n(a["w_ple_proj_2"][0]), _n_units(a["w_ple_gate_2"][0]),
    ]
    return np.concatenate(parts, 0)


def kernel(**inputs):
    import concourse.bacc as bacc
    from concourse.bass_utils import run_bass_kernel_spmd

    a = {n: np.asarray(v) for n, v in inputs.items()}
    conv = np.concatenate([a["ffn_conv_w"][0], a["ffn_conv_b"]], 0).reshape(4, 44, P).transpose(2, 1, 0).reshape(P, 176)
    params = np.concatenate([
        a["mla_q_norm"][0].reshape(4, P).T, a["mla_kv_norm"][0].reshape(2, P).T,
        a["q_norm_2"][0].reshape(1, P).T, a["k_norm_2"][0].reshape(1, P).T, conv,
        np.broadcast_to(a["swa_sinks"][0], (P, 32))]
        + [a[n][0].reshape(KT, P).T for n in ("norm_mix_pre", "norm_ffn_pre", "pre_mix_norm_2", "pre_mlp_norm_2",
                                              "pre_ple_norm_2")], 1)
    post = ["norm_mix_post", "norm_ffn_post", "post_mix_norm_2", "post_mlp_norm_2", "post_ple_norm_2"]
    arrays = {
        "stream": _stream(a), "x": a["x"][0], "consts": _constants(), "params": params,
        "post_gains": np.stack([a[n][0] for n in post]),
        "bucket_table": a["rel_bias_table"], "bucket_hot": _bucket_hot(),
        "rpb": np.pad(a["rel_pos_bias_2"][0], ((0, 0), (0, 0), (48, 48))).reshape(-1),
        "p_t": a["p_2"][0, 0].reshape(SEQ, 2, P).transpose(2, 1, 0),
    }
    arrays = {f"in_{n}": np.ascontiguousarray(v) for n, v in arrays.items()}
    nc = bacc.Bacc("TRN2", target_bir_lowering=False, num_devices=1)
    args = [nc.dram_tensor(n, v.shape, F32, kind="ExternalInput").ap() for n, v in arrays.items()]
    args.append(nc.dram_tensor("out_x", (SEQ, D), F32, kind="ExternalOutput").ap())
    program(nc, *args)
    r = run_bass_kernel_spmd(nc, [arrays], core_ids=[0])
    return r.results[0]["out_x"].reshape(1, SEQ, D)
```
